# Optimizing a Trainium2 kernel written in Bass

```python
import jax
import jax.numpy as jnp
from jax import lax
import numpy as np

D_MODEL = 1024
BATCH = 1
SEQ = 2048
DEPTH = 1

D_MIX = D_MODEL
MLSTM_HEADS = 4
MLSTM_DH = (D_MIX // 2) // MLSTM_HEADS
MLSTM_W = MLSTM_HEADS * MLSTM_DH
GLA_HEADS = 4
GLA_DV = (D_MIX // 2) // GLA_HEADS
GLA_DK = GLA_DV // 2
GLA_WV = GLA_HEADS * GLA_DV
GLA_WK = GLA_HEADS * GLA_DK
GLA_GATE_RANK = 16
GLA_GATE_NORM = 16.0
CONV_WIDTH = 4
MLSTM_CHUNK = 128
GLA_CHUNK = 64
D_PROJ = 4 * MLSTM_W + 2 * MLSTM_HEADS + 2 * GLA_WK + 2 * GLA_WV + GLA_GATE_RANK
N_GROUPS = 4
EXPERTS_PER_GROUP = 8
N_EXPERTS = N_GROUPS * EXPERTS_PER_GROUP
TOP_K = 2
D_EXPERT = D_MODEL // 2
MOE_BLOCK = 256
EPS = 1e-6

kernel_name = 'hymba_mlstm_gla_hmoe'

'''Hybrid decoder trunk. Each of DEPTH layers: x += W_out[ concat( mLSTM heads , GLA heads ) ] of RMSNorm(x)
from one combined input projection; x += hierarchical MoE (top-1 group, top-2 expert in group) of RMSNorm(x);
final RMSNorm. Input x: (BATCH, SEQ, D_MODEL) float32; output (BATCH, SEQ, D_MODEL).'''

def rmsnorm(x, g):
    xf = x.astype(jnp.float32)
    y = xf * lax.rsqrt(jnp.mean(xf * xf, axis=-1, keepdims=True) + EPS)
    return (y * g.astype(jnp.float32)).astype(x.dtype)

def head_rmsnorm(h):
    h = h * lax.rsqrt(jnp.mean(h * h, axis=-1, keepdims=True) + EPS)
    return h.reshape(h.shape[0], h.shape[1], -1)

def split_proj(p):
    sizes = [MLSTM_W, MLSTM_W, MLSTM_W, MLSTM_W, MLSTM_HEADS, MLSTM_HEADS,
             GLA_WK, GLA_WK, GLA_WV, GLA_WV, GLA_GATE_RANK]
    offs, acc = [], 0
    for s in sizes[:-1]:
        acc += s
        offs.append(acc)
    return jnp.split(p, offs, axis=-1)

def heads(t, n_heads):
    return t.reshape(t.shape[0], t.shape[1], n_heads, -1)

def to_chunks(t, L):
    B, S = t.shape[0], t.shape[1]
    t = t.reshape((B, S // L, L) + t.shape[2:])
    return jnp.swapaxes(jnp.moveaxis(t, 1, 0), 2, 3)

def from_chunks(y):
    y = jnp.moveaxis(jnp.swapaxes(y, 2, 3), 0, 1)
    B, NC, L = y.shape[0], y.shape[1], y.shape[2]
    return y.reshape((B, NC * L) + y.shape[3:])

def causal_dwconv(u, w, b):
    out = lax.conv_general_dilated(u, w[:, None, :], window_strides=(1,),
                                   padding=[(CONV_WIDTH - 1, 0)],
                                   dimension_numbers=('NWC', 'WIO', 'NWC'),
                                   feature_group_count=u.shape[-1])
    return out + b

def mlstm_chunked(q, k, v, ig, lf):
    B, S, H, dk = q.shape
    dv = v.shape[-1]
    L = MLSTM_CHUNK
    tri = jnp.tril(jnp.ones((L, L), dtype=bool))

    def body(carry, inp):
        C, n, m = carry
        qc, kc, vc, ic, fc = inp
        b = jnp.cumsum(fc, axis=-1)
        logD = jnp.where(tri, b[..., :, None] - b[..., None, :] + ic[..., None, :], -jnp.inf)
        m_inter = b + m[..., None]
        m_j = jnp.maximum(m_inter, jnp.max(logD, axis=-1))
        s = jnp.einsum('bhjd,bhsd->bhjs', qc, kc) * jnp.exp(logD - m_j[..., None])
        a = jnp.exp(m_inter - m_j)
        num = jnp.einsum('bhjs,bhsv->bhjv', s, vc) + a[..., None] * jnp.einsum('bhjd,bhdv->bhjv', qc, C)
        den = jnp.sum(s, axis=-1) + a * jnp.einsum('bhjd,bhd->bhj', qc, n)
        h = num / jnp.maximum(jnp.abs(den), jnp.exp(-m_j))[..., None]
        g = b[..., -1]
        logw = g[..., None] - b + ic
        m_new = jnp.maximum(g + m, jnp.max(logw, axis=-1))
        kw = kc * jnp.exp(logw - m_new[..., None])[..., None]
        decay = jnp.exp(g + m - m_new)
        C_new = decay[..., None, None] * C + jnp.einsum('bhsd,bhsv->bhdv', kw, vc)
        n_new = decay[..., None] * n + jnp.sum(kw, axis=2)
        return (C_new, n_new, m_new), h

    init = (jnp.zeros((B, H, dk, dv), jnp.float32), jnp.zeros((B, H, dk), jnp.float32),
            jnp.zeros((B, H), jnp.float32))
    xs = (to_chunks(q, L), to_chunks(k, L), to_chunks(v, L), to_chunks(ig, L), to_chunks(lf, L))
    _, hs = lax.scan(body, init, xs)
    return from_chunks(hs)

def gla_chunked(q, k, v, la):
    B, S, H, dk = q.shape
    dv = v.shape[-1]
    L = GLA_CHUNK
    tri = jnp.tril(jnp.ones((L, L), dtype=bool))[..., None]

    def body(Sst, inp):
        qc, kc, vc, ac = inp
        Bc = jnp.cumsum(ac, axis=2)
        diff = jnp.where(tri, Bc[:, :, :, None, :] - Bc[:, :, None, :, :], -jnp.inf)
        A = jnp.einsum('bhjc,bhsc,bhjsc->bhjs', qc, kc, jnp.exp(diff))
        o = jnp.einsum('bhjs,bhsv->bhjv', A, vc) + jnp.einsum('bhjc,bhcv->bhjv', qc * jnp.exp(Bc), Sst)
        gL = Bc[:, :, -1, :]
        kd = kc * jnp.exp(gL[:, :, None, :] - Bc)
        S_new = jnp.exp(gL)[..., None] * Sst + jnp.einsum('bhsc,bhsv->bhcv', kd, vc)
        return S_new, o

    init = jnp.zeros((B, H, dk, dv), jnp.float32)
    xs = (to_chunks(q, L), to_chunks(k, L), to_chunks(v, L), to_chunks(la, L))
    _, os_ = lax.scan(body, init, xs)
    return from_chunks(os_)

def parallel_mixer(xn, w_in, conv_w, conv_b, b_gate, w_gla_gate, b_gla_gate, head_norm, w_out):
    f32 = jnp.float32
    Bsz, S, _ = xn.shape
    p = xn @ w_in
    q_m, k_m, v_m, o_m, i_m, f_m, q_g, k_g, v_g, z_g, r_g = split_proj(p)
    qk = jax.nn.silu(causal_dwconv(jnp.concatenate([q_m, k_m], axis=-1), conv_w, conv_b))
    q_m, k_m = jnp.split(qk, 2, axis=-1)
    gates = jnp.concatenate([i_m, f_m], axis=-1).astype(f32) + b_gate.astype(f32)
    ig = gates[..., :MLSTM_HEADS]
    lf = jax.nn.log_sigmoid(gates[..., MLSTM_HEADS:])
    h_m = mlstm_chunked(heads(q_m, MLSTM_HEADS).astype(f32),
                        heads(k_m, MLSTM_HEADS).astype(f32) * (MLSTM_DH ** -0.5),
                        heads(v_m, MLSTM_HEADS).astype(f32), ig, lf)
    la = jax.nn.log_sigmoid((r_g @ w_gla_gate + b_gla_gate).astype(f32)) / GLA_GATE_NORM
    h_g = gla_chunked(heads(q_g, GLA_HEADS).astype(f32) * (GLA_DK ** -0.5),
                      heads(k_g, GLA_HEADS).astype(f32),
                      heads(v_g, GLA_HEADS).astype(f32), heads(la, GLA_HEADS))
    hc = jnp.concatenate([head_rmsnorm(h_m), head_rmsnorm(h_g)], axis=-1)
    gate_out = jnp.concatenate([jax.nn.sigmoid(o_m), jax.nn.silu(z_g)], axis=-1).astype(f32)
    y = hc * head_norm.astype(f32) * gate_out
    return y.astype(xn.dtype) @ w_out

def hier_moe(xn, w_group, b_group, w_expert, b_expert, w_gu, w_down):
    f32 = jnp.float32
    Bsz, S, D = xn.shape
    T = Bsz * S
    xt = xn.reshape(T, D)
    g_logit = (xt @ w_group).astype(f32) + b_group.astype(f32)
    g_prob = jax.nn.softmax(g_logit, axis=-1)
    g_sel = jnp.argmax(g_logit, axis=-1)
    g_gate = jnp.take_along_axis(g_prob, g_sel[:, None], axis=-1)
    e_logit = ((xt @ w_expert).astype(f32) + b_expert.astype(f32)).reshape(T, N_GROUPS, EXPERTS_PER_GROUP)
    e_logit = jnp.take_along_axis(e_logit, g_sel[:, None, None], axis=1)[:, 0]
    top_v, top_i = lax.top_k(e_logit, TOP_K)
    wts = jax.nn.softmax(top_v, axis=-1) * g_gate
    eid = (g_sel[:, None] * EXPERTS_PER_GROUP + top_i).reshape(-1).astype(jnp.int32)
    tid = jnp.repeat(jnp.arange(T, dtype=jnp.int32), TOP_K)
    wflat = wts.reshape(-1)
    order = jnp.argsort(eid)
    se, st, sw = eid[order], tid[order], wflat[order]
    counts = jnp.bincount(eid, length=N_EXPERTS).astype(jnp.int32)
    pcounts = (counts + MOE_BLOCK - 1) // MOE_BLOCK * MOE_BLOCK
    pend = jnp.cumsum(pcounts)
    pstart = pend - pcounts
    start = jnp.cumsum(counts) - counts
    n_assign = T * TOP_K
    pos = pstart[se] + jnp.arange(n_assign, dtype=jnp.int32) - start[se]
    n_blocks = (n_assign + MOE_BLOCK - 1) // MOE_BLOCK + N_EXPERTS
    tok_buf = jnp.full((n_blocks * MOE_BLOCK,), T, jnp.int32).at[pos].set(st)
    w_buf = jnp.zeros((n_blocks * MOE_BLOCK,), f32).at[pos].set(sw)
    blk_exp = jnp.minimum(jnp.searchsorted(pend, jnp.arange(n_blocks, dtype=jnp.int32) * MOE_BLOCK,
                                           side='right'), N_EXPERTS - 1)
    xt_pad = jnp.concatenate([xt, jnp.zeros((1, D), xt.dtype)], axis=0)

    def expert_block(args):
        tok, wb, e = args
        xb = xt_pad[tok]
        gate, up = jnp.split(xb @ w_gu[e], 2, axis=-1)
        yb = (jax.nn.silu(gate) * up) @ w_down[e]
        return yb.astype(f32) * wb[:, None]

    ys = lax.map(expert_block, (tok_buf.reshape(n_blocks, MOE_BLOCK),
                                w_buf.reshape(n_blocks, MOE_BLOCK), blk_exp))
    y = jax.ops.segment_sum(ys.reshape(-1, D), tok_buf, num_segments=T + 1)[:T]
    return y.astype(xn.dtype).reshape(Bsz, S, D)

def setup_inputs(seed: int = 0) -> dict:
    key = jax.random.key(seed)
    ks = jax.random.split(key, 20)
    f32 = jnp.float32
    nrm = lambda k, shape, scale: jax.random.normal(k, shape, f32) * scale
    x = jax.random.normal(ks[0], (BATCH, SEQ, D_MODEL), f32)
    norm_mix = 1.0 + nrm(ks[1], (DEPTH, D_MODEL), 0.02)
    w_in = nrm(ks[2], (DEPTH, D_MODEL, D_PROJ), D_MODEL ** -0.5)
    conv_w = nrm(ks[3], (DEPTH, CONV_WIDTH, 2 * MLSTM_W), CONV_WIDTH ** -0.5)
    conv_b = nrm(ks[4], (DEPTH, 2 * MLSTM_W), 0.02)
    i_bias = nrm(ks[5], (DEPTH, MLSTM_HEADS), 0.1)
    f_bias = jnp.linspace(3.0, 6.0, MLSTM_HEADS, dtype=f32)[None, :] + nrm(ks[6], (DEPTH, MLSTM_HEADS), 0.1)
    b_mlstm_gate = jnp.concatenate([i_bias, f_bias], axis=-1)
    w_gla_gate = nrm(ks[7], (DEPTH, GLA_GATE_RANK, GLA_WK), GLA_GATE_RANK ** -0.5)
    b_gla_gate = nrm(ks[8], (DEPTH, GLA_WK), 0.1)
    head_norm = 1.0 + nrm(ks[9], (DEPTH, D_MIX), 0.02)
    w_out = nrm(ks[10], (DEPTH, D_MIX, D_MODEL), D_MIX ** -0.5)
    norm_ffn = 1.0 + nrm(ks[11], (DEPTH, D_MODEL), 0.02)
    w_group = nrm(ks[12], (DEPTH, D_MODEL, N_GROUPS), D_MODEL ** -0.5)
    b_group = nrm(ks[13], (DEPTH, N_GROUPS), 0.01)
    w_expert = nrm(ks[14], (DEPTH, D_MODEL, N_EXPERTS), D_MODEL ** -0.5)
    b_expert = nrm(ks[15], (DEPTH, N_EXPERTS), 0.01)
    w_gu = nrm(ks[16], (DEPTH, N_EXPERTS, D_MODEL, 2 * D_EXPERT), D_MODEL ** -0.5)
    w_down = nrm(ks[17], (DEPTH, N_EXPERTS, D_EXPERT, D_MODEL), D_EXPERT ** -0.5)
    norm_final = 1.0 + nrm(ks[18], (D_MODEL,), 0.02)
    return {'x': x, 'norm_mix': norm_mix, 'w_in': w_in, 'conv_w': conv_w, 'conv_b': conv_b,
            'b_mlstm_gate': b_mlstm_gate, 'w_gla_gate': w_gla_gate, 'b_gla_gate': b_gla_gate,
            'head_norm': head_norm, 'w_out': w_out, 'norm_ffn': norm_ffn, 'w_group': w_group,
            'b_group': b_group, 'w_expert': w_expert, 'b_expert': b_expert, 'w_gu': w_gu,
            'w_down': w_down, 'norm_final': norm_final}

def reference(x, norm_mix, w_in, conv_w, conv_b, b_mlstm_gate, w_gla_gate, b_gla_gate,
              head_norm, w_out, norm_ffn, w_group, b_group, w_expert, b_expert, w_gu,
              w_down, norm_final):
    h = x
    for l in range(DEPTH):
        h = h + parallel_mixer(rmsnorm(h, norm_mix[l]), w_in[l], conv_w[l], conv_b[l],
                               b_mlstm_gate[l], w_gla_gate[l], b_gla_gate[l], head_norm[l], w_out[l])
        h = h + hier_moe(rmsnorm(h, norm_ffn[l]), w_group[l], b_group[l], w_expert[l],
                         b_expert[l], w_gu[l], w_down[l])
    return rmsnorm(h, norm_final)


_drawn_inputs = setup_inputs


def setup_inputs(seed=0):
    import zlib

    import numpy as np

    out = dict(_drawn_inputs(seed))
    spreads = {}
    factors = {'conv_b': 3.605,
     'head_norm': 2.688,
     'b_group': 22.474,
     'b_expert': 15.99,
     'norm_final': 8.417,
     'norm_ffn': 3.207}
    for name, (base, spread) in spreads.items():
        noise = np.random.default_rng([zlib.crc32(name.encode()), seed]).standard_normal(out[name].shape)
        drawn = base * np.exp(spread * noise) if base else spread * noise
        out[name] = jnp.asarray(drawn.astype(out[name].dtype))
    for name, factor in factors.items():
        out[name] = (out[name] * factor).astype(out[name].dtype)
    return out
```

```python
import math
from contextlib import ExitStack

import concourse.bass as bass
from concourse import mybir

F32 = mybir.dt.float32
F32R = mybir.dt.float32r
I32 = mybir.dt.int32
U32 = mybir.dt.uint32
ALU = mybir.AluOpType
ACT = mybir.ActivationFunctionType
AX_X = mybir.AxisListType.X

P = 128
D = 1024
KC = D // P
T = 2048
NT = T // P
GRP = 512
NG = T // GRP
CPG = GRP // P
H = 4
DV = P
DK = 64
RANK = 16
CW = 4
W = H * DV
D_PROJ = 4 * W + 2 * H + 2 * H * DK + 2 * W + RANK
OFF_QK, OFF_VM, OFF_OM = 0, 2 * W, 3 * W
OFF_I = 4 * W
OFF_F = OFF_I + H
OFF_QKG = OFF_F + H
OFF_VG = OFF_QKG + 2 * H * DK
OFF_ZG = OFF_VG + W
OFF_R = OFF_ZG + W
NE, NGRP, EPG = 32, 4, 8
DE = 512
NBLK = 2 * T // P + NE
YB = NBLK + NT
EPS = 1e-6
SUB = 32
NSUB = P // SUB
VT_CAP = 1e30
NEG = -1e30
TABLES = "natural_log_exp_and_others"
LN_CAP = 2.0 ** 60
C_I, C_F, C_R, C_QKG, C_QK = 0, 32, 64, 80, 80 + 512
C_ALL = C_QK + 1024


def mm3(pe, out, ah, al, bh, bl, first, last):
    pe.matmul(out, ah, bh, start=first, stop=False)
    pe.matmul(out, ah, bl, start=False, stop=False)
    return pe.matmul(out, al, bh, start=False, stop=last)


def neg_abs(dve, out, x):
    return dve.scalar_tensor_tensor(out=out, in0=x, scalar=-1.0, in1=x, op0=ALU.mult, op1=ALU.min)


def constants(nc, sem, ctx, K):
    def sb(name, shape, dt=F32):
        return ctx.enter_context(nc.sbuf_tensor(name, shape, dt))

    K["ident"] = sb("ident", [P, P])
    K["ones"] = sb("ones", [P, P])
    K["below"] = sb("below", [P, P])
    K["keep"] = sb("keep", [P, P])
    K["drop"] = sb("drop", [P, P])
    K["eps"] = sb("eps", [P, 1])
    K["one"] = sb("one", [P, 1])
    s = sem("const_set")
    s2 = sem("const_made")
    with nc.Block() as block:
        @block.gpsimd
        def _(pool):
            pool.memset(K["ident"][:, :], 0.0).then_inc(s, 1)
            pool.memset(K["ones"][:, :], 1.0).then_inc(s, 1)
            pool.memset(K["below"][:, :], 1.0).then_inc(s, 1)
            pool.memset(K["keep"][:, :], 1.0).then_inc(s, 1)
            pool.memset(K["drop"][:, :], 0.0).then_inc(s, 1)
            pool.memset(K["eps"][:, :], EPS).then_inc(s, 1)
            pool.memset(K["one"][:, :], 1.0).then_inc(s, 1)
            pool.wait_ge(s, 7)
            row_minus_col = dict(base=0, pattern=[[-1, P]], channel_multiplier=1)
            col_minus_row = dict(base=0, pattern=[[1, P]], channel_multiplier=-1)
            pool.affine_select(out=K["ident"][:, :], in_=K["ident"][:, :], compare_op=ALU.not_equal,
                               fill=1.0, **row_minus_col).then_inc(s2, 1)
            pool.affine_select(out=K["below"][:, :], in_=K["below"][:, :], compare_op=ALU.is_gt,
                               fill=0.0, **col_minus_row).then_inc(s2, 1)
            pool.affine_select(out=K["keep"][:, :], in_=K["keep"][:, :], compare_op=ALU.is_ge,
                               fill=0.0, **col_minus_row).then_inc(s2, 1)
            pool.affine_select(out=K["drop"][:, :], in_=K["drop"][:, :], compare_op=ALU.is_ge,
                               fill=NEG, **col_minus_row).then_inc(s2, 1)
            pool.wait_ge(s2, 4)


def project_tokens(nc, sem, K, x, norm_mix, w_in, head_norm, S):
    ORDER = (OFF_OM, OFF_ZG, OFF_VM, OFF_VG)
    x_v = x.rearrange("b (t p) d -> (b t) p d", p=P)
    with ExitStack() as ctx:
        def sb(name, shape, dt=F32):
            return ctx.enter_context(nc.sbuf_tensor(name, shape, dt))

        def pb(name, shape):
            return ctx.enter_context(nc.psum_tensor(name, shape, F32))

        w_hi = sb("wt_hi", [P, 4, KC, W], F32R)
        w_lo = sb("wt_lo", [P, 4, KC, W], F32R)
        NSTAGE = 4
        stage = sb("wt_stage", [P, NSTAGE, W])
        x_in = sb("x_in", [P, 2, D])
        xn = sb("xn", [P, D])
        xT_hi = [sb(f"xT_hi{i}", [P, KC, P], F32R) for i in range(2)]
        xT_lo = [sb(f"xT_lo{i}", [P, KC, P], F32R) for i in range(2)]
        sq = sb("sq", [P, D])
        ssq = sb("ssq", [P, 1])
        lnv = sb("lnv", [P, 1])
        rstd = sb("rstd", [P, 1])
        g_mix = sb("g_mix", [P, KC])
        hn = sb("hn", [P, D])
        e_o = sb("e_o", [P, W])
        e_z = sb("e_z", [P, W])
        gate = sb("gate", [P, D])
        val = sb("val", [P, D])
        ps_t = pb("ps_t", [P, KC, P])
        ps_u = [pb(f"ps_u{i}", [P, W]) for i in range(4)]

        par_in, x_sem = sem("ta_params"), [sem("ta_x0"), sem("ta_x1")]
        w_in_sem = [sem(f"ta_w{i}") for i in range(NSTAGE)]
        w_hid, w_split = sem("ta_w_hi"), sem("ta_w_split")
        ssq_ready, rstd_ready, xn_ready = sem("ta_ssq"), sem("ta_rstd"), sem("ta_xn")
        xposed, hi_ready, lo_ready = sem("ta_xposed"), sem("ta_hi"), sem("ta_lo")
        unit = sem("ta_unit")
        e_ready, gate_half, gate_ready, val_ready = (sem("ta_e"), sem("ta_gate_o"), sem("ta_gate"),
                                                     sem("ta_val"))
        e_capped, sig_ready = sem("ta_e_capped"), sem("ta_sig")
        xT_out, gate_out, val_out = sem("ta_xT_out"), sem("ta_gate_out"), sem("ta_val_out")

        def over_tiles(eng, step):
            with eng.Fori(0, NT // 2 - 1) as i:
                for u in range(2):
                    step(2 * i + u, u, True, i)
            step(NT - 2, 0, True, NT // 2 - 1)
            step(NT - 1, 1, False, NT // 2 - 1)

        with nc.Block() as block:
            @block.sync
            def _(sp):
                sp.dma_start(x_in[:, 0, :], x_v[0]).then_inc(x_sem[0], 16)
                with nc.allow_non_contiguous_dma("norm weights by partition"):
                    sp.dma_start(g_mix[:, :], norm_mix.rearrange("l (c p) -> p (l c)", p=P)).then_inc(par_in, 16)
                sp.dma_start(hn[:, :], head_norm.to_broadcast((P, D))).then_inc(par_in, 16)
                sp.dma_start(x_in[:, 1, :], x_v[1]).then_inc(x_sem[1], 16)
                for n in range(4):
                    for k in range(KC):
                        i = n * KC + k
                        if i >= NSTAGE:
                            sp.wait_ge(w_split, i - NSTAGE + 1)
                        sp.dma_start(stage[:, i % NSTAGE, :],
                                     w_in[0, k * P:(k + 1) * P, ORDER[n]:ORDER[n] + W]
                                     ).then_inc(w_in_sem[i % NSTAGE], 16)
                sp.wait_ge(hi_ready, 1)
                sp.wait_ge(lo_ready, 1)
                sp.dma_start(S["xT_hi"][:, :, 0:P].rearrange("c p t -> p c t"), xT_hi[0][:, :, :].bitcast(F32)).then_inc(xT_out, 16)
                sp.dma_start(S["xT_lo"][:, :, 0:P].rearrange("c p t -> p c t"), xT_lo[0][:, :, :].bitcast(F32)).then_inc(xT_out, 16)

                def step(t, u, has_next, i):
                    if has_next:
                        if isinstance(t, int) is False:
                            sp.dma_start(x_in[:, u, :], x_v[bass.ds(t + 2, 1)].rearrange("o p d -> (o p) d")
                                         ).then_inc(x_sem[u], 16)
                        n = 1 - u
                        sp.wait_ge(hi_ready, t + 2)
                        sp.wait_ge(lo_ready, t + 2)
                        col = bass.ds(t * P + P, P)
                        sp.dma_start(S["xT_hi"][:, :, col].rearrange("c p t -> p c t"), xT_hi[n][:, :, :].bitcast(F32)).then_inc(xT_out, 16)
                        sp.dma_start(S["xT_lo"][:, :, col].rearrange("c p t -> p c t"), xT_lo[n][:, :, :].bitcast(F32)).then_inc(xT_out, 16)
                    row = bass.ds(t, 1)
                    sp.wait_ge(gate_ready, t + 1)
                    sp.dma_start(S["gate"][row].rearrange("o p d -> (o p) d"), gate[:, :]).then_inc(gate_out, 16)
                    sp.wait_ge(val_ready, 2 * t + 2)
                    sp.dma_start(S["val"][row].rearrange("o p d -> (o p) d"), val[:, :]).then_inc(val_out, 16)

                over_tiles(sp, step)
                sp.wait_ge(xT_out, 32 * NT)
                sp.wait_ge(gate_out, 16 * NT)
                sp.wait_ge(val_out, 16 * NT)

            @block.scalar
            def _(act):
                act.preload_act_table_set(TABLES)

                def norm(t, u, n_loaded):
                    act.wait_ge(ssq_ready, t + 1)
                    act.activation(lnv[:, :], ssq[:, :], ACT.Ln, bias=K["eps"][:, :], scale=1.0 / D)
                    act.drain()
                    act.activation(rstd[:, :], lnv[:, :], ACT.Exp, scale=-0.5)
                    act.drain()
                    act.wait_ge(x_sem[u], n_loaded)
                    act.wait_ge(xposed, t)
                    act.activation(xn[:, :], x_in[:, u, :], ACT.Copy, scale=rstd[:, 0:1]).then_inc(xn_ready, 1)

                def hi(t, u):
                    act.wait_ge(xposed, t + 1)
                    for half in range(2):
                        c = slice(4 * half, 4 * half + 4)
                        last = act.activation(xT_hi[u][:, c, :], ps_t[:, c, :], ACT.Copy)
                    last.then_inc(hi_ready, 1)

                norm(0, 0, 16)
                hi(0, 0)
                act.wait_ge(par_in, 32)
                for i in range(4 * KC):
                    n, k = divmod(i, KC)
                    act.wait_ge(w_in_sem[i % NSTAGE], 16 * (i // NSTAGE + 1))
                    act.activation(w_hi[:, n, k, :], stage[:, i % NSTAGE, :], ACT.Copy,
                                   scale=g_mix[:, k:k + 1]).then_inc(w_hid, 1)

                def step(t, u, has_next, i):
                    if has_next:
                        norm(t + 1, 1 - u, 16 * i + (16 if u == 0 else 32))
                    act.wait_ge(unit, 4 * t + 1)
                    act.wait_ge(gate_half, t)
                    act.activation(e_o[:, :], ps_u[0][:, :], ACT.Exp, scale=-1.0).then_inc(e_ready, 1)
                    act.wait_ge(unit, 4 * t + 2)
                    act.wait_ge(gate_ready, t)
                    act.activation(e_z[:, :], ps_u[1][:, :], ACT.Exp, scale=-1.0).then_inc(e_ready, 1)
                    for n, e in enumerate((e_o, e_z)):
                        act.wait_ge(e_capped, 2 * t + n + 1)
                        act.activation(e[:, :], e[:, :], ACT.Ln, bias=K["one"][:, :])
                        act.drain()
                        act.activation(e[:, :], e[:, :], ACT.Exp, scale=-1.0).then_inc(sig_ready, 1)
                    if has_next:
                        act.wait_ge(xT_out, 32 * t)
                        hi(t + 1, 1 - u)
                    act.wait_ge(val_out, 16 * t)
                    act.wait_ge(unit, 4 * t + 3)
                    act.activation(val[:, 0:W], ps_u[2][:, :], ACT.Copy).then_inc(val_ready, 1)
                    act.wait_ge(unit, 4 * t + 4)
                    act.activation(val[:, W:D], ps_u[3][:, :], ACT.Copy).then_inc(val_ready, 1)

                over_tiles(act, step)

            @block.vector
            def _(dve):
                def squares(t, u, n_loaded):
                    dve.wait_ge(x_sem[u], n_loaded)
                    dve.wait_ge(xn_ready, t)
                    dve.tensor_tensor_reduce(sq[:, :], x_in[:, u, :], x_in[:, u, :], 1.0, 0.0, ALU.mult,
                                             ALU.add, ssq[:, :]).then_inc(ssq_ready, 1)

                def lo(t, u):
                    dve.wait_ge(hi_ready, t + 1)
                    for half in range(2):
                        c = slice(4 * half, 4 * half + 4)
                        last = dve.tensor_tensor(xT_lo[u][:, c, :], ps_t[:, c, :], xT_hi[u][:, c, :].bitcast(F32),
                                                 ALU.subtract)
                    last.then_inc(lo_ready, 1)

                squares(0, 0, 16)
                lo(0, 0)
                dve.wait_ge(par_in, 32)
                for i in range(4 * KC):
                    n, k = divmod(i, KC)
                    dve.wait_ge(w_hid, i + 1)
                    dve.scalar_tensor_tensor(out=w_lo[:, n, k, :], in0=stage[:, i % NSTAGE, :],
                                             scalar=g_mix[:, k:k + 1], in1=w_hi[:, n, k, :].bitcast(F32),
                                             op0=ALU.mult, op1=ALU.subtract).then_inc(w_split, 1)

                def step(t, u, has_next, i):
                    if has_next:
                        squares(t + 1, 1 - u, 16 * i + (16 if u == 0 else 32))
                    for n, e in enumerate((e_o, e_z)):
                        dve.wait_ge(e_ready, 2 * t + n + 1)
                        dve.tensor_scalar(e[:, :], e[:, :], LN_CAP, None, ALU.min).then_inc(e_capped, 1)
                    dve.wait_ge(sig_ready, 2 * t + 1)
                    dve.wait_ge(gate_out, 16 * t)
                    dve.tensor_tensor(gate[:, 0:W], e_o[:, :], hn[:, 0:W], ALU.mult).then_inc(gate_half, 1)
                    dve.wait_ge(sig_ready, 2 * t + 2)
                    dve.tensor_tensor(e_z[:, :], e_z[:, :], ps_u[1][:, :], ALU.mult)
                    dve.drain()
                    dve.tensor_tensor(gate[:, W:D], e_z[:, :], hn[:, W:D], ALU.mult).then_inc(gate_ready, 1)
                    if has_next:
                        lo(t + 1, 1 - u)

                over_tiles(dve, step)

            @block.tensor
            def _(pe):
                def xpose(t, u):
                    pe.wait_ge(xn_ready, t + 1)
                    pe.wait_ge(lo_ready, t)
                    for c in range(KC):
                        last = pe.transpose(ps_t[:, c, :], xn[:, c * P:(c + 1) * P], K["ident"][:, :])
                    last.then_inc(xposed, 1)

                def product(t, u, n):
                    pe.wait_ge(w_split, KC * (n + 1))
                    if n == 0:
                        pe.wait_ge(e_ready, 2 * t)
                        pe.wait_ge(lo_ready, t + 1)
                    elif n == 1:
                        pe.wait_ge(gate_ready, t)
                    else:
                        pe.wait_ge(val_ready, 2 * t)
                    for k in range(KC):
                        last = mm3(pe, ps_u[n][:, :], xT_hi[u][:, k, :], xT_lo[u][:, k, :],
                                   w_hi[:, n, k, :], w_lo[:, n, k, :], k == 0, k == KC - 1)
                    last.then_inc(unit, 1)

                xpose(0, 0)

                def step(t, u, has_next, i):
                    product(t, u, 0)
                    product(t, u, 1)
                    if has_next:
                        xpose(t + 1, 1 - u)
                    product(t, u, 2)
                    product(t, u, 3)

                over_tiles(pe, step)


def project_channels(nc, sem, K, norm_mix, w_in, conv_w, conv_b, b_gate, w_gla, b_gla, S):
    NU = 13
    NV = 7
    NRES = 2 * NV + 8
    NCONV = 8
    with ExitStack() as ctx:
        def sb(name, shape, dt=F32):
            return ctx.enter_context(nc.sbuf_tensor(name, shape, dt))

        def pb(name, shape):
            return ctx.enter_context(nc.psum_tensor(name, shape, F32))

        w_hi = sb("wc_hi", [P, KC, C_ALL], F32R)
        w_lo = sb("wc_lo", [P, KC, C_ALL], F32R)
        stage = sb("wc_stage", [P, 2, C_ALL])
        xT_hi = sb("xc_hi", [P, KC, GRP], F32R)
        xT_lo = sb("xc_lo", [P, KC, GRP], F32R)
        g_mix = sb("gc_mix", [P, KC])
        cw = sb("cw", [P, CW, NCONV])
        cb = sb("cb", [P, NCONV])
        bi = sb("bi", [H, 1])
        bf = sb("bf", [H, 1])
        wg = sb("wg", [RANK, 2 * P])
        bg = sb("bg", [P, 2])
        ln_scale = sb("ln_scale", [H, 1])
        halo = sb("halo", [P, NCONV, CW - 1])
        cin = [sb(f"cin{i}", [P, GRP + CW - 1]) for i in range(2)]
        acc = [sb(f"acc{i}", [P, GRP]) for i in range(2)]
        th = [sb(f"th{i}", [P, GRP]) for i in range(2)]
        vt = th
        res = [sb(f"res{i}", [P, GRP]) for i in range(2)]
        keep_run = sb("keep_run", [P, GRP])
        max_run = sb("max_run", [H, GRP])
        IG, FG, BR, UR, CM, E1, E2, NM = [sb(f"row{i}", [H, GRP]) for i in range(8)]
        m_run = sb("m_run", [H, CPG + 1])
        dec = sb("dec", [H, CPG])
        rT = sb("rT", [RANK, GRP])
        la = sb("la", [P, GRP])
        ex = sb("ex", [P, GRP])
        Bc = sb("Bc", [P, GRP])
        gl = sb("gl", [P, CPG])
        ps_u = [pb(f"pc_u{i}", [P, GRP]) for i in range(4)]
        ps_la = pb("pc_la", [P, GRP])

        par = sem("tc_params")
        zeroed, made = sem("tc_zeroed"), sem("tc_masks")
        w_in_sem, w_hid, w_split = [sem("tc_w0"), sem("tc_w1")], sem("tc_w_hi"), sem("tc_w_split")
        halved = sem("tc_conv_halved")
        x_sem = sem("tc_x")
        unit, la_done = sem("tc_unit"), sem("tc_la")
        small_in, rT_ready = sem("tc_small"), sem("tc_rT")
        f_abs, f_log, row_args, row_exp = sem("tc_f_abs"), sem("tc_f_log"), sem("tc_row_args"), sem("tc_row_exp")
        z_ready, z_abs, z_log, b_ready = sem("tc_z"), sem("tc_z_abs"), sem("tc_z_log"), sem("tc_B")
        vt_ready, q_sub, gl_ready = sem("tc_vt"), sem("tc_q_sub"), sem("tc_gl")
        cin_ready, acc_ready, th_ready = sem("tc_cin"), sem("tc_acc"), sem("tc_tanh")
        res_ready, res_out = sem("tc_res"), [sem("tc_res_out0"), sem("tc_res_out1")]
        rows_out, gl_out = sem("tc_rows_out"), sem("tc_gl_out")

        def unit_cols(n):
            if n == 0:
                return 0, C_QKG
            if n <= 4:
                pair, is_q = (n - 1) // 2, (n - 1) % 2
                return C_QKG + (0 if is_q else 2 * P) + pair * P, P
            return C_QK + (n - 5) * P, P

        def chunks(ap):
            return ap.rearrange("p (c l) -> p c l", l=P)

        def at(ap, first):
            v = ap[:, first:GRP:P]
            return v.rearrange("p (c o) -> p c o", o=1).to_broadcast((v.shape[0], CPG, P))

        with nc.Block() as block:
            @block.gpsimd
            def _(pool):
                pool.memset(keep_run[:, :], 1.0).then_inc(zeroed, 1)
                pool.memset(max_run[:, :], 0.0).then_inc(zeroed, 1)
                pool.memset(halo[:, :, :], 0.0).then_inc(made, 1)
                pool.memset(m_run[:, :], 0.0).then_inc(made, 1)
                pool.memset(ln_scale[:, :], math.log(DV ** -0.5)).then_inc(made, 1)
                pool.memset(stage[:, :, 0:C_QKG], 0.0).then_inc(made, 1)
                pool.wait_ge(zeroed, 2)
                pool.memset(keep_run[:, 0:GRP:P], 0.0).then_inc(made, 1)
                pool.memset(max_run[:, 0:GRP:P], NEG).then_inc(made, 1)

            @block.sync
            def _(sp):
                sp.wait_ge(made, 4)
                with nc.allow_non_contiguous_dma("parameters by channel"):
                    sp.dma_start(g_mix[:, :], norm_mix.rearrange("l (c p) -> p (l c)", p=P)).then_inc(par, 16)
                    for w in range(CW):
                        sp.dma_start(cw[:, w, :], conv_w[0, w].rearrange("(m p) -> p m", p=P)).then_inc(par, 16)
                    sp.dma_start(cb[:, :], conv_b.rearrange("l (m p) -> p (l m)", p=P)).then_inc(par, 16)
                    sp.dma_start(bi[:, :], b_gate[:, 0:H].rearrange("l h -> h l")).then_inc(par, 16)
                    sp.dma_start(bf[:, :], b_gate[:, H:2 * H].rearrange("l h -> h l")).then_inc(par, 16)
                    sp.dma_start(wg[:, :], w_gla[0]).then_inc(par, 16)
                    sp.dma_start(bg[:, :], b_gla.rearrange("l (c p) -> p (l c)", p=P)).then_inc(par, 16)
                    for k in range(KC):
                        if k >= 2:
                            sp.wait_ge(w_split, k - 1)
                        r = slice(k * P, k * P + P)
                        for c, off, n in ((C_I, OFF_I, H), (C_F, OFF_F, H), (C_R, OFF_R, RANK),
                                          (C_QKG, OFF_QKG, 4 * P), (C_QK, OFF_QK, 8 * P)):
                            sp.dma_start(stage[:, k % 2, c:c + n], w_in[0, r, off:off + n]
                                         ).then_inc(w_in_sem[k % 2], 16)
                with sp.Fori(0, NG) as g:
                    tok = bass.ds(g * GRP, GRP)
                    sp.wait_ge(unit, NU * g)
                    sp.dma_start(xT_hi[:, :, :].bitcast(F32), S["xT_hi"][:, :, tok].rearrange("c p t -> p c t")).then_inc(x_sem, 16)
                    sp.dma_start(xT_lo[:, :, :].bitcast(F32), S["xT_lo"][:, :, tok].rearrange("c p t -> p c t")).then_inc(x_sem, 16)

                    def store(i, dst):
                        sp.wait_ge(res_ready, NRES * g + i + 1)
                        sp.dma_start(dst, res[i % 2][:, :]).then_inc(res_out[i % 2], 16)

                    for pair in range(2):
                        for v in range(5):
                            store(NV * pair + v, S["kR"][pair, v, :, tok])
                            if pair == 0 and v == 0:
                                sp.wait_ge(row_exp, 4 * (g + 1))
                                for q, ap in enumerate((UR, E1, E2, FG)):
                                    sp.dma_start(S["rows"][q, :, tok], ap[:, :]).then_inc(rows_out, 16)
                                sp.dma_start(S["nM"][:, tok], NM[:, :]).then_inc(rows_out, 16)
                                sp.dma_start(S["dec"][:, bass.ds(g * CPG, CPG)], dec[:, :]).then_inc(rows_out, 16)
                        sp.wait_ge(gl_ready, 2 * g + pair + 1)
                        sp.dma_start(S["gl"][pair, :, bass.ds(g * CPG, CPG)], gl[:, :]).then_inc(gl_out, 16)
                        for v in range(2):
                            store(NV * pair + 5 + v, S["qG"][pair, v, :, tok])
                    for m in range(NCONV):
                        store(2 * NV + m, S["qk"][m, :, tok])
                for b in range(2):
                    sp.wait_ge(res_out[b], 16 * NG * NRES // 2)
                sp.wait_ge(rows_out, 16 * 6 * NG)
                sp.wait_ge(gl_out, 16 * 2 * NG)

            @block.tensor
            def _(pe):
                pe.wait_ge(par, 16 * 10)
                pe.wait_ge(w_split, KC)
                with pe.Fori(0, NG) as g:
                    pe.wait_ge(x_sem, 32 * g + 32)

                    def product(n, producer_free):
                        for s, v in producer_free:
                            pe.wait_ge(s, v)
                        c, m = unit_cols(n)
                        for k in range(KC):
                            last = mm3(pe, ps_u[n % 4][0:m, :], w_hi[:, k, c:c + m], w_lo[:, k, c:c + m],
                                       xT_hi[:, k, :], xT_lo[:, k, :], k == 0, k == KC - 1)
                        last.then_inc(unit, 1)

                    def gate(pair):
                        pe.wait_ge(rT_ready, g + 1)
                        pe.wait_ge(z_ready, 2 * g + pair)
                        pe.matmul(ps_la[:, :], wg[:, pair * P:(pair + 1) * P], rT[:, :],
                                  start=True, stop=True).then_inc(la_done, 1)

                    product(0, [(cin_ready, NCONV * g)])
                    product(1, [])
                    gate(0)
                    product(2, [])
                    gate(1)
                    product(3, [])
                    product(4, [(small_in, 2 * g + 2), (rT_ready, g + 1)])
                    product(5, [(res_ready, NRES * g + 5)])
                    product(6, [(res_ready, NRES * g + NV)])
                    product(7, [(res_ready, NRES * g + NV + 5)])
                    product(8, [(res_ready, NRES * g + 2 * NV)])
                    for n in range(9, NU):
                        product(n, [(cin_ready, NCONV * g + n - 8)])

            @block.scalar
            def _(act):
                act.preload_act_table_set(TABLES)
                act.wait_ge(par, 16 * 10)
                act.wait_ge(made, 6)
                for k in range(KC):
                    act.wait_ge(w_in_sem[k % 2], 80 * (k // 2 + 1))
                    act.activation(w_hi[:, k, :], stage[:, k % 2, :], ACT.Copy,
                                   scale=g_mix[:, k:k + 1]).then_inc(w_hid, 1)
                with act.Fori(0, NG) as g:
                    act.preload_act_table_set(TABLES)
                    act.wait_ge(unit, NU * g + 1)
                    act.wait_ge(la_done, 2 * g)
                    act.activation(rT[:, :], ps_u[0][C_R:C_R + RANK, :], ACT.Copy).then_inc(rT_ready, 1)
                    act.wait_ge(rows_out, 96 * g)
                    act.activation(IG[:, :], ps_u[0][C_I:C_I + H, :], ACT.Copy).then_inc(small_in, 1)
                    act.activation(FG[:, :], ps_u[0][C_F:C_F + H, :], ACT.Copy).then_inc(small_in, 1)
                    act.wait_ge(f_abs, g + 1)
                    act.activation(E1[:, :], E1[:, :], ACT.Exp)
                    act.drain()
                    act.activation(E1[:, :], E1[:, :], ACT.Ln, bias=K["one"][0:H, :]).then_inc(f_log, 1)
                    for pair in range(2):
                        j = 2 * g + pair
                        act.wait_ge(la_done, j + 1)
                        act.wait_ge(b_ready, j)
                        act.activation(la[:, :], ps_la[:, :], ACT.Identity, bias=bg[:, pair:pair + 1]).then_inc(z_ready, 1)
                        act.wait_ge(z_abs, j + 1)
                        act.activation(ex[:, :], ex[:, :], ACT.Exp)
                        act.drain()
                        act.activation(ex[:, :], ex[:, :], ACT.Ln, bias=K["one"][:, :]).then_inc(z_log, 1)
                        if pair == 0:
                            act.wait_ge(row_args, g + 1)
                            act.activation(E1[:, :], E1[:, :], ACT.Exp).then_inc(row_exp, 1)
                            act.activation(E2[:, :], E2[:, :], ACT.Exp, scale=-1.0).then_inc(row_exp, 1)
                            act.activation(FG[:, :], FG[:, :], ACT.Exp, bias=ln_scale[:, :]).then_inc(row_exp, 1)
                            act.activation(dec[:, :], dec[:, :], ACT.Exp).then_inc(row_exp, 1)
                        act.wait_ge(b_ready, j + 1)
                        for v in range(5):
                            i = NV * pair + v
                            if i >= 2:
                                act.wait_ge(res_ready, NRES * g + i - 1)
                            first = SUB * v + SUB // 2 - 1 if v < NSUB else P - 1
                            for c in range(CPG):
                                a = c * P
                                last = act.activation(vt[i % 2][:, a:a + P], Bc[:, a:a + P], ACT.Exp,
                                                      scale=-1.0, bias=Bc[:, a + first:a + first + 1])
                            last.then_inc(vt_ready, 1)
                        act.wait_ge(gl_out, 16 * j)
                        act.activation(gl[:, :], Bc[:, P - 1:GRP:P], ACT.Exp).then_inc(gl_ready, 1)
                        i = NV * pair + 5
                        act.wait_ge(res_ready, NRES * g + i - 1)
                        act.activation(vt[i % 2][:, :], Bc[:, :], ACT.Exp).then_inc(vt_ready, 1)
                        i += 1
                        act.wait_ge(q_sub, j + 1)
                        act.activation(vt[i % 2][:, :], vt[i % 2][:, :], ACT.Exp).then_inc(vt_ready, 1)
                    act.preload_act_table_set("exp_and_others")

                    def copy_in(m):
                        b = m % 2
                        act.wait_ge(unit, NU * g + 6 + m)
                        act.wait_ge(acc_ready, NCONV * g + m - 1) if m >= 2 else act.wait_ge(acc_ready, NCONV * g)
                        act.activation(cin[b][:, CW - 1:CW - 1 + GRP], ps_u[(5 + m) % 4][:, :], ACT.Copy).then_inc(cin_ready, 1)

                    def tanh(m):
                        act.wait_ge(acc_ready, NCONV * g + m + 1)
                        act.wait_ge(res_ready, NRES * g + 2 * NV + max(m - 1, 0))
                        act.activation(th[m % 2][:, :], acc[m % 2][:, :], ACT.Tanh).then_inc(th_ready, 1)

                    copy_in(0)
                    for m in range(1, NCONV):
                        copy_in(m)
                        tanh(m - 1)
                    tanh(NCONV - 1)

            @block.vector
            def _(dve):
                dve.wait_ge(par, 16 * 10)
                dve.wait_ge(made, 6)
                for k in range(KC):
                    dve.wait_ge(w_hid, k + 1)
                    dve.scalar_tensor_tensor(out=w_lo[:, k, :], in0=stage[:, k % 2, :],
                                             scalar=g_mix[:, k:k + 1], in1=w_hi[:, k, :].bitcast(F32),
                                             op0=ALU.mult, op1=ALU.subtract).then_inc(w_split, 1)
                dve.tensor_scalar(cw[:, :, :], cw[:, :, :], 0.5, None, ALU.mult)
                dve.tensor_scalar(cb[:, :], cb[:, :], 0.5, None, ALU.mult)
                dve.drain()
                with dve.Fori(0, NG) as g:
                    dve.wait_ge(small_in, 2 * g + 2)
                    dve.tensor_scalar(IG[:, :], IG[:, :], bi[:, 0:1], None, ALU.add)
                    dve.tensor_scalar(FG[:, :], FG[:, :], bf[:, 0:1], None, ALU.add)
                    dve.drain()
                    neg_abs(dve, E1[:, :], FG[:, :]).then_inc(f_abs, 1)

                    def z_abs_step(pair):
                        dve.wait_ge(z_ready, 2 * g + pair + 1)
                        neg_abs(dve, ex[:, :], la[:, :]).then_inc(z_abs, 1)

                    z_abs_step(0)
                    dve.wait_ge(f_log, g + 1)
                    dve.scalar_tensor_tensor(out=FG[:, :], in0=FG[:, :], scalar=0.0, in1=E1[:, :],
                                             op0=ALU.min, op1=ALU.subtract)
                    dve.drain()
                    dve.tensor_tensor_scan(BR[:, :], keep_run[0:H, :], FG[:, :], 0.0, ALU.mult, ALU.add)
                    dve.drain()
                    dve.tensor_tensor(UR[:, :], IG[:, :], BR[:, :], ALU.subtract)
                    dve.drain()
                    dve.tensor_tensor_scan(CM[:, :], max_run[:, :], UR[:, :], NEG, ALU.add, ALU.max)
                    dve.tensor_copy(m_run[:, 0:1], m_run[:, CPG:CPG + 1])
                    dve.drain()
                    dve.tensor_tensor_scan(m_run[:, 1:CPG + 1], CM[:, P - 1:GRP:P], BR[:, P - 1:GRP:P],
                                           m_run[:, 0:1], ALU.max, ALU.add)
                    dve.drain()
                    m_bc = m_run[:, 0:CPG].rearrange("p (c o) -> p c o", o=1).to_broadcast((H, CPG, P))
                    dve.tensor_tensor(chunks(CM[:, :]), chunks(CM[:, :]), m_bc, ALU.max)
                    dve.drain()
                    dve.tensor_tensor(chunks(E1[:, :]), m_bc, chunks(CM[:, :]), ALU.subtract)
                    dve.tensor_tensor(E2[:, :], BR[:, :], CM[:, :], ALU.add)
                    dve.tensor_scalar(NM[:, :], CM[:, :], -1.0, None, ALU.mult)
                    dve.tensor_tensor(chunks(FG[:, :]), chunks(UR[:, :]), at(CM, P - 1), ALU.subtract)
                    dve.tensor_tensor(dec[:, :], m_run[:, 0:CPG], CM[:, P - 1:GRP:P], ALU.subtract).then_inc(row_args, 1)

                    def result(i, producer, out_fn):
                        dve.wait_ge(res_out[i % 2], 8 * NRES * g + 16 * (i // 2))
                        dve.wait_ge(*producer)
                        out_fn(res[i % 2][:, :]).then_inc(res_ready, 1)

                    for pair in range(2):
                        j = 2 * g + pair
                        if pair:
                            z_abs_step(1)
                        dve.wait_ge(z_log, j + 1)
                        dve.scalar_tensor_tensor(out=la[:, :], in0=la[:, :], scalar=0.0, in1=ex[:, :],
                                                 op0=ALU.min, op1=ALU.subtract)
                        dve.drain()
                        dve.tensor_scalar(la[:, :], la[:, :], 1.0 / 16.0, None, ALU.mult)
                        dve.drain()
                        dve.tensor_tensor_scan(Bc[:, :], keep_run[:, :], la[:, :], 0.0, ALU.mult, ALU.add).then_inc(b_ready, 1)
                        kps, qps = ps_u[(1 + 2 * pair) % 4], ps_u[(2 + 2 * pair) % 4]
                        dve.wait_ge(unit, NU * g + 2 + 2 * pair)
                        for v in range(5):
                            i = NV * pair + v
                            result(i, (vt_ready, 2 * NV * g + i + 1), lambda o: dve.scalar_tensor_tensor(
                                out=o, in0=vt[i % 2][:, :], scalar=VT_CAP, in1=kps[:, :], op0=ALU.min, op1=ALU.mult))
                        i = NV * pair + 6
                        blocks = Bc[:, :].rearrange("p (b l) -> p b l", l=SUB)
                        ref = Bc[:, SUB // 2 - 1:GRP:SUB].rearrange("p (b o) -> p b o", o=1).to_broadcast((P, GRP // SUB, SUB))
                        dve.drain()
                        dve.wait_ge(unit, NU * g + 3 + 2 * pair)
                        dve.tensor_tensor(vt[i % 2][:, :].rearrange("p (b l) -> p b l", l=SUB), blocks, ref,
                                          ALU.subtract).then_inc(q_sub, 1)
                        for v in (5, 6):
                            i = NV * pair + v
                            result(i, (vt_ready, 2 * NV * g + i + 1), lambda o: dve.scalar_tensor_tensor(
                                out=o, in0=qps[:, :], scalar=DK ** -0.5, in1=vt[i % 2][:, :], op0=ALU.mult, op1=ALU.mult))

                    def conv(m):
                        b = m % 2
                        dve.wait_ge(cin_ready, NCONV * g + m + 1)
                        dve.tensor_copy(cin[b][:, 0:CW - 1], halo[:, m, :])
                        dve.drain()
                        dve.tensor_scalar(acc[b][:, :], cin[b][:, 0:GRP], cw[:, 0, m:m + 1], cb[:, m:m + 1], ALU.mult, ALU.add)
                        dve.tensor_copy(halo[:, m, :], cin[b][:, GRP:GRP + CW - 1])
                        for w in range(1, CW):
                            dve.drain()
                            last = dve.scalar_tensor_tensor(out=acc[b][:, :], in0=cin[b][:, w:w + GRP],
                                                            scalar=cw[:, w, m:m + 1], in1=acc[b][:, :],
                                                            op0=ALU.mult, op1=ALU.add)
                        last.then_inc(acc_ready, 1)

                    def silu(m):
                        i = 2 * NV + m
                        result(i, (th_ready, NCONV * g + m + 1), lambda o: dve.scalar_tensor_tensor(
                            out=o, in0=th[m % 2][:, :], scalar=1.0, in1=acc[m % 2][:, :], op0=ALU.add, op1=ALU.mult))

                    conv(0)
                    for m in range(1, NCONV):
                        conv(m)
                        silu(m - 1)
                    silu(NCONV - 1)


def recur(nc, sem, K, S):
    DA = DV + 1
    with ExitStack() as ctx:
        def sb(name, shape, dt=F32):
            return ctx.enter_context(nc.sbuf_tensor(name, shape, dt))

        def pb(name, shape):
            return ctx.enter_context(nc.psum_tensor(name, shape, F32))

        qk = [sb(f"r_qk{i}", [P, 2 * H, P]) for i in range(2)]
        kr = [sb(f"r_kr{i}", [P, 2, 5, P]) for i in range(2)]
        q2 = [sb(f"r_q2{i}", [P, 2, 2, 2, P]) for i in range(2)]
        va = [sb(f"r_va{i}", [P, H, DA]) for i in range(2)]
        vg = [sb(f"r_vg{i}", [P, H, P]) for i in range(2)]
        gate = [sb(f"r_gate{i}", [P, D]) for i in range(2)]
        rowT = [sb(f"r_row{i}", [4 * H, P]) for i in range(2)]
        nM = [sb(f"r_nM{i}", [P, H, P]) for i in range(2)]
        dec = sb("r_dec", [P, H, NT])
        gl = sb("r_gl", [P, 2, NT])
        cols = sb("r_cols", [P, 4 * H])
        U, A, EN, WC = 0, H, 2 * H, 3 * H
        arg = sb("r_arg", [P, H, P])
        pm = sb("r_pm", [P, H, P])
        sT = sb("r_sT", [P, H, P])
        kw = sb("r_kw", [P, H, P])
        kd = sb("r_kd", [P, 2, P])
        aT = sb("r_aT", [P, 2 * H // 2, P])
        qc = sb("r_qc", [P, H, DA])
        num = sb("r_num", [P, H, DA])
        nd = sb("r_nd", [P, H])
        hm = sb("r_hm", [P, H, P])
        junk = sb("r_junk", [P, P])
        junk2 = sb("r_junk2", [P, P])
        ms = sb("r_ms", [P, 2 * H])
        ms_ln = sb("r_msln", [P, 2 * H])
        rs = sb("r_rs", [P, 2 * H])
        y = sb("r_y", [P, D])
        C = sb("r_C", [P, H, DA])
        zero = sb("r_zero", [P, D])
        G = sb("r_G", [P, 2, P])
        bank = [pb(f"r_ps{i}", [P, 512]) for i in range(8)]
        ps_qk = bank[0][:, :].rearrange("p (h j) -> p h j", h=H)
        ps_o = ps_qk
        ps_k = bank[1][:, :].rearrange("p (h j) -> p h j", h=H)
        ps_gkv = bank[1][:, :].rearrange("p (h j) -> p h j", h=2)
        ps_kd = bank[2][:, 0:2 * P].rearrange("p (h j) -> p h j", h=2)
        ps_cols = bank[2][:, 2 * P:2 * P + 4 * H]
        ps_a = bank[3][:, :].rearrange("p (h j) -> p h j", h=H)

        def head(b, h):
            if h < 3:
                return bank[4 + b][:, h * DA:(h + 1) * DA]
            return bank[7][:, b * DA:(b + 1) * DA]

        N_, C_, KV_ = 0, 1, 2

        fixed, made = sem("rc_fixed"), sem("rc_made")
        zero_made, zeroed = sem("rc_zero"), sem("rc_zeroed")
        loaded = [sem("rc_loaded0"), sem("rc_loaded1")]
        NL = 9
        scored, turned, a_done = sem("rc_scored"), sem("rc_turned"), sem("rc_a_done")
        qc_done, n_done, kv_done = sem("rc_qC"), sem("rc_num"), sem("rc_kv")
        o_done, gkv_done = sem("rc_o"), sem("rc_gkv")
        arg_ready, cols_ready, pm_ready = sem("rc_arg"), sem("rc_cols"), sem("rc_pm")
        kw_ready, kd_ready, qcs_ready = sem("rc_kw"), sem("rc_kd"), sem("rc_qcs")
        sT_ready, aT_ready, num_ready = sem("rc_sT"), sem("rc_aT"), sem("rc_num_sum")
        hm_ready, ms_m, ms_g, rs_ready = sem("rc_hm"), sem("rc_ms_m"), sem("rc_ms_g"), sem("rc_rs")
        y_ready, y_out, C_ready, G_ready = sem("rc_y"), sem("rc_y_out"), sem("rc_C"), sem("rc_G")

        def over_tiles(eng, step):
            with eng.Fori(0, NT // 2) as i:
                for u in range(2):
                    step(2 * i + u, u, i)

        with nc.Block() as block:
            @block.gpsimd
            def _(pool):
                pool.memset(C[:, :, :], 0.0).then_inc(made, 1)
                pool.memset(G[:, :, :], 0.0).then_inc(made, 1)
                for u in range(2):
                    pool.memset(q2[u][:, :, :, :, :], 0.0).then_inc(made, 1)
                    pool.memset(va[u][:, :, DV:DA], 1.0).then_inc(made, 1)

                def step(t, u, i):
                    pool.wait_ge(loaded[u], 16 * NL * i + 16 * NL)
                    pool.wait_ge(pm_ready, t)
                    pool.tensor_tensor(arg[:, :, :], nM[u][:, :, :],
                                       K["drop"][:, :].rearrange("p (o j) -> p o j", o=1).to_broadcast((P, H, P)),
                                       ALU.add).then_inc(arg_ready, 1)

                pool.memset(zero[:, :], 0.0).then_inc(zero_made, 1)
                pool.wait_ge(zero_made, 1)
                for n in range(0, YB, YB // 5):
                    pool.dma_start(S["ys"][n * P:(n + YB // 5) * P, :].rearrange("(n p) d -> p n d", p=P),
                                   zero[:, :].rearrange("p (o d) -> p o d", o=1).to_broadcast((P, YB // 5, D))
                                   ).then_inc(zeroed, 16)
                over_tiles(pool, step)
                pool.wait_ge(zeroed, 5 * 16)

            @block.sync
            def _(sp):
                sp.dma_start(dec[:, :, :].rearrange("p h c -> p (h c)"),
                             S["dec"].rearrange("(o h) c -> o (h c)", o=1).to_broadcast((P, H * NT))).then_inc(fixed, 16)
                sp.dma_start(gl[:, :, :], S["gl"].rearrange("q p c -> p q c")).then_inc(fixed, 16)
                sp.wait_ge(made, 6)

                def step(t, u, waits):
                    first, tile = (sp.snap(t * P), sp.snap(t)) if waits else (t * P, t)
                    tok, row = bass.ds(first, P), bass.ds(tile, 1)
                    if waits:
                        sp.wait_ge(y_ready, t - 1)
                        sp.wait_ge(gkv_done, t - 1)

                    def load(dst, src):
                        sp.dma_start(dst, src).then_inc(loaded[u], 16)

                    load(qk[u][:, :, :], S["qk"][:, :, tok].rearrange("m p t -> p m t"))
                    load(rowT[u][:, :], S["rows"][:, :, tok].rearrange("q h t -> (q h) t"))
                    load(nM[u][:, :, :], S["nM"][:, tok].rearrange("(o h) t -> o h t", o=1).to_broadcast((P, H, P)))
                    load(kr[u][:, :, :, :], S["kR"][:, :, :, tok].rearrange("q v p t -> p q v t"))
                    for h in range(2):
                        r = slice(h * DK, (h + 1) * DK)
                        load(q2[u][r, :, :, h, :], S["qG"][:, :, r, tok].rearrange("q v p t -> p q v t"))
                    load(va[u][:, :, 0:DV], S["val"][row, :, 0:W].rearrange("o p (h d) -> (o p) h d", h=H))
                    load(vg[u][:, :, :], S["val"][row, :, W:D].rearrange("o p (h d) -> (o p) h d", h=H))
                    load(gate[u][:, :], S["gate"][row].rearrange("o p d -> (o p) d"))

                step(0, 0, False)
                step(1, 1, False)
                with sp.Fori(1, NT // 2) as i:
                    for u in range(2):
                        step(2 * i + u, u, True)
                sp.wait_ge(y_out, 16 * NT)

            @block.tensor
            def _(pe):
                pe.wait_ge(made, 6)

                def step(t, u, i):
                    pe.wait_ge(loaded[u], 16 * NL * i + 16 * NL)
                    pe.wait_ge(y_ready, t)
                    for h in range(H):
                        last = pe.matmul(ps_qk[:, h, :], qk[u][:, H + h, :], qk[u][:, h, :], start=True, stop=True)
                    last.then_inc(scored, 1)
                    pe.wait_ge(cols_ready, t)
                    pe.wait_ge(kd_ready, t)
                    pe.wait_ge(G_ready, t)
                    for h in range(H):
                        pe.transpose(ps_k[:, h, :], qk[u][:, H + h, :], K["ident"][:, :])
                    for q in range(2):
                        pe.transpose(ps_kd[:, q, :], kr[u][:, q, 4, :], K["ident"][:, :])
                    last = pe.transpose(ps_cols, rowT[u][:, :], K["ident"][0:4 * H, 0:4 * H])
                    last.then_inc(turned, 1)
                    pe.wait_ge(aT_ready, t)
                    for q in range(2):
                        for r in range(NSUB):
                            j = slice(r * SUB, (r + 1) * SUB)
                            last = pe.matmul(ps_a[:, 2 * q:2 * q + 2, j], kr[u][:, q, r, :], q2[u][:, q, 1, :, j],
                                             start=True, stop=True)
                    last.then_inc(a_done, 1)
                    pe.wait_ge(C_ready, t)
                    pe.wait_ge(qcs_ready, t)
                    pe.wait_ge(num_ready, t)
                    for h in range(H):
                        last = pe.matmul(head(C_, h), qk[u][:, h, :], C[:, h, :], start=True, stop=True)
                    last.then_inc(qc_done, 1)
                    pe.wait_ge(kw_ready, t + 1)
                    for h in range(H):
                        last = pe.matmul(head(KV_, h), kw[:, h, :], va[u][:, h, :], start=True, stop=True)
                    last.then_inc(kv_done, 1)
                    pe.wait_ge(sT_ready, t + 1)
                    for h in range(H):
                        last = pe.matmul(head(N_, h), sT[:, h, :], va[u][:, h, :], start=True, stop=True)
                    last.then_inc(n_done, 1)
                    pe.wait_ge(aT_ready, t + 1)
                    pe.wait_ge(G_ready, t)
                    for h in range(H):
                        pe.matmul(ps_o[:, h, :], aT[:, h, :], vg[u][:, h, :], start=True, stop=False)
                        last = pe.matmul(ps_o[:, h, :], q2[u][:, h // 2, 0, h % 2, :], G[:, h // 2, :],
                                         start=False, stop=True)
                    last.then_inc(o_done, 1)
                    pe.wait_ge(kd_ready, t + 1)
                    for q in range(2):
                        last = pe.matmul(ps_gkv[:, q, :], kd[:, q, :],
                                         vg[u][:, 2 * q:2 * q + 2, :].rearrange("p h d -> p (h d)"), start=True, stop=True)
                    last.then_inc(gkv_done, 1)

                over_tiles(pe, step)

            @block.scalar
            def _(act):
                act.preload_act_table_set(TABLES)

                def step(t, u, i):
                    act.wait_ge(turned, t + 1)
                    act.wait_ge(num_ready, t)
                    act.activation(cols[:, :], ps_cols, ACT.Copy).then_inc(cols_ready, 1)
                    act.drain()
                    act.wait_ge(arg_ready, t + 1)
                    act.wait_ge(sT_ready, t)
                    for h in range(H):
                        last = act.activation(pm[:, h, :], arg[:, h, :], ACT.Exp, bias=cols[:, U + h:U + h + 1])
                    last.then_inc(pm_ready, 1)
                    act.wait_ge(kv_done, t)
                    for h in range(H):
                        last = act.activation(kw[:, h, :], ps_k[:, h, :], ACT.Copy, scale=cols[:, WC + h:WC + h + 1])
                    last.then_inc(kw_ready, 1)
                    act.wait_ge(gkv_done, t)
                    act.activation(kd[:, :, :], ps_kd, ACT.Copy).then_inc(kd_ready, 1)
                    act.wait_ge(n_done, t + 1)
                    act.wait_ge(num_ready, t)
                    for h in range(H):
                        last = act.activation(qc[:, h, :], head(C_, h), ACT.Copy, scale=cols[:, A + h:A + h + 1])
                    last.then_inc(qcs_ready, 1)
                    act.wait_ge(o_done, t + 1)
                    act.wait_ge(rs_ready, t)
                    for h in range(H):
                        last = act.activation(junk2[:, :], ps_o[:, h, :], ACT.Square, accum_out=ms[:, H + h:H + h + 1])
                        act.drain()
                    act.wait_ge(ms_m, t + 1)
                    act.activation(ms_ln[:, :], ms[:, :], ACT.Ln, scale=1.0 / DV, bias=K["eps"][:, :])
                    act.drain()
                    act.wait_ge(y_ready, t)
                    act.activation(rs[:, :], ms_ln[:, :], ACT.Exp, scale=-0.5).then_inc(rs_ready, 1)
                    act.wait_ge(y_ready, t + 1)
                    act.dma_start(S["y"][bass.ds(t, 1)].rearrange("o p d -> (o p) d"), y[:, :]).then_inc(y_out, 16)

                over_tiles(act, step)

            @block.vector
            def _(dve):
                dve.wait_ge(fixed, 32)

                def step(t, u, i):
                    dve.wait_ge(scored, t + 1)
                    dve.wait_ge(n_done, t)
                    dve.wait_ge(pm_ready, t + 1)
                    dve.scalar_tensor_tensor(out=sT[:, :, :], in0=ps_qk, scalar=DV ** -0.5, in1=pm[:, :, :],
                                             op0=ALU.mult, op1=ALU.mult).then_inc(sT_ready, 1)
                    dve.wait_ge(a_done, t + 1)
                    dve.wait_ge(o_done, t)
                    dve.tensor_tensor(aT[:, :, :], ps_a,
                                      K["keep"][:, :].rearrange("p (o j) -> p o j", o=1).to_broadcast((P, H, P)),
                                      ALU.mult).then_inc(aT_ready, 1)
                    dve.wait_ge(qcs_ready, t + 1)
                    for h in range(H):
                        last = dve.scalar_tensor_tensor(out=C[:, h, :], in0=C[:, h, :], scalar=dec[:, h, bass.ds(t, 1)],
                                                        in1=head(KV_, h), op0=ALU.mult, op1=ALU.add)
                    last.then_inc(C_ready, 1)
                    dve.wait_ge(n_done, t + 1)
                    dve.wait_ge(qcs_ready, t + 1)
                    dve.tensor_tensor(num[:, 0:3, :], qc[:, 0:3, :],
                                      bank[4][:, 0:3 * DA].rearrange("p (h d) -> p h d", d=DA), ALU.add)
                    dve.tensor_tensor(num[:, 3, :], qc[:, 3, :], head(N_, 3), ALU.add).then_inc(num_ready, 1)
                    dve.drain()
                    den = num[:, :, DV:DA].rearrange("p h o -> p (h o)")
                    dve.scalar_tensor_tensor(out=nd[:, :], in0=den, scalar=-1.0, in1=den, op0=ALU.mult, op1=ALU.max)
                    dve.drain()
                    dve.tensor_tensor(nd[:, :], nd[:, :], cols[:, EN:EN + H], ALU.max)
                    dve.drain()
                    dve.reciprocal(nd[:, :], nd[:, :])
                    dve.drain()
                    dve.tensor_tensor(hm[:, :, :], num[:, :, 0:DV],
                                      nd[:, :].rearrange("p (h o) -> p h o", o=1).to_broadcast((P, H, DV)), ALU.mult)
                    dve.drain()
                    dve.wait_ge(rs_ready, t)
                    for h in range(H):
                        last = dve.tensor_tensor_reduce(junk[:, :], hm[:, h, :], hm[:, h, :], 1.0, 0.0, ALU.mult, ALU.add,
                                                        ms[:, h:h + 1])
                        if h == H - 1:
                            last.then_inc(ms_m, 1)
                        dve.drain()
                    dve.wait_ge(rs_ready, t + 1)
                    dve.wait_ge(y_out, 16 * t)
                    for h in range(2 * H):
                        c = slice(h * DV, (h + 1) * DV)
                        src = hm[:, h, :] if h < H else ps_o[:, h - H, :]
                        last = dve.scalar_tensor_tensor(out=y[:, c], in0=src, scalar=rs[:, h:h + 1], in1=gate[u][:, c],
                                                        op0=ALU.mult, op1=ALU.mult)
                    last.then_inc(y_ready, 1)
                    dve.wait_ge(gkv_done, t + 1)
                    for h in range(H):
                        r = slice((h % 2) * DK, (h % 2 + 1) * DK)
                        last = dve.scalar_tensor_tensor(out=G[r, h // 2, :], in0=G[r, h // 2, :],
                                                        scalar=gl[r, h // 2, bass.ds(t, 1)],
                                                        in1=ps_gkv[r, h // 2, (h % 2) * P:(h % 2 + 1) * P],
                                                        op0=ALU.mult, op1=ALU.add)
                    last.then_inc(G_ready, 1)

                over_tiles(dve, step)


def project_out_and_route(nc, sem, K, x, w_out, norm_ffn, w_group, b_group, w_expert, b_expert, S, R):
    x_v = x.rearrange("b (t p) d -> (b t) p d", p=P)
    NLG = NGRP + NE
    NS = (NBLK + 1) * P
    with ExitStack() as ctx:
        def sb(name, shape, dt=F32):
            return ctx.enter_context(nc.sbuf_tensor(name, shape, dt))

        def pb(name, shape):
            return ctx.enter_context(nc.psum_tensor(name, shape, F32))

        w_hi = sb("wo_hi", [P, KC, D], F32R)
        w_lo = sb("wo_lo", [P, KC, D], F32R)
        stage = sb("wo_stage", [P, 2, D])
        w_r = sb("w_router", [P, KC, NLG])
        b_r = sb("b_router", [P, NLG])
        nf = sb("norm_ffn_bc", [P, D])
        y_in = [sb(f"y_in{i}", [P, D]) for i in range(2)]
        x_in = [sb(f"xr_in{i}", [P, D]) for i in range(2)]
        yT_hi = [sb(f"yT_hi{i}", [P, KC, P], F32R) for i in range(2)]
        yT_lo = [sb(f"yT_lo{i}", [P, KC, P], F32R) for i in range(2)]
        h1 = [sb(f"h1_{i}", [P, D]) for i in range(2)]
        xt = [sb(f"xt_{i}", [P, D]) for i in range(2)]
        xtT = sb("xtT", [P, KC, P])
        sq = sb("sq_c", [P, D])
        ssq = sb("ssq_c", [P, 1])
        lnv = sb("lnv_c", [P, 1])
        rstd = sb("rstd_c", [P, 1])
        lg = sb("lg", [P, NLG])
        g8 = sb("g8", [P, 8])
        gm = sb("gm", [P, 8])
        gi = sb("gi", [P, 8], U32)
        gif = sb("gif", [P, 1])
        ngm = sb("ngm", [P, 1])
        gex = sb("gex", [P, NGRP])
        gsum = sb("gsum", [P, 1])
        og = sb("og", [P, NGRP])
        selg = sb("selg", [P, NGRP, EPG])
        sel = sb("sel", [P, EPG])
        em = sb("em", [P, 8])
        ei = sb("ei", [P, 8], U32)
        eif = sb("eif", [P, 2])
        nem = sb("nem", [P, 1])
        e2 = sb("e2", [P, 1])
        den = sb("den_r", [P, 1])
        iota = sb("iota", [P, NE])
        oh = sb("oh", [P, NT, 2, NE])
        cnt = sb("cnt", [P, NT + 1, NE])
        both = sb("both", [P, NT, NE])
        ids = sb("ids", [P, NT], I32)
        zero = sb("zero_ids", [P, NBLK + 1], I32)
        total = sb("total", [P, NE])
        nbi = sb("nbi", [P, NE], I32)
        nbf = sb("nbf", [P, NE])
        base = sb("base", [P, NE])
        incl = sb("incl", [P, NE])
        rank = sb("rank", [P, NT, NE])
        pick = sb("pick", [P, NT, 2, NE])
        posf = sb("posf", [P, NT * 2])
        ps_y = pb("pr_y", [P, KC, P])
        ps_o = pb("pr_o", [P, D])
        ps_x = pb("pr_x", [P, KC, P])
        ps_l = pb("pr_l", [P, 512])
        ps_c = pb("pr_c", [P, 512])

        par, made = sem("rt_params"), sem("rt_made")
        w_in_sem, w_hid, w_split = [sem("rt_w0"), sem("rt_w1")], sem("rt_w_hi"), sem("rt_w_split")
        y_sem, x_sem = [sem("rt_y0"), sem("rt_y1")], [sem("rt_x0"), sem("rt_x1")]
        y_turned, hi_ready, lo_ready = sem("rt_y_turned"), sem("rt_hi"), sem("rt_lo")
        out_done, h1_ready, ssq_ready = sem("rt_out"), sem("rt_h1"), sem("rt_ssq")
        scaled, xt_ready, x_turned, xtT_ready = sem("rt_scaled"), sem("rt_xt"), sem("rt_x_turned"), sem("rt_xtT")
        lg_done, ngm_ready, gsum_ready = sem("rt_logits"), sem("rt_ngm"), sem("rt_gsum")
        nem_ready, e2_ready, routed = sem("rt_nem"), sem("rt_e2"), sem("rt_routed")
        h1_out, xt_out = [sem("rt_h1_out0"), sem("rt_h1_out1")], [sem("rt_xt_out0"), sem("rt_xt_out1")]
        counted, ranked, pos_ready, cleared = sem("rt_counted"), sem("rt_ranked"), sem("rt_pos"), sem("rt_cleared")
        scattered = sem("rt_scattered")

        def over_tiles(eng, step):
            with eng.Fori(0, NT // 2) as i:
                for u in range(2):
                    step(2 * i + u, u, i)

        with nc.Block() as block:
            @block.gpsimd
            def _(pool):
                pool.iota(iota[:, :], [[1, NE]], base=0, channel_multiplier=0,
                          allow_small_or_imprecise_dtypes=True).then_inc(made, 1)
                pool.iota(ids[:, :], [[P, NT]], base=0, channel_multiplier=1).then_inc(made, 1)
                pool.memset(zero[:, :], 0).then_inc(made, 1)
                pool.memset(g8[:, :], -3.0e38).then_inc(made, 1)
                pool.memset(cnt[:, 0, :], 0.0).then_inc(made, 1)
                pool.wait_ge(made, 5)
                pool.dma_start(S["slots"].rearrange("(p n) o -> p (n o)", p=P), zero[:, :]).then_inc(cleared, 16)
                pool.wait_ge(cleared, 16)
                pool.wait_ge(pos_ready, 1)
                for j in range(2 * NT):
                    pool.indirect_dma_start(S["slots"], bass.IndirectOffsetOnAxis(ap=R["pos"][:, j:j + 1], axis=0),
                                            ids[:, j // 2:j // 2 + 1], None).then_inc(scattered, 16)
                pool.wait_ge(scattered, 16 * 2 * NT)

            @block.sync
            def _(sp):
                sp.dma_start(y_in[0][:, :], S["y"][0]).then_inc(y_sem[0], 16)
                sp.dma_start(x_in[0][:, :], x_v[0]).then_inc(x_sem[0], 16)
                for k in range(KC):
                    if k >= 2:
                        sp.wait_ge(w_split, k - 1)
                    sp.dma_start(stage[:, k % 2, :], w_out[0, k * P:(k + 1) * P, :]).then_inc(w_in_sem[k % 2], 16)
                with nc.allow_non_contiguous_dma("small router weights"):
                    sp.dma_start(w_r[:, :, 0:NGRP], w_group.rearrange("l (c p) n -> p (l c) n", p=P)).then_inc(par, 16)
                    sp.dma_start(w_r[:, :, NGRP:], w_expert.rearrange("l (c p) n -> p (l c) n", p=P)).then_inc(par, 16)
                    sp.dma_start(b_r[:, 0:NGRP], b_group.to_broadcast((P, NGRP))).then_inc(par, 16)
                    sp.dma_start(b_r[:, NGRP:], b_expert.to_broadcast((P, NE))).then_inc(par, 16)
                    sp.dma_start(nf[:, :], norm_ffn.to_broadcast((P, D))).then_inc(par, 16)

                def step(t, u, first):
                    tile = t if first else sp.snap(t)
                    if not first:
                        sp.wait_ge(y_turned, t - 1)
                        sp.wait_ge(h1_ready, t - 1)
                    if not (first and t == 0):
                        sp.dma_start(y_in[u][:, :], S["y"][bass.ds(tile, 1)].rearrange("o p d -> (o p) d")).then_inc(y_sem[u], 16)
                        sp.dma_start(x_in[u][:, :], x_v[bass.ds(tile, 1)].rearrange("o p d -> (o p) d")).then_inc(x_sem[u], 16)

                step(1, 1, True)
                with sp.Fori(1, NT // 2) as i:
                    for u in range(2):
                        step(2 * i + u, u, False)

            @block.tensor
            def _(pe):
                def turn_y(t, u, n_loaded):
                    pe.wait_ge(lo_ready, t)
                    pe.wait_ge(y_sem[u], n_loaded)
                    for c in range(KC):
                        last = pe.transpose(ps_y[:, c, :], y_in[u][:, c * P:(c + 1) * P], K["ident"][:, :])
                    last.then_inc(y_turned, 1)

                def project(t, u):
                    pe.wait_ge(lo_ready, t + 1)
                    pe.wait_ge(h1_ready, t)
                    for n in range(2):
                        c = slice(n * 512, n * 512 + 512)
                        for k in range(KC):
                            last = mm3(pe, ps_o[:, c], yT_hi[u][:, k, :], yT_lo[u][:, k, :],
                                       w_hi[:, k, c], w_lo[:, k, c], k == 0, k == KC - 1)
                    last.then_inc(out_done, 1)

                def route(t, u):
                    pe.wait_ge(xtT_ready, t)
                    pe.wait_ge(xt_ready, t + 1)
                    for c in range(KC):
                        last = pe.transpose(ps_x[:, c, :], xt[u][:, c * P:(c + 1) * P], K["ident"][:, :])
                    last.then_inc(x_turned, 1)
                    pe.wait_ge(xtT_ready, t + 1)
                    pe.wait_ge(ngm_ready, t)
                    for c in range(KC):
                        last = pe.matmul(ps_l[:, 0:NLG], xtT[:, c, :], w_r[:, c, :], start=c == 0, stop=c == KC - 1)
                    last.then_inc(lg_done, 1)

                turn_y(0, 0, 16)
                pe.wait_ge(w_split, KC)
                pe.wait_ge(par, 80)
                project(0, 0)
                turn_y(1, 1, 16)

                with pe.Fori(0, NT // 2 - 1) as i:
                    for u in range(2):
                        t = 2 * i + u
                        project(t + 1, 1 - u)
                        turn_y(t + 2, u, 16 * i + 32)
                        route(t, u)
                project(NT - 1, 1)
                route(NT - 2, 0)
                route(NT - 1, 1)
                pe.wait_ge(counted, 1)
                pe.matmul(ps_c[:, 0:NE], K["ones"][:, :], cnt[:, NT, :], start=True, stop=True).then_inc(ranked, 1)
                pe.wait_ge(routed, NT)
                pe.matmul(ps_l[:, :], K["below"][:, :], both[:, :, :].rearrange("p t e -> p (t e)"), start=True, stop=False)
                pe.matmul(ps_l[:, :], K["ones"][:, :], cnt[:, 0:NT, :].rearrange("p t e -> p (t e)"),
                          start=False, stop=True).then_inc(ranked, 1)

            @block.scalar
            def _(act):
                act.preload_act_table_set(TABLES)

                def hi(t, u):
                    act.wait_ge(y_turned, t + 1)
                    for half in range(2):
                        c = slice(4 * half, 4 * half + 4)
                        last = act.activation(yT_hi[u][:, c, :], ps_y[:, c, :], ACT.Copy)
                    last.then_inc(hi_ready, 1)

                hi(0, 0)
                for k in range(KC):
                    act.wait_ge(w_in_sem[k % 2], 16 * (k // 2 + 1))
                    act.activation(w_hi[:, k, :], stage[:, k % 2, :], ACT.Copy).then_inc(w_hid, 1)

                def step(t, u, has_next):
                    if has_next:
                        hi(t + 1, 1 - u)
                    act.wait_ge(h1_ready, t + 1)
                    act.dma_start(S["h1"][bass.ds(t, 1)].rearrange("o p d -> (o p) d"), h1[u][:, :]).then_inc(h1_out[u], 16)
                    act.wait_ge(ssq_ready, t + 1)
                    act.activation(lnv[:, :], ssq[:, :], ACT.Ln, scale=1.0 / D, bias=K["eps"][:, :])
                    act.drain()
                    act.activation(rstd[:, :], lnv[:, :], ACT.Exp, scale=-0.5)
                    act.drain()
                    act.wait_ge(xt_ready, t)
                    act.activation(sq[:, :], h1[u][:, :], ACT.Copy, scale=rstd[:, 0:1]).then_inc(scaled, 1)
                    act.wait_ge(xt_ready, t + 1)
                    act.dma_start(S["xt"][bass.ds(t * P, P), :], xt[u][:, :]).then_inc(xt_out[u], 16)
                    act.wait_ge(x_turned, t + 1)
                    act.wait_ge(lg_done, t)
                    act.activation(xtT[:, 0:4, :], ps_x[:, 0:4, :], ACT.Copy)
                    act.activation(xtT[:, 4:8, :], ps_x[:, 4:8, :], ACT.Copy).then_inc(xtT_ready, 1)
                    act.wait_ge(ngm_ready, t + 1)
                    act.activation(gex[:, :], lg[:, 0:NGRP], ACT.Exp, bias=ngm[:, :], accum_out=gsum[:, :]).then_inc(gsum_ready, 1)
                    act.wait_ge(nem_ready, t + 1)
                    act.activation(e2[:, :], em[:, 1:2], ACT.Exp, bias=nem[:, :]).then_inc(e2_ready, 1)

                with act.Fori(0, NT // 2 - 1) as i:
                    for u in range(2):
                        step(2 * i + u, u, True)
                step(NT - 2, 0, True)
                step(NT - 1, 1, False)
                for u in range(2):
                    act.wait_ge(h1_out[u], 8 * NT)
                    act.wait_ge(xt_out[u], 8 * NT)

            @block.vector
            def _(dve):
                def lo(t, u):
                    dve.wait_ge(hi_ready, t + 1)
                    for half in range(2):
                        c = slice(4 * half, 4 * half + 4)
                        last = dve.tensor_tensor(yT_lo[u][:, c, :], ps_y[:, c, :], yT_hi[u][:, c, :].bitcast(F32), ALU.subtract)
                    last.then_inc(lo_ready, 1)

                lo(0, 0)
                for k in range(KC):
                    dve.wait_ge(w_hid, k + 1)
                    dve.tensor_tensor(w_lo[:, k, :], stage[:, k % 2, :], w_hi[:, k, :].bitcast(F32), ALU.subtract).then_inc(w_split, 1)
                dve.wait_ge(made, 5)
                dve.wait_ge(par, 80)

                def residual(t, u, i):
                    n_loaded = 16 * i + 16
                    dve.wait_ge(x_sem[u], n_loaded)
                    dve.wait_ge(out_done, t + 1)
                    if not (isinstance(t, int) and t < 2):
                        dve.wait_ge(h1_out[u], 16 * i)
                    dve.tensor_tensor(h1[u][:, :], ps_o[:, :], x_in[u][:, :], ALU.add).then_inc(h1_ready, 1)

                def norm(t, u):
                    dve.wait_ge(scaled, t)
                    dve.tensor_tensor_reduce(xt[u][:, :], h1[u][:, :], h1[u][:, :], 1.0, 0.0, ALU.mult, ALU.add,
                                             ssq[:, :]).then_inc(ssq_ready, 1)

                def step(t, u, has_next, i):
                    dve.drain()
                    if not (isinstance(t, int) and t < 2):
                        dve.wait_ge(xt_out[u], 16 * i)
                    norm(t, u)
                    if has_next:
                        lo(t + 1, 1 - u)
                    dve.wait_ge(scaled, t + 1)
                    dve.tensor_tensor(xt[u][:, :], sq[:, :], nf[:, :], ALU.mult).then_inc(xt_ready, 1)
                    dve.wait_ge(lg_done, t + 1)
                    dve.tensor_tensor(lg[:, :], ps_l[:, 0:NLG], b_r[:, :], ALU.add)
                    dve.drain()
                    dve.tensor_copy(g8[:, 0:NGRP], lg[:, 0:NGRP])
                    dve.drain()
                    dve.max(gm[:, :], g8[:, :])
                    dve.drain()
                    dve.tensor_scalar(ngm[:, :], gm[:, 0:1], -1.0, None, ALU.mult).then_inc(ngm_ready, 1)
                    dve.max_index(gi[:, :], gm[:, :], g8[:, :])
                    dve.drain()
                    dve.tensor_copy(gif[:, :], gi[:, 0:1])
                    dve.drain()
                    dve.tensor_scalar(og[:, :], iota[:, 0:NGRP], gif[:, 0:1], None, ALU.is_equal)
                    dve.drain()
                    dve.tensor_tensor(selg[:, :, :], lg[:, NGRP:].rearrange("p (g e) -> p g e", g=NGRP),
                                      og[:, :].rearrange("p (g o) -> p g o", o=1).to_broadcast((P, NGRP, EPG)), ALU.mult)
                    dve.drain()
                    dve.tensor_reduce(sel[:, :], selg[:, :, :].rearrange("p g e -> p e g"), AX_X, ALU.add)
                    dve.drain()
                    dve.max(em[:, :], sel[:, :])
                    dve.drain()
                    dve.tensor_scalar(nem[:, :], em[:, 0:1], -1.0, None, ALU.mult).then_inc(nem_ready, 1)
                    dve.max_index(ei[:, :], em[:, :], sel[:, :])
                    dve.drain()
                    dve.tensor_copy(eif[:, :], ei[:, 0:2])
                    dve.drain()
                    dve.scalar_tensor_tensor(out=eif[:, :], in0=gif[:, :].to_broadcast((P, 2)), scalar=float(EPG),
                                             in1=eif[:, :], op0=ALU.mult, op1=ALU.add)
                    dve.drain()
                    row = bass.ds(t, 1)
                    for c in range(2):
                        dve.tensor_scalar(oh[:, row, c, :].rearrange("p o e -> p (o e)"), iota[:, :], eif[:, c:c + 1], None, ALU.is_equal)
                    dve.drain()
                    dve.tensor_tensor(both[:, row, :], oh[:, row, 0, :], oh[:, row, 1, :], ALU.add)
                    dve.drain()
                    dve.tensor_tensor(cnt[:, bass.ds(t + 1, 1), :], cnt[:, row, :], both[:, row, :], ALU.add)
                    dve.wait_ge(e2_ready, t + 1)
                    dve.scalar_tensor_tensor(out=den[:, :], in0=e2[:, :], scalar=1.0, in1=gsum[:, :], op0=ALU.add, op1=ALU.mult)
                    dve.drain()
                    dve.reciprocal(R["wt"][:, row, 0], den[:, :])
                    dve.drain()
                    dve.tensor_tensor(R["wt"][:, row, 1], R["wt"][:, row, 0], e2[:, :], ALU.mult).then_inc(routed, 1)
                    if has_next:
                        residual(t + 1, 1 - u, i + u)

                residual(0, 0, 0)
                step(0, 0, True, 0)
                step(1, 1, True, 0)
                with dve.Fori(1, NT // 2 - 1) as i:
                    for u in range(2):
                        step(2 * i + u, u, True, i)
                step(NT - 2, 0, True, NT // 2 - 1)
                step(NT - 1, 1, False, NT // 2 - 1)
                dve.tensor_copy(posf[:, 0:1], cnt[:, NT, 0:1]).then_inc(counted, 1)
                dve.wait_ge(ranked, 1)
                dve.tensor_scalar(nbi[:, :], ps_c[:, 0:NE], float(P - 1), None, ALU.add)
                dve.drain()
                dve.tensor_scalar(nbi[:, :], nbi[:, :], 7, None, ALU.arith_shift_right)
                dve.drain()
                dve.tensor_scalar(nbf[:, :], nbi[:, :], 1.0, None, ALU.max)
                dve.drain()
                dve.tensor_copy(R["nb"][:, :], nbf[:, :])
                dve.tensor_tensor_scan(incl[:, :], K["ones"][:, 0:NE], nbf[:, :], 0.0, ALU.mult, ALU.add)
                dve.drain()
                dve.tensor_tensor(base[:, :], incl[:, :], nbf[:, :], ALU.subtract)
                dve.tensor_copy(R["incl"][:, :], incl[:, :])
                dve.drain()
                dve.tensor_copy(R["first"][:, :], base[:, :])
                dve.tensor_scalar(base[:, :], base[:, :], float(P), None, ALU.mult)
                dve.drain()
                dve.wait_ge(ranked, 2)
                dve.tensor_tensor(rank[:, :, :], ps_l[:, :].rearrange("p (t e) -> p t e", t=NT),
                                  base[:, :].rearrange("p (o e) -> p o e", o=1).to_broadcast((P, NT, NE)), ALU.add)
                dve.drain()
                for c in range(2):
                    dve.tensor_tensor(pick[:, :, c, :], oh[:, :, c, :], rank[:, :, :], ALU.mult)
                dve.drain()
                dve.tensor_reduce(posf[:, :], pick[:, :, :, :].rearrange("p t c e -> p (t c) e"), AX_X, ALU.add)
                dve.drain()
                dve.tensor_copy(R["pos"][:, :], posf[:, :]).then_inc(pos_ready, 1)


def experts(nc, sem, K, w_gu, w_down, S, R):
    NPC = KC + DE // P
    KD = DE // P
    with ExitStack() as ctx:
        def sb(name, shape, dt=F32):
            return ctx.enter_context(nc.sbuf_tensor(name, shape, dt))

        def pb(name, shape):
            return ctx.enter_context(nc.psum_tensor(name, shape, F32))

        w_hi = sb("we_hi", [P, NPC, D], F32R)
        w_lo = sb("we_lo", [P, NPC, D], F32R)
        stage = sb("we_stage", [P, NPC, D])
        idx = sb("idx", [P, 1], I32)
        none = sb("idx_zero", [P, 1], I32)
        tok = sb("idx_tok", [P, 1], I32)
        xg = sb("xg", [P, D])
        xT_hi = sb("xe_hi", [P, KC, P], F32R)
        xT_lo = sb("xe_lo", [P, KC, P], F32R)
        sg = sb("sg", [P, DE])
        hh = sb("hh", [P, DE])
        hT_hi = sb("hT_hi", [P, KD, P], F32R)
        hT_lo = sb("hT_lo", [P, KD, P], F32R)
        ysb = sb("ysb", [P, D])
        ps_g = pb("pe_g", [P, DE])
        ps_u = pb("pe_u", [P, DE])
        ps_x = pb("pe_x", [P, KC, P])
        ps_h = pb("pe_h", [P, KD, P])
        ps_y = pb("pe_y", [P, D])

        w_in_sem = [sem(f"ex_w{i}") for i in range(NPC)]
        w_hid, w_split = sem("ex_w_hi"), sem("ex_w_split")
        idx_sem, xg_sem = sem("ex_idx"), sem("ex_xg")
        x_turned, x_hi, x_lo = sem("ex_x_turned"), sem("ex_x_hi"), sem("ex_x_lo")
        gate_done, up_done, silu_ready, h_ready = sem("ex_gate"), sem("ex_up"), sem("ex_silu"), sem("ex_h")
        h_turned, h_hi, h_lo = sem("ex_h_turned"), sem("ex_h_hi"), sem("ex_h_lo")
        down_done, y_half, y_ready, y_out = sem("ex_down"), sem("ex_y_half"), sem("ex_y"), sem("ex_y_out")

        def counts(eng, e):
            col = e if isinstance(e, int) else bass.ds(e, 1)
            col = slice(e, e + 1) if isinstance(e, int) else col
            return (eng.value_load(R["first"][0:1, col], min_val=0, max_val=NBLK - 1),
                    eng.value_load(R["nb"][0:1, col], min_val=1, max_val=T // P))

        with nc.Block() as block:
            @block.sync
            def _(sp):
                def load(e, waits):
                    ex = e if isinstance(e, int) else sp.snap(e)
                    row = bass.ds(ex, 1)
                    for i in range(NPC):
                        if waits:
                            sp.wait_ge(w_split, NPC * e + (i + 1 - NPC))
                        src = (w_gu[0, row, i * P:(i + 1) * P, :] if i < KC
                               else w_down[0, row, (i - KC) * P:(i - KC + 1) * P, :])
                        sp.dma_start(stage[:, i, :], src.rearrange("o p n -> (o p) n")).then_inc(w_in_sem[i], 16)

                load(0, False)
                with sp.Fori(1, NE) as e:
                    load(e, True)

            @block.gpsimd
            def _(pool):
                pool.memset(none[:, :], 0)
                pool.drain()
                total = pool.value_load(R["incl"][0:1, NE - 1:NE], min_val=NE, max_val=NBLK)
                with pool.Fori(0, total + 1) as b:
                    pool.dma_start(idx[:, :], S["slots"][bass.ds(b * P, P), :]).then_inc(idx_sem, 16)
                    pool.wait_ge(idx_sem, 16 * b + 16)
                    pool.wait_ge(x_turned, b)
                    pool.tensor_tensor(tok[:, :], idx[:, :], none[:, :], ALU.add)
                    pool.drain()
                    pool.indirect_dma_start(xg[:, :], None, S["xt"], bass.IndirectOffsetOnAxis(ap=tok[:, 0:1], axis=0)
                                            ).then_inc(xg_sem, 16)
                    pool.wait_ge(xg_sem, 16 * b + 16)
                pool.wait_ge(y_out, total * 16)

            @block.tensor
            def _(pe):
                def turn_x(b):
                    pe.wait_ge(x_lo, b)
                    pe.wait_ge(xg_sem, 16 * b + 16)
                    for c in range(KC):
                        last = pe.transpose(ps_x[:, c, :], xg[:, c * P:(c + 1) * P], K["ident"][:, :])
                    last.then_inc(x_turned, 1)

                turn_x(0)
                with pe.Fori(0, NE) as e:
                    first, n = counts(pe, e)
                    with pe.Fori(0, n) as j:
                        b = pe.snap(first + j)
                        pe.wait_ge(x_lo, b + 1)
                        pe.wait_ge(silu_ready, b)
                        for k in range(KC):
                            pe.wait_ge(w_split, NPC * e + k + 1)
                            last = mm3(pe, ps_g[:, :], xT_hi[:, k, :], xT_lo[:, k, :], w_hi[:, k, 0:DE],
                                       w_lo[:, k, 0:DE], k == 0, k == KC - 1)
                        last.then_inc(gate_done, 1)
                        pe.wait_ge(h_ready, b)
                        for k in range(KC):
                            last = mm3(pe, ps_u[:, :], xT_hi[:, k, :], xT_lo[:, k, :], w_hi[:, k, DE:D],
                                       w_lo[:, k, DE:D], k == 0, k == KC - 1)
                        last.then_inc(up_done, 1)
                        turn_x(b + 1)
                        pe.wait_ge(h_ready, b + 1)
                        pe.wait_ge(h_lo, b)
                        for c in range(KD):
                            last = pe.transpose(ps_h[:, c, :], hh[:, c * P:(c + 1) * P], K["ident"][:, :])
                        last.then_inc(h_turned, 1)
                        pe.wait_ge(w_split, NPC * e + NPC)
                        pe.wait_ge(h_lo, b + 1)
                        pe.wait_ge(y_ready, b)
                        pe.wait_ge(y_half, b)
                        for h in range(2):
                            c = slice(h * 512, h * 512 + 512)
                            for k in range(KD):
                                last = mm3(pe, ps_y[:, c], hT_hi[:, k, :], hT_lo[:, k, :], w_hi[:, KC + k, c],
                                           w_lo[:, KC + k, c], k == 0, k == KD - 1)
                        last.then_inc(down_done, 1)

            @block.scalar
            def _(act):
                act.preload_act_table_set("silu_and_others")

                def x_high(b):
                    act.wait_ge(x_turned, b + 1)
                    act.activation(xT_hi[:, 0:4, :], ps_x[:, 0:4, :], ACT.Copy)
                    act.activation(xT_hi[:, 4:8, :], ps_x[:, 4:8, :], ACT.Copy).then_inc(x_hi, 1)

                x_high(0)
                with act.Fori(0, NE) as e:
                    first, n = counts(act, e)
                    for i in range(NPC):
                        act.wait_ge(w_in_sem[i], 16 * e + 16)
                        if i == 0:
                            act.wait_ge(up_done, first)
                        if i == KC:
                            act.wait_ge(down_done, first)
                        act.activation(w_hi[:, i, :], stage[:, i, :], ACT.Copy).then_inc(w_hid, 1)
                    with act.Fori(0, n) as j:
                        b = act.snap(first + j)
                        act.wait_ge(gate_done, b + 1)
                        act.wait_ge(h_ready, b)
                        act.activation(sg[:, :], ps_g[:, :], ACT.Silu).then_inc(silu_ready, 1)
                        act.wait_ge(up_done, b + 1)
                        x_high(b + 1)
                        act.wait_ge(h_turned, b + 1)
                        act.wait_ge(down_done, b)
                        act.activation(hT_hi[:, :, :], ps_h[:, :, :], ACT.Copy).then_inc(h_hi, 1)
                        act.wait_ge(down_done, b + 1)
                        act.wait_ge(y_out, 16 * b)
                        act.activation(ysb[:, 0:512], ps_y[:, 0:512], ACT.Copy).then_inc(y_half, 1)
                        act.wait_ge(y_half, b + 1)
                        act.wait_ge(y_ready, b + 1)
                        act.dma_start(S["ys"][bass.ds(b * P, P), :], ysb[:, :]).then_inc(y_out, 16)

            @block.vector
            def _(dve):
                def x_low(b):
                    dve.wait_ge(x_hi, b + 1)
                    dve.tensor_tensor(xT_lo[:, 0:4, :], ps_x[:, 0:4, :], xT_hi[:, 0:4, :].bitcast(F32), ALU.subtract)
                    dve.tensor_tensor(xT_lo[:, 4:8, :], ps_x[:, 4:8, :], xT_hi[:, 4:8, :].bitcast(F32), ALU.subtract).then_inc(x_lo, 1)

                x_low(0)
                with dve.Fori(0, NE) as e:
                    first, n = counts(dve, e)
                    for i in range(NPC):
                        dve.wait_ge(w_hid, NPC * e + i + 1)
                        dve.tensor_tensor(w_lo[:, i, :], stage[:, i, :], w_hi[:, i, :].bitcast(F32), ALU.subtract).then_inc(w_split, 1)
                    with dve.Fori(0, n) as j:
                        b = dve.snap(first + j)
                        dve.wait_ge(up_done, b + 1)
                        dve.wait_ge(silu_ready, b + 1)
                        dve.wait_ge(h_turned, b)
                        dve.tensor_tensor(hh[:, :], sg[:, :], ps_u[:, :], ALU.mult).then_inc(h_ready, 1)
                        x_low(b + 1)
                        dve.wait_ge(h_hi, b + 1)
                        dve.tensor_tensor(hT_lo[:, :, :], ps_h[:, :, :], hT_hi[:, :, :].bitcast(F32), ALU.subtract).then_inc(h_lo, 1)
                        dve.wait_ge(down_done, b + 1)
                        dve.wait_ge(y_out, 16 * b)
                        dve.tensor_copy(ysb[:, 512:1024], ps_y[:, 512:1024]).then_inc(y_ready, 1)


def combine(nc, sem, K, norm_final, S, R, out):
    out_v = out.rearrange("b (t p) d -> (b t) p d", p=P)
    with ExitStack() as ctx:
        def sb(name, shape, dt=F32):
            return ctx.enter_context(nc.sbuf_tensor(name, shape, dt))

        NB = 2
        h1 = [sb(f"f_h1{i}", [P, D]) for i in range(NB)]
        y0 = [sb(f"f_y0{i}", [P, D]) for i in range(NB)]
        y1 = [sb(f"f_y1{i}", [P, D]) for i in range(NB)]
        o = [sb(f"f_o{i}", [P, D]) for i in range(NB)]
        nf = sb("f_norm", [P, D])
        ssq = sb("f_ssq", [P, 1])
        lnv = sb("f_ln", [P, 1])
        rstd = sb("f_rstd", [P, 1])
        par = sem("fn_params")
        h_sem, y0_sem, y1_sem, o_out = [[sem(f"fn_{n}{i}") for i in range(NB)] for n in ("h", "y0_", "y1_", "out")]
        summed, ssq_ready, rstd_ready, o_ready = sem("fn_summed"), sem("fn_ssq"), sem("fn_rstd"), sem("fn_o")

        with nc.Block() as block:
            @block.gpsimd
            def _(pool):
                for t in range(NT):
                    u = t % NB
                    if t >= NB:
                        pool.wait_ge(summed, t - NB + 1)
                    for c, (y, s) in enumerate(((y0, y0_sem), (y1, y1_sem))):
                        pool.indirect_dma_start(y[u][:, :], None, S["ys"], bass.IndirectOffsetOnAxis(
                            ap=R["pos"][:, 2 * t + c:2 * t + c + 1], axis=0)).then_inc(s[u], 16)

            @block.sync
            def _(sp):
                sp.dma_start(nf[:, :], norm_final.rearrange("(o d) -> o d", o=1).to_broadcast((P, D))).then_inc(par, 16)

                def load(t, u):
                    sp.dma_start(h1[u][:, :], S["h1"][bass.ds(t, 1)].rearrange("o p d -> (o p) d")).then_inc(h_sem[u], 16)

                def store(t, u):
                    sp.wait_ge(o_ready, t + 1)
                    sp.dma_start(out_v[bass.ds(t, 1)].rearrange("o p d -> (o p) d"), o[u][:, :]).then_inc(o_out[u], 16)

                load(0, 0)
                load(1, 1)
                with sp.Fori(0, NT // 2 - 1) as i:
                    for u in range(2):
                        t = sp.snap(2 * i + u)
                        store(t, u)
                        load(t + 2, u)
                store(NT - 2, 0)
                store(NT - 1, 1)
                for u in range(2):
                    sp.wait_ge(o_out[u], 8 * NT)

            @block.scalar
            def _(act):
                act.preload_act_table_set(TABLES)
                with act.Fori(0, NT) as t:
                    act.wait_ge(ssq_ready, t + 1)
                    act.activation(lnv[:, :], ssq[:, :], ACT.Ln, scale=1.0 / D, bias=K["eps"][:, :])
                    act.drain()
                    act.wait_ge(o_ready, t)
                    act.activation(rstd[:, :], lnv[:, :], ACT.Exp, scale=-0.5).then_inc(rstd_ready, 1)

            @block.vector
            def _(dve):
                dve.wait_ge(par, 16)
                with dve.Fori(0, NT // 2) as i:
                    for u in range(2):
                        t = 2 * i + u
                        wt = R["wt"][:, bass.ds(t, 1), :].rearrange("p o c -> p (o c)")
                        for s in (h_sem, y0_sem, y1_sem):
                            dve.wait_ge(s[u], 16 * i + 16)
                        dve.scalar_tensor_tensor(out=h1[u][:, :], in0=y0[u][:, :], scalar=wt[:, 0:1], in1=h1[u][:, :],
                                                 op0=ALU.mult, op1=ALU.add)
                        dve.drain()
                        dve.scalar_tensor_tensor(out=h1[u][:, :], in0=y1[u][:, :], scalar=wt[:, 1:2], in1=h1[u][:, :],
                                                 op0=ALU.mult, op1=ALU.add).then_inc(summed, 1)
                        dve.drain()
                        dve.wait_ge(rstd_ready, t)
                        dve.wait_ge(o_out[u], 16 * i)
                        dve.tensor_tensor_reduce(o[u][:, :], h1[u][:, :], h1[u][:, :], 1.0, 0.0, ALU.mult, ALU.add,
                                                 ssq[:, :]).then_inc(ssq_ready, 1)
                        dve.drain()
                        dve.wait_ge(rstd_ready, t + 1)
                        dve.scalar_tensor_tensor(out=o[u][:, :], in0=h1[u][:, :], scalar=rstd[:, 0:1], in1=nf[:, :],
                                                 op0=ALU.mult, op1=ALU.mult).then_inc(o_ready, 1)


def program(nc, x, norm_mix, w_in, conv_w, conv_b, b_mlstm_gate, w_gla_gate, b_gla_gate,
            head_norm, w_out, norm_ffn, w_group, b_group, w_expert, b_expert, w_gu,
            w_down, norm_final, out):
    def scratch(name, shape, dt=F32):
        return nc.dram_tensor(name, shape, dt).ap()

    S = {
        "xT_hi": scratch("s_xT_hi", (KC, P, T)),
        "xT_lo": scratch("s_xT_lo", (KC, P, T)),
        "gate": scratch("s_gate", (NT, P, D)),
        "val": scratch("s_val", (NT, P, D)),
        "qk": scratch("s_qk", (8, P, T)),
        "kR": scratch("s_kR", (2, 5, P, T)),
        "qG": scratch("s_qG", (2, 2, P, T)),
        "gl": scratch("s_gl", (2, P, NT)),
        "rows": scratch("s_rows", (4, H, T)),
        "nM": scratch("s_nM", (H, T)),
        "y": scratch("s_y", (NT, P, D)),
        "h1": scratch("s_h1", (NT, P, D)),
        "xt": scratch("s_xt", (T, D)),
        "slots": scratch("s_slots", ((NBLK + 1) * P, 1), I32),
        "ys": scratch("s_ys", (YB * P, D)),
        "dec": scratch("s_dec", (H, NT)),
    }
    def phase(build, *args):
        own = []

        def sem(name):
            own.append(nc.alloc_semaphore(name=name))
            return own[-1]

        build(nc, sem, *args)
        nc.clear_and_free_semaphores(own)
        nc.all_engine_barrier()

    with ExitStack() as ctx:
        K = {}
        phase(constants, ctx, K)
        phase(project_tokens, K, x, norm_mix, w_in, head_norm, S)
        phase(project_channels, K, norm_mix, w_in, conv_w, conv_b, b_mlstm_gate, w_gla_gate, b_gla_gate, S)
        phase(recur, K, S)
        R = {
            "pos": ctx.enter_context(nc.sbuf_tensor("pos", [P, 2 * NT], I32)),
            "wt": ctx.enter_context(nc.sbuf_tensor("wt", [P, NT, 2], F32)),
            "nb": ctx.enter_context(nc.sbuf_tensor("nb", [P, NE], I32)),
            "first": ctx.enter_context(nc.sbuf_tensor("first", [P, NE], I32)),
            "incl": ctx.enter_context(nc.sbuf_tensor("incl_i", [P, NE], I32)),
        }
        phase(project_out_and_route, K, x, w_out, norm_ffn, w_group, b_group, w_expert, b_expert, S, R)
        phase(experts, K, w_gu, w_down, S, R)
        phase(combine, K, norm_final, S, R, out)


_INS = ["x", "norm_mix", "w_in", "conv_w", "conv_b", "b_mlstm_gate", "w_gla_gate", "b_gla_gate", "head_norm",
        "w_out", "norm_ffn", "w_group", "b_group", "w_expert", "b_expert", "w_gu", "w_down", "norm_final"]


def kernel(**inputs):
    import numpy as np
    import concourse.bacc as bacc
    from concourse.bass_utils import run_bass_kernel_spmd

    nc = bacc.Bacc("TRN2", target_bir_lowering=False, num_devices=1)
    arrays, args = {}, []
    for name in _INS:
        a = np.ascontiguousarray(inputs[name])
        arrays[f"in_{name}_dram"] = a
        args.append(nc.dram_tensor(f"in_{name}_dram", a.shape, mybir.dt.from_np(a.dtype), kind="ExternalInput").ap())
    out = nc.dram_tensor("out_0_dram", (1, T, D), F32, kind="ExternalOutput").ap()
    program(nc, *args, out)
    r = run_bass_kernel_spmd(nc, [arrays], core_ids=[0])
    return r.results[0]["out_0_dram"]
```

```python
import math
from contextlib import ExitStack

import concourse.bass as bass
from concourse import mybir

F32 = mybir.dt.float32
F32R = mybir.dt.float32r
I32 = mybir.dt.int32
ALU = mybir.AluOpType
ACT = mybir.ActivationFunctionType
AX_X = mybir.AxisListType.X

P = 128
D = 1024
KC = D // P
T = 2048
NT = T // P
GRP = 512
NG = T // GRP
CPG = GRP // P
H = 4
DV = P
DK = 64
RANK = 16
CW = 4
W = H * DV
D_PROJ = 4 * W + 2 * H + 2 * H * DK + 2 * W + RANK
OFF_QK, OFF_VM, OFF_OM = 0, 2 * W, 3 * W
OFF_I = 4 * W
OFF_F = OFF_I + H
OFF_QKG = OFF_F + H
OFF_VG = OFF_QKG + 2 * H * DK
OFF_ZG = OFF_VG + W
OFF_R = OFF_ZG + W
NE, NGRP, EPG = 32, 4, 8
DE = 512
NBLK = 2 * T // P + NE
YB = NBLK + NT
EPS = 1e-6
SUB = 32
NSUB = P // SUB
VT_CAP = 1e30
NEG = -1e30
TABLES = "natural_log_exp_and_others"
LN_CAP = 2.0 ** 60
C_I, C_F, C_R, C_QKG, C_QK = 0, 32, 64, 80, 80 + 512
C_ALL = C_QK + 1024


def mm3(pe, out, ah, al, bh, bl, first, last):
    pe.matmul(out, ah, bh, start=first, stop=False)
    pe.matmul(out, ah, bl, start=False, stop=False)
    return pe.matmul(out, al, bh, start=False, stop=last)


def neg_abs(dve, out, x):
    return dve.scalar_tensor_tensor(out=out, in0=x, scalar=-1.0, in1=x, op0=ALU.mult, op1=ALU.min)


def constants(nc, sem, ctx, K):
    def sb(name, shape, dt=F32):
        return ctx.enter_context(nc.sbuf_tensor(name, shape, dt))

    K["ident"] = sb("ident", [P, P])
    K["ones"] = sb("ones", [P, P])
    K["below"] = sb("below", [P, P])
    K["keep"] = sb("keep", [P, P])
    K["drop"] = sb("drop", [P, P])
    K["eps"] = sb("eps", [P, 1])
    K["one"] = sb("one", [P, 1])
    s = sem("const_set")
    s2 = sem("const_made")
    with nc.Block() as block:
        @block.gpsimd
        def _(pool):
            pool.memset(K["ident"][:, :], 0.0).then_inc(s, 1)
            pool.memset(K["ones"][:, :], 1.0).then_inc(s, 1)
            pool.memset(K["below"][:, :], 1.0).then_inc(s, 1)
            pool.memset(K["keep"][:, :], 1.0).then_inc(s, 1)
            pool.memset(K["drop"][:, :], 0.0).then_inc(s, 1)
            pool.memset(K["eps"][:, :], EPS).then_inc(s, 1)
            pool.memset(K["one"][:, :], 1.0).then_inc(s, 1)
            pool.wait_ge(s, 7)
            row_minus_col = dict(base=0, pattern=[[-1, P]], channel_multiplier=1)
            col_minus_row = dict(base=0, pattern=[[1, P]], channel_multiplier=-1)
            pool.affine_select(out=K["ident"][:, :], in_=K["ident"][:, :], compare_op=ALU.not_equal,
                               fill=1.0, **row_minus_col).then_inc(s2, 1)
            pool.affine_select(out=K["below"][:, :], in_=K["below"][:, :], compare_op=ALU.is_gt,
                               fill=0.0, **col_minus_row).then_inc(s2, 1)
            pool.affine_select(out=K["keep"][:, :], in_=K["keep"][:, :], compare_op=ALU.is_ge,
                               fill=0.0, **col_minus_row).then_inc(s2, 1)
            pool.affine_select(out=K["drop"][:, :], in_=K["drop"][:, :], compare_op=ALU.is_ge,
                               fill=NEG, **col_minus_row).then_inc(s2, 1)
            pool.wait_ge(s2, 4)


def project_tokens(nc, sem, K, x, norm_mix, w_in, head_norm, S):
    ORDER = (OFF_OM, OFF_ZG, OFF_VM, OFF_VG)
    x_v = x.rearrange("b (t p) d -> (b t) p d", p=P)
    with ExitStack() as ctx:
        def sb(name, shape, dt=F32):
            return ctx.enter_context(nc.sbuf_tensor(name, shape, dt))

        def pb(name, shape):
            return ctx.enter_context(nc.psum_tensor(name, shape, F32))

        w_hi = sb("wt_hi", [P, 4, KC, W], F32R)
        w_lo = sb("wt_lo", [P, 4, KC, W], F32R)
        NSTAGE = 8
        stage = sb("wt_stage", [P, NSTAGE, W])
        x_in = sb("x_in", [P, 2, D])
        xn = sb("xn", [P, D])
        xT_hi = [sb(f"xT_hi{i}", [P, KC, P], F32R) for i in range(2)]
        xT_lo = [sb(f"xT_lo{i}", [P, KC, P], F32R) for i in range(2)]
        sq = sb("sq", [P, D])
        ssq = sb("ssq", [P, 1])
        lnv = sb("lnv", [P, 1])
        rstd = sb("rstd", [P, 1])
        g_mix = sb("g_mix", [P, KC])
        hn = sb("hn", [P, D])
        e_o = sb("e_o", [P, W])
        e_z = sb("e_z", [P, W])
        gate = sb("gate", [P, D])
        val = sb("val", [P, D])
        xg = sb("xT_g", [P, KC, P])
        zero = sb("zero_y", [P, D])
        ps_t = pb("ps_t", [P, KC, P])
        ps_u = [pb(f"ps_u{i}", [P, W]) for i in range(4)]

        par_in, x_sem = sem("ta_params"), [sem("ta_x0"), sem("ta_x1")]
        w_in_sem = [sem(f"ta_w{i}") for i in range(NSTAGE)]
        w_hid, w_split = sem("ta_w_hi"), sem("ta_w_split")
        ssq_ready, xn_ready = sem("ta_ssq"), sem("ta_xn")
        xposed, hi_ready, lo_ready = sem("ta_xposed"), sem("ta_hi"), sem("ta_lo")
        unit = sem("ta_unit")
        e_ready, gate_half, gate_ready, val_ready = (sem("ta_e"), sem("ta_gate_o"), sem("ta_gate"),
                                                     sem("ta_val"))
        e_capped, sig_ready = sem("ta_e_capped"), sem("ta_sig")
        xg_ready, zero_made, zeroed = sem("ta_xg"), sem("ta_zero"), sem("ta_zeroed")
        xT_out, gate_out, val_out = sem("ta_xT_out"), sem("ta_gate_out"), sem("ta_val_out")

        def over_tiles(eng, step):
            with eng.Fori(0, NT // 2 - 1) as i:
                for u in range(2):
                    step(2 * i + u, u, True, i)
            step(NT - 2, 0, True, NT // 2 - 1)
            step(NT - 1, 1, False, NT // 2 - 1)

        with nc.Block() as block:
            @block.gpsimd
            def _(pool):
                pool.memset(zero[:, :], 0.0).then_inc(zero_made, 1)
                pool.wait_ge(zero_made, 1)
                with pool.Fori(0, NT) as t:
                    row = pool.snap((t * 2 + NE) * P)
                    pool.wait_ge(unit, 3 * t + 12)
                    pool.dma_start(S["ys"][bass.ds(row, 2 * P), :].rearrange("(n p) d -> p n d", p=P),
                                   zero[:, :].rearrange("p (o d) -> p o d", o=1).to_broadcast((P, 2, D))
                                   ).then_inc(zeroed, 16)
                pool.wait_ge(zeroed, 16 * NT)

            @block.sync
            def _(sp):
                sp.dma_start(x_in[:, 0, :], x_v[0]).then_inc(x_sem[0], 16)
                with nc.allow_non_contiguous_dma("norm weights by partition"):
                    sp.dma_start(g_mix[:, :], norm_mix.rearrange("l (c p) -> p (l c)", p=P)).then_inc(par_in, 16)
                sp.dma_start(hn[:, :], head_norm.to_broadcast((P, D))).then_inc(par_in, 16)
                sp.dma_start(x_in[:, 1, :], x_v[1]).then_inc(x_sem[1], 16)
                for n in range(4):
                    for k in range(KC):
                        i = n * KC + k
                        if i >= NSTAGE:
                            sp.wait_ge(w_split, i - NSTAGE + 1)
                        sp.dma_start(stage[:, i % NSTAGE, :],
                                     w_in[0, k * P:(k + 1) * P, ORDER[n]:ORDER[n] + W]
                                     ).then_inc(w_in_sem[i % NSTAGE], 16)
                sp.wait_ge(xg_ready, 1)
                sp.dma_start(S["xT"][:, :, 0:P].rearrange("c p t -> p c t"), xg[:, :, :]).then_inc(xT_out, 16)

                def step(t, u, has_next, i):
                    if has_next:
                        if isinstance(t, int) is False:
                            sp.dma_start(x_in[:, u, :], x_v[bass.ds(t + 2, 1)].rearrange("o p d -> (o p) d")
                                         ).then_inc(x_sem[u], 16)
                        sp.wait_ge(xg_ready, t + 2)
                        col = bass.ds(t * P + P, P)
                        sp.dma_start(S["xT"][:, :, col].rearrange("c p t -> p c t"), xg[:, :, :]).then_inc(xT_out, 16)
                    row = bass.ds(t, 1)
                    sp.wait_ge(gate_ready, t + 1)
                    sp.dma_start(S["gate"][row].rearrange("o p d -> (o p) d"), gate[:, :]).then_inc(gate_out, 16)
                    sp.wait_ge(val_ready, 2 * t + 2)
                    sp.dma_start(S["val"][row].rearrange("o p d -> (o p) d"), val[:, :]).then_inc(val_out, 16)

                over_tiles(sp, step)
                sp.wait_ge(xT_out, 16 * NT)
                sp.wait_ge(gate_out, 16 * NT)
                sp.wait_ge(val_out, 16 * NT)

            @block.scalar
            def _(act):
                act.preload_act_table_set(TABLES)

                def norm(t, u, n_loaded):
                    act.wait_ge(ssq_ready, t + 1)
                    act.activation(lnv[:, :], ssq[:, :], ACT.Ln, bias=K["eps"][:, :], scale=1.0 / D)
                    act.drain()
                    act.activation(rstd[:, :], lnv[:, :], ACT.Exp, scale=-0.5)
                    act.drain()
                    act.wait_ge(x_sem[u], n_loaded)
                    act.wait_ge(xposed, t)
                    act.activation(xn[:, :], x_in[:, u, :], ACT.Copy, scale=rstd[:, 0:1]).then_inc(xn_ready, 1)

                def hi(t, u):
                    act.wait_ge(xposed, t + 1)
                    for half in range(2):
                        c = slice(4 * half, 4 * half + 4)
                        last = act.activation(xT_hi[u][:, c, :], ps_t[:, c, :], ACT.Copy)
                    last.then_inc(hi_ready, 1)

                norm(0, 0, 16)
                hi(0, 0)
                act.wait_ge(par_in, 32)
                for i in range(4 * KC):
                    n, k = divmod(i, KC)
                    act.wait_ge(w_in_sem[i % NSTAGE], 16 * (i // NSTAGE + 1))
                    act.activation(w_hi[:, n, k, :], stage[:, i % NSTAGE, :], ACT.Copy,
                                   scale=g_mix[:, k:k + 1]).then_inc(w_hid, 1)

                def step(t, u, has_next, i):
                    if has_next:
                        norm(t + 1, 1 - u, 16 * i + (16 if u == 0 else 32))
                    act.wait_ge(unit, 4 * t + 1)
                    act.wait_ge(gate_half, t)
                    act.activation(e_o[:, :], ps_u[0][:, :], ACT.Exp, scale=-1.0).then_inc(e_ready, 1)
                    act.wait_ge(unit, 4 * t + 2)
                    act.wait_ge(gate_ready, t)
                    act.activation(e_z[:, :], ps_u[1][:, :], ACT.Exp, scale=-1.0).then_inc(e_ready, 1)
                    for n, e in enumerate((e_o, e_z)):
                        act.wait_ge(e_capped, 2 * t + n + 1)
                        act.activation(e[:, :], e[:, :], ACT.Ln, bias=K["one"][:, :])
                        act.drain()
                        act.activation(e[:, :], e[:, :], ACT.Exp, scale=-1.0).then_inc(sig_ready, 1)
                    if has_next:
                        hi(t + 1, 1 - u)
                    act.wait_ge(val_out, 16 * t)
                    act.wait_ge(unit, 4 * t + 3)
                    act.activation(val[:, 0:W], ps_u[2][:, :], ACT.Copy).then_inc(val_ready, 1)
                    act.wait_ge(unit, 4 * t + 4)
                    act.activation(val[:, W:D], ps_u[3][:, :], ACT.Copy).then_inc(val_ready, 1)

                over_tiles(act, step)

            @block.vector
            def _(dve):
                def squares(t, u, n_loaded):
                    dve.wait_ge(x_sem[u], n_loaded)
                    dve.wait_ge(xn_ready, t)
                    dve.tensor_tensor_reduce(sq[:, :], x_in[:, u, :], x_in[:, u, :], 1.0, 0.0, ALU.mult,
                                             ALU.add, ssq[:, :]).then_inc(ssq_ready, 1)

                def lo(t, u):
                    dve.wait_ge(hi_ready, t + 1)
                    for half in range(2):
                        c = slice(4 * half, 4 * half + 4)
                        last = dve.tensor_tensor(xT_lo[u][:, c, :], ps_t[:, c, :], xT_hi[u][:, c, :].bitcast(F32),
                                                 ALU.subtract)
                    last.then_inc(lo_ready, 1)

                def weighted(t):
                    dve.wait_ge(hi_ready, t + 1)
                    if not (isinstance(t, int) and t == 0):
                        dve.wait_ge(xT_out, 16 * t)
                    for half in range(2):
                        c = slice(4 * half, 4 * half + 4)
                        last = dve.tensor_tensor(xg[:, c, :], ps_t[:, c, :], g_mix[:, c].rearrange(
                            "p (k o) -> p k o", o=1).to_broadcast((P, 4, P)), ALU.mult)
                    last.then_inc(xg_ready, 1)

                squares(0, 0, 16)
                dve.wait_ge(par_in, 32)
                weighted(0)
                lo(0, 0)
                for i in range(4 * KC):
                    n, k = divmod(i, KC)
                    dve.wait_ge(w_hid, i + 1)
                    dve.scalar_tensor_tensor(out=w_lo[:, n, k, :], in0=stage[:, i % NSTAGE, :],
                                             scalar=g_mix[:, k:k + 1], in1=w_hi[:, n, k, :].bitcast(F32),
                                             op0=ALU.mult, op1=ALU.subtract).then_inc(w_split, 1)

                def step(t, u, has_next, i):
                    if has_next:
                        squares(t + 1, 1 - u, 16 * i + (16 if u == 0 else 32))
                    for n, e in enumerate((e_o, e_z)):
                        dve.wait_ge(e_ready, 2 * t + n + 1)
                        dve.tensor_scalar(e[:, :], e[:, :], LN_CAP, None, ALU.min).then_inc(e_capped, 1)
                    dve.wait_ge(sig_ready, 2 * t + 1)
                    dve.wait_ge(gate_out, 16 * t)
                    dve.tensor_tensor(gate[:, 0:W], e_o[:, :], hn[:, 0:W], ALU.mult).then_inc(gate_half, 1)
                    dve.wait_ge(sig_ready, 2 * t + 2)
                    dve.tensor_tensor(e_z[:, :], e_z[:, :], ps_u[1][:, :], ALU.mult)
                    dve.drain()
                    dve.tensor_tensor(gate[:, W:D], e_z[:, :], hn[:, W:D], ALU.mult).then_inc(gate_ready, 1)
                    if has_next:
                        weighted(t + 1)
                        lo(t + 1, 1 - u)

                over_tiles(dve, step)

            @block.tensor
            def _(pe):
                def xpose(t, u):
                    pe.wait_ge(xn_ready, t + 1)
                    pe.wait_ge(lo_ready, t)
                    for c in range(KC):
                        last = pe.transpose(ps_t[:, c, :], xn[:, c * P:(c + 1) * P], K["ident"][:, :])
                    last.then_inc(xposed, 1)

                def product(t, u, n):
                    pe.wait_ge(w_split, KC * (n + 1))
                    if n == 0:
                        pe.wait_ge(e_ready, 2 * t)
                        pe.wait_ge(lo_ready, t + 1)
                    elif n == 1:
                        pe.wait_ge(gate_ready, t)
                    else:
                        pe.wait_ge(val_ready, 2 * t)
                    for k in range(KC):
                        last = mm3(pe, ps_u[n][:, :], xT_hi[u][:, k, :], xT_lo[u][:, k, :],
                                   w_hi[:, n, k, :], w_lo[:, n, k, :], k == 0, k == KC - 1)
                    last.then_inc(unit, 1)

                xpose(0, 0)

                def step(t, u, has_next, i):
                    product(t, u, 0)
                    product(t, u, 1)
                    if has_next:
                        xpose(t + 1, 1 - u)
                    product(t, u, 2)
                    product(t, u, 3)

                over_tiles(pe, step)


def project_channels(nc, sem, K, norm_mix, w_in, conv_w, conv_b, b_gate, w_gla, b_gla, S):
    NU = 13
    NV = 7
    NRES = 2 * NV + 8
    NCONV = 8
    with ExitStack() as ctx:
        def sb(name, shape, dt=F32):
            return ctx.enter_context(nc.sbuf_tensor(name, shape, dt))

        def pb(name, shape):
            return ctx.enter_context(nc.psum_tensor(name, shape, F32))

        w_hi = sb("wc_hi", [P, KC, C_ALL], F32R)
        w_lo = sb("wc_lo", [P, KC, C_ALL], F32R)
        stage = sb("xc_stage", [P, KC, GRP])
        stage_s = sb("wc_small", [P, KC, C_QKG])
        xT_hi = sb("xc_hi", [P, KC, GRP], F32R)
        xT_lo = sb("xc_lo", [P, KC, GRP], F32R)
        cw = sb("cw", [P, CW, NCONV])
        cb = sb("cb", [P, NCONV])
        bi = sb("bi", [H, 1])
        bf = sb("bf", [H, 1])
        wg = sb("wg", [RANK, 2 * P])
        bg = sb("bg", [P, 2])
        ln_scale = sb("ln_scale", [H, 1])
        halo = sb("halo", [P, NCONV, CW - 1])
        cin = [sb(f"cin{i}", [P, GRP + CW - 1]) for i in range(2)]
        acc = [sb(f"acc{i}", [P, GRP]) for i in range(3)]
        th = [sb(f"th{i}", [P, GRP]) for i in range(2)]
        vt = th
        res = [sb(f"res{i}", [P, GRP]) for i in range(2)]
        keep_run = sb("keep_run", [P, GRP])
        max_run = sb("max_run", [H, GRP])
        IG, FG, BR, UR, CM, E1, E2, NM = [sb(f"row{i}", [H, GRP]) for i in range(8)]
        m_run = sb("m_run", [H, CPG + 1])
        dec = sb("dec", [H, CPG])
        rT = sb("rT", [RANK, GRP])
        la = sb("la", [P, GRP])
        ex = sb("ex", [P, GRP])
        Bc = sb("Bc", [P, GRP])
        gl = sb("gl", [P, CPG])
        NPU = 7
        ps_u = [pb(f"pc_u{i}", [P, GRP]) for i in range(NPU)]
        ps_la = pb("pc_la", [P, GRP])

        par = sem("tc_params")
        zeroed, made = sem("tc_zeroed"), sem("tc_masks")
        w_small_in = sem("tc_w_small")
        w_in_sem, w_hid, w_split = [sem(f"tc_w{i}") for i in range(4)], sem("tc_w_hi"), sem("tc_w_split")
        x_sem = [sem(f"tc_x{k}") for k in range(KC)]
        x_hid, x_split, halved = sem("tc_x_hi"), sem("tc_x_split"), sem("tc_halved")
        unit, la_done = sem("tc_unit"), sem("tc_la")
        small_in, rT_ready = sem("tc_small"), sem("tc_rT")
        f_abs, f_log, row_args, row_exp = sem("tc_f_abs"), sem("tc_f_log"), sem("tc_row_args"), sem("tc_row_exp")
        z_ready, z_abs, z_log, b_ready = sem("tc_z"), sem("tc_z_abs"), sem("tc_z_log"), sem("tc_B")
        vt_ready, q_sub, gl_ready = sem("tc_vt"), sem("tc_q_sub"), sem("tc_gl")
        cin_ready, acc_ready, th_ready = sem("tc_cin"), sem("tc_acc"), sem("tc_tanh")
        res_ready, res_out = sem("tc_res"), [sem("tc_res_out0"), sem("tc_res_out1")]
        rows_out, gl_out = sem("tc_rows_out"), sem("tc_gl_out")

        def unit_cols(n):
            if n == 0:
                return 0, C_QKG
            if n <= 4:
                pair, is_q = (n - 1) // 2, (n - 1) % 2
                return C_QKG + (0 if is_q else 2 * P) + pair * P, P
            return C_QK + (n - 5) * P, P

        def w_stage(n):
            return stage_s[:, :, :] if n == 0 else stage[:, :, ((n - 1) % 4) * P:((n - 1) % 4 + 1) * P]

        def w_unit(w, n):
            c, m = unit_cols(n)
            return w[:, :, c:c + m]

        X_NEXT = 6
        W_TOP, W_GATES, W_PAIR, W_CONV = range(0, 5), (5,), ((6, 7), (8,)), range(9, NU)

        def chunks(ap):
            return ap.rearrange("p (c l) -> p c l", l=P)

        def at(ap, first):
            v = ap[:, first:GRP:P]
            return v.rearrange("p (c o) -> p c o", o=1).to_broadcast((v.shape[0], CPG, P))

        with nc.Block() as block:
            @block.gpsimd
            def _(pool):
                pool.memset(keep_run[:, :], 1.0).then_inc(zeroed, 1)
                pool.memset(max_run[:, :], 0.0).then_inc(zeroed, 1)
                pool.memset(halo[:, :, :], 0.0).then_inc(made, 1)
                pool.memset(m_run[:, :], 0.0).then_inc(made, 1)
                pool.memset(ln_scale[:, :], math.log(DV ** -0.5)).then_inc(made, 1)
                pool.memset(stage_s[:, :, :], 0.0).then_inc(made, 1)
                pool.wait_ge(zeroed, 2)
                pool.memset(keep_run[:, 0:GRP:P], 0.0).then_inc(made, 1)
                pool.memset(max_run[:, 0:GRP:P], NEG).then_inc(made, 1)
                pool.wait_ge(x_split, KC)
                for n in range(1, NU):
                    if n > 4:
                        pool.wait_ge(w_split, n - 3)
                    c, m = unit_cols(n)
                    off = c - C_QK + OFF_QK if n > 4 else c - C_QKG + OFF_QKG
                    pool.dma_start(w_stage(n), w_in[0, :, off:off + m].rearrange("(k p) n -> p k n", p=P)
                                 ).then_inc(w_in_sem[(n - 1) % 4], 16)

            @block.sync
            def _(sp):
                def load_x(g, ks):
                    for k in ks:
                        sp.dma_start(stage[:, k, :], S["xT"][k, :, bass.ds(g * GRP, GRP)]).then_inc(x_sem[k], 16)

                load_x(0, range(KC))
                sp.wait_ge(made, 4)
                with nc.allow_non_contiguous_dma("parameters by channel"):
                    for c, off, n in ((C_I, OFF_I, H), (C_F, OFF_F, H), (C_R, OFF_R, RANK)):
                        sp.dma_start(stage_s[:, :, c:c + n], w_in[0, :, off:off + n].rearrange("(k p) n -> p k n", p=P)
                                     ).then_inc(w_small_in, 16)
                    for w in range(CW):
                        sp.dma_start(cw[:, w, :], conv_w[0, w].rearrange("(m p) -> p m", p=P)).then_inc(par, 16)
                    sp.dma_start(cb[:, :], conv_b.rearrange("l (m p) -> p (l m)", p=P)).then_inc(par, 16)
                    sp.dma_start(bi[:, :], b_gate[:, 0:H].rearrange("l h -> h l")).then_inc(par, 16)
                    sp.dma_start(bf[:, :], b_gate[:, H:2 * H].rearrange("l h -> h l")).then_inc(par, 16)
                    sp.dma_start(wg[:, :], w_gla[0]).then_inc(par, 16)
                    sp.dma_start(bg[:, :], b_gla.rearrange("l (c p) -> p (l c)", p=P)).then_inc(par, 16)

                def group(g, has_next):
                    following = g + 1 if isinstance(g, int) else sp.snap(g + 1)
                    tok = bass.ds(g * GRP, GRP)

                    def store(i, dst):
                        sp.wait_ge(res_ready, NRES * g + i + 1)
                        sp.dma_start(dst, res[i % 2][:, :]).then_inc(res_out[i % 2], 16)

                    for pair in range(2):
                        for v in range(5):
                            store(NV * pair + v, S["kR"][pair, v, :, tok])
                            if pair == 0 and v == 0:
                                sp.wait_ge(row_exp, 4 * (g + 1))
                                for q, ap in enumerate((UR, E1, E2, FG)):
                                    sp.dma_start(S["rows"][q, :, tok], ap[:, :]).then_inc(rows_out, 16)
                                sp.dma_start(S["nM"][:, tok], NM[:, :]).then_inc(rows_out, 16)
                                sp.dma_start(S["dec"][:, bass.ds(g * CPG, CPG)], dec[:, :]).then_inc(rows_out, 16)
                        sp.wait_ge(gl_ready, 2 * g + pair + 1)
                        sp.dma_start(S["gl"][pair, :, bass.ds(g * CPG, CPG)], gl[:, :]).then_inc(gl_out, 16)
                        for v in range(2):
                            store(NV * pair + 5 + v, S["qG"][pair, v, :, tok])
                    for m in range(NCONV):
                        store(2 * NV + m, S["qk"][m, :, tok])
                        opening = isinstance(g, int) and g == 0
                        if has_next and m in ((2, 3) if opening else range(4)):
                            if opening:
                                sp.wait_ge(w_split, NU)
                                load_x(following, range(4 * m - 8, 4 * m - 4))
                            else:
                                sp.wait_ge(x_split, KC * g + KC)
                                load_x(following, range(2 * m, 2 * m + 2))

                group(0, True)
                with sp.Fori(1, NG - 1) as g:
                    group(g, True)
                group(NG - 1, False)
                for b in range(2):
                    sp.wait_ge(res_out[b], 16 * NG * NRES // 2)
                sp.wait_ge(rows_out, 16 * 6 * NG)
                sp.wait_ge(gl_out, 16 * 2 * NG)

            @block.tensor
            def _(pe):
                def group(g, opening):
                    def product(n, producer_free):
                        pe.wait_ge(w_split, n + 1)
                        for s, v in producer_free:
                            pe.wait_ge(s, v)
                        c, m = unit_cols(n)
                        for k in range(KC):
                            if n == 0:
                                pe.wait_ge(x_split, KC * g + k + 1)
                            last = mm3(pe, ps_u[n % NPU][0:m, :], w_hi[:, k, c:c + m], w_lo[:, k, c:c + m],
                                       xT_hi[:, k, :], xT_lo[:, k, :], k == 0, k == KC - 1)
                        last.then_inc(unit, 1)

                    def gate(pair):
                        pe.wait_ge(rT_ready, g + 1)
                        pe.wait_ge(z_ready, 2 * g + pair)
                        pe.matmul(ps_la[:, :], wg[:, pair * P:(pair + 1) * P], rT[:, :],
                                  start=True, stop=True).then_inc(la_done, 1)

                    for n in range(NPU):
                        product(n, [] if opening or n == 6 else [(cin_ready, NCONV * g - 5 + n)])
                        if opening and n == 0:
                            pe.wait_ge(par, 16 * 9)
                        if n in (1, 2):
                            gate(n - 1)
                    product(7, [(small_in, 2 * g + 2), (rT_ready, g + 1)])
                    product(8, [(res_ready, NRES * g + 5)])
                    product(9, [(res_ready, NRES * g + NV)])
                    product(10, [(res_ready, NRES * g + NV + 5)])
                    product(11, [(res_ready, NRES * g + 2 * NV)])
                    product(12, [(cin_ready, NCONV * g + 1)])

                group(0, True)
                with pe.Fori(1, NG) as g:
                    group(g, False)

            @block.scalar
            def _(act):
                act.preload_act_table_set(TABLES)

                def w_high(n):
                    if n == 0:
                        act.wait_ge(w_small_in, 48)
                    else:
                        act.wait_ge(w_in_sem[(n - 1) % 4], 16 * ((n - 1) // 4 + 1))
                    act.activation(w_unit(w_hi, n), w_stage(n), ACT.Copy).then_inc(w_hid, 1)

                def x_high(g):
                    for k in range(KC):
                        act.wait_ge(x_sem[k], 16 * g + 16)
                        act.activation(xT_hi[:, k, :], stage[:, k, :], ACT.Copy).then_inc(x_hid, 1)

                x_high(0)

                def group(g, opening, has_next):
                    if opening:
                        act.wait_ge(made, 6)
                        for n in W_TOP:
                            w_high(n)
                        act.wait_ge(par, 16 * 9)
                        act.wait_ge(halved, 1)
                    act.preload_act_table_set(TABLES)
                    act.wait_ge(unit, NU * g + 1)
                    act.wait_ge(la_done, 2 * g)
                    act.activation(rT[:, :], ps_u[0][C_R:C_R + RANK, :], ACT.Copy).then_inc(rT_ready, 1)
                    act.wait_ge(rows_out, 96 * g)
                    act.activation(IG[:, :], ps_u[0][C_I:C_I + H, :], ACT.Copy).then_inc(small_in, 1)
                    act.activation(FG[:, :], ps_u[0][C_F:C_F + H, :], ACT.Copy).then_inc(small_in, 1)
                    act.wait_ge(f_abs, g + 1)
                    act.activation(E1[:, :], E1[:, :], ACT.Exp)
                    act.drain()
                    act.activation(E1[:, :], E1[:, :], ACT.Ln, bias=K["one"][0:H, :]).then_inc(f_log, 1)
                    if opening:
                        for n in W_GATES:
                            w_high(n)
                    for pair in range(2):
                        j = 2 * g + pair
                        act.wait_ge(la_done, j + 1)
                        act.wait_ge(b_ready, j)
                        act.activation(la[:, :], ps_la[:, :], ACT.Identity, bias=bg[:, pair:pair + 1]).then_inc(z_ready, 1)
                        act.wait_ge(z_abs, j + 1)
                        act.activation(ex[:, :], ex[:, :], ACT.Exp)
                        act.drain()
                        act.activation(ex[:, :], ex[:, :], ACT.Ln, bias=K["one"][:, :]).then_inc(z_log, 1)
                        if pair == 0:
                            act.wait_ge(row_args, g + 1)
                            act.activation(E1[:, :], E1[:, :], ACT.Exp).then_inc(row_exp, 1)
                            act.activation(E2[:, :], E2[:, :], ACT.Exp, scale=-1.0).then_inc(row_exp, 1)
                            act.activation(FG[:, :], FG[:, :], ACT.Exp, bias=ln_scale[:, :]).then_inc(row_exp, 1)
                            act.activation(dec[:, :], dec[:, :], ACT.Exp).then_inc(row_exp, 1)
                        act.wait_ge(b_ready, j + 1)
                        for v in range(5):
                            i = NV * pair + v
                            if i >= 2:
                                act.wait_ge(res_ready, NRES * g + i - 1)
                            first = SUB * v + SUB // 2 - 1 if v < NSUB else P - 1
                            for c in range(CPG):
                                a = c * P
                                last = act.activation(vt[i % 2][:, a:a + P], Bc[:, a:a + P], ACT.Exp,
                                                      scale=-1.0, bias=Bc[:, a + first:a + first + 1])
                            last.then_inc(vt_ready, 1)
                        act.wait_ge(gl_out, 16 * j)
                        act.activation(gl[:, :], Bc[:, P - 1:GRP:P], ACT.Exp).then_inc(gl_ready, 1)
                        i = NV * pair + 5
                        act.wait_ge(res_ready, NRES * g + i - 1)
                        act.activation(vt[i % 2][:, :], Bc[:, :], ACT.Exp).then_inc(vt_ready, 1)
                        i += 1
                        act.wait_ge(q_sub, j + 1)
                        act.activation(vt[i % 2][:, :], vt[i % 2][:, :], ACT.Exp).then_inc(vt_ready, 1)
                        if opening:
                            for n in W_PAIR[pair]:
                                w_high(n)
                    act.preload_act_table_set("exp_and_others")

                    def copy_in(m):
                        b = m % 2
                        act.wait_ge(unit, NU * g + 6 + m)
                        act.wait_ge(acc_ready, NCONV * g + m - 1) if m >= 2 else act.wait_ge(acc_ready, NCONV * g)
                        act.activation(cin[b][:, CW - 1:CW - 1 + GRP], ps_u[(5 + m) % NPU][:, :], ACT.Copy)
                        act.wait_ge(res_ready, NRES * g + 2 * NV + m - 2) if m >= 3 else act.wait_ge(res_ready, NRES * g)
                        act.activation(acc[m % 3][:, :], ps_u[(5 + m) % NPU][:, :], ACT.Identity,
                                       scale=cw[:, CW - 1, m:m + 1], bias=cb[:, m:m + 1]).then_inc(cin_ready, 1)

                    def tanh(m):
                        act.wait_ge(acc_ready, NCONV * g + m + 1)
                        act.wait_ge(res_ready, NRES * g + 2 * NV + max(m - 1, 0))
                        act.activation(th[m % 2][:, :], acc[m % 3][:, :], ACT.Tanh).then_inc(th_ready, 1)

                    for m in range(NCONV):
                        if opening and m < len(W_CONV):
                            w_high(W_CONV[m])
                        copy_in(m)
                        if has_next and m == X_NEXT:
                            act.wait_ge(unit, NU * g + NU)
                            x_high(g + 1)
                        if m:
                            tanh(m - 1)
                    tanh(NCONV - 1)

                group(0, True, True)
                with act.Fori(1, NG - 1) as g:
                    group(g, False, True)
                group(NG - 1, False, False)

            @block.vector
            def _(dve):
                def x_low(g):
                    for k in range(KC):
                        dve.wait_ge(x_hid, KC * g + k + 1)
                        dve.tensor_tensor(xT_lo[:, k, :], stage[:, k, :], xT_hi[:, k, :].bitcast(F32), ALU.subtract
                                          ).then_inc(x_split, 1)

                x_low(0)
                dve.wait_ge(par, 16 * 9)
                dve.wait_ge(made, 6)
                dve.tensor_scalar(cw[:, :, :], cw[:, :, :], 0.5, None, ALU.mult)
                dve.drain()
                dve.tensor_scalar(cb[:, :], cb[:, :], 0.5, None, ALU.mult).then_inc(halved, 1)
                dve.drain()

                def w_low(n):
                    dve.wait_ge(w_hid, n + 1)
                    dve.tensor_tensor(w_unit(w_lo, n), w_stage(n), w_unit(w_hi, n).bitcast(F32), ALU.subtract
                                      ).then_inc(w_split, 1)

                def group(g, opening, has_next):
                    if opening:
                        for n in W_TOP:
                            w_low(n)
                    dve.wait_ge(small_in, 2 * g + 2)
                    dve.tensor_scalar(IG[:, :], IG[:, :], bi[:, 0:1], None, ALU.add)
                    dve.tensor_scalar(FG[:, :], FG[:, :], bf[:, 0:1], None, ALU.add)
                    dve.drain()
                    neg_abs(dve, E1[:, :], FG[:, :]).then_inc(f_abs, 1)

                    def z_abs_step(pair):
                        dve.wait_ge(z_ready, 2 * g + pair + 1)
                        neg_abs(dve, ex[:, :], la[:, :]).then_inc(z_abs, 1)

                    z_abs_step(0)
                    dve.wait_ge(f_log, g + 1)
                    dve.scalar_tensor_tensor(out=FG[:, :], in0=FG[:, :], scalar=0.0, in1=E1[:, :],
                                             op0=ALU.min, op1=ALU.subtract)
                    dve.drain()
                    dve.tensor_tensor_scan(BR[:, :], keep_run[0:H, :], FG[:, :], 0.0, ALU.mult, ALU.add)
                    dve.drain()
                    dve.tensor_tensor(UR[:, :], IG[:, :], BR[:, :], ALU.subtract)
                    dve.drain()
                    dve.tensor_tensor_scan(CM[:, :], max_run[:, :], UR[:, :], NEG, ALU.add, ALU.max)
                    dve.tensor_copy(m_run[:, 0:1], m_run[:, CPG:CPG + 1])
                    dve.drain()
                    dve.tensor_tensor_scan(m_run[:, 1:CPG + 1], CM[:, P - 1:GRP:P], BR[:, P - 1:GRP:P],
                                           m_run[:, 0:1], ALU.max, ALU.add)
                    dve.drain()
                    m_bc = m_run[:, 0:CPG].rearrange("p (c o) -> p c o", o=1).to_broadcast((H, CPG, P))
                    dve.tensor_tensor(chunks(CM[:, :]), chunks(CM[:, :]), m_bc, ALU.max)
                    dve.drain()
                    dve.tensor_tensor(chunks(E1[:, :]), m_bc, chunks(CM[:, :]), ALU.subtract)
                    dve.tensor_tensor(E2[:, :], BR[:, :], CM[:, :], ALU.add)
                    dve.tensor_scalar(NM[:, :], CM[:, :], -1.0, None, ALU.mult)
                    dve.tensor_tensor(chunks(FG[:, :]), chunks(UR[:, :]), at(CM, P - 1), ALU.subtract)
                    dve.tensor_tensor(dec[:, :], m_run[:, 0:CPG], CM[:, P - 1:GRP:P], ALU.subtract).then_inc(row_args, 1)
                    if opening:
                        for n in W_GATES:
                            w_low(n)

                    def result(i, producer, out_fn):
                        dve.wait_ge(res_out[i % 2], 8 * NRES * g + 16 * (i // 2))
                        dve.wait_ge(*producer)
                        out_fn(res[i % 2][:, :]).then_inc(res_ready, 1)

                    for pair in range(2):
                        j = 2 * g + pair
                        if pair:
                            z_abs_step(1)
                        dve.wait_ge(z_log, j + 1)
                        dve.scalar_tensor_tensor(out=la[:, :], in0=la[:, :], scalar=0.0, in1=ex[:, :],
                                                 op0=ALU.min, op1=ALU.subtract)
                        dve.drain()
                        dve.tensor_scalar(la[:, :], la[:, :], 1.0 / 16.0, None, ALU.mult)
                        dve.drain()
                        dve.tensor_tensor_scan(Bc[:, :], keep_run[:, :], la[:, :], 0.0, ALU.mult, ALU.add).then_inc(b_ready, 1)
                        kps, qps = ps_u[1 + 2 * pair], ps_u[2 + 2 * pair]
                        dve.wait_ge(unit, NU * g + 2 + 2 * pair)
                        for v in range(5):
                            i = NV * pair + v
                            result(i, (vt_ready, 2 * NV * g + i + 1), lambda o: dve.scalar_tensor_tensor(
                                out=o, in0=vt[i % 2][:, :], scalar=VT_CAP, in1=kps[:, :], op0=ALU.min, op1=ALU.mult))
                        i = NV * pair + 6
                        blocks = Bc[:, :].rearrange("p (b l) -> p b l", l=SUB)
                        ref = Bc[:, SUB // 2 - 1:GRP:SUB].rearrange("p (b o) -> p b o", o=1).to_broadcast((P, GRP // SUB, SUB))
                        dve.drain()
                        dve.wait_ge(unit, NU * g + 3 + 2 * pair)
                        dve.tensor_tensor(vt[i % 2][:, :].rearrange("p (b l) -> p b l", l=SUB), blocks, ref,
                                          ALU.subtract).then_inc(q_sub, 1)
                        for v in (5, 6):
                            i = NV * pair + v
                            result(i, (vt_ready, 2 * NV * g + i + 1), lambda o: dve.scalar_tensor_tensor(
                                out=o, in0=qps[:, :], scalar=DK ** -0.5, in1=vt[i % 2][:, :], op0=ALU.mult, op1=ALU.mult))
                        if opening:
                            for n in W_PAIR[pair]:
                                w_low(n)

                    def conv(m):
                        b = m % 2
                        dve.wait_ge(cin_ready, NCONV * g + m + 1)
                        dve.tensor_copy(cin[b][:, 0:CW - 1], halo[:, m, :])
                        dve.drain()
                        dve.tensor_copy(halo[:, m, :], cin[b][:, GRP:GRP + CW - 1])
                        for w in range(CW - 1):
                            last = dve.scalar_tensor_tensor(out=acc[m % 3][:, :], in0=cin[b][:, w:w + GRP],
                                                            scalar=cw[:, w, m:m + 1], in1=acc[m % 3][:, :],
                                                            op0=ALU.mult, op1=ALU.add)
                            if w < CW - 2:
                                dve.drain()
                        last.then_inc(acc_ready, 1)

                    def silu(m):
                        i = 2 * NV + m
                        result(i, (th_ready, NCONV * g + m + 1), lambda o: dve.scalar_tensor_tensor(
                            out=o, in0=th[m % 2][:, :], scalar=1.0, in1=acc[m % 3][:, :], op0=ALU.add, op1=ALU.mult))

                    for m in range(NCONV):
                        if opening and m < len(W_CONV):
                            w_low(W_CONV[m])
                        if has_next and m == X_NEXT:
                            x_low(g + 1)
                        conv(m)
                        if m:
                            silu(m - 1)
                    silu(NCONV - 1)

                group(0, True, True)
                with dve.Fori(1, NG - 1) as g:
                    group(g, False, True)
                group(NG - 1, False, False)


def recur(nc, sem, K, S, w_out, w_stage):
    DA = DV + 1
    with ExitStack() as ctx:
        def sb(name, shape, dt=F32):
            return ctx.enter_context(nc.sbuf_tensor(name, shape, dt))

        def pb(name, shape):
            return ctx.enter_context(nc.psum_tensor(name, shape, F32))

        qk = [sb(f"r_qk{i}", [P, 2 * H, P]) for i in range(2)]
        kr = [sb(f"r_kr{i}", [P, 2, 5, P]) for i in range(2)]
        q2 = [sb(f"r_q2{i}", [P, 2, 2, 2, P]) for i in range(2)]
        va = [sb(f"r_va{i}", [P, H, DA]) for i in range(2)]
        vg = [sb(f"r_vg{i}", [P, H, P]) for i in range(2)]
        gate = [sb(f"r_gate{i}", [P, D]) for i in range(2)]
        o_g = [sb(f"r_o{i}", [P, H, P]) for i in range(2)]
        rowT = [sb(f"r_row{i}", [4 * H, P]) for i in range(2)]
        nM = [sb(f"r_nM{i}", [P, H, P]) for i in range(2)]
        dec = sb("r_dec", [P, H, NT])
        gl = sb("r_gl", [P, 2, NT])
        cols = [sb(f"r_cols{i}", [P, 4 * H]) for i in range(2)]
        U, A, EN, WC = 0, H, 2 * H, 3 * H
        arg = sb("r_arg", [P, H, P])
        pm = sb("r_pm", [P, H, P])
        sT = sb("r_sT", [P, H, P])
        kw = sb("r_kw", [P, H, P])
        kd = sb("r_kd", [P, 2, P])
        aT = sb("r_aT", [P, 2 * H // 2, P])
        qc = sb("r_qc", [P, H, DA])
        num = [sb(f"r_num{i}", [P, H, DA]) for i in range(2)]
        nd = sb("r_nd", [P, H])
        hm = sb("r_hm", [P, H, P])
        junk = sb("r_junk", [P, H, P])
        junk_g = sb("r_junk_g", [P, H, P])
        ms = sb("r_ms", [P, 2 * H])
        ms_ln = sb("r_msln", [P, 2 * H])
        rs = sb("r_rs", [P, 2 * H])
        y = sb("r_y", [P, D])
        C = sb("r_C", [P, H, DA])
        G = sb("r_G", [P, 2, P])
        bank = [pb(f"r_ps{i}", [P, 512]) for i in range(8)]
        ps_qk = bank[0][:, :].rearrange("p (h j) -> p h j", h=H)
        ps_o = ps_qk
        ps_k = bank[1][:, :].rearrange("p (h j) -> p h j", h=H)
        ps_gkv = bank[1][:, :].rearrange("p (h j) -> p h j", h=2)
        ps_kd = bank[2][:, 0:2 * P].rearrange("p (h j) -> p h j", h=2)
        ps_cols = bank[2][:, 2 * P:2 * P + 4 * H]
        ps_a = bank[3][:, :].rearrange("p (h j) -> p h j", h=H)

        def head(b, h):
            if h < 3:
                return bank[4 + b][:, h * DA:(h + 1) * DA]
            return bank[7][:, b * DA:(b + 1) * DA]

        N_, C_, KV_ = 0, 1, 2

        fixed, made, w_in_sem = sem("rc_fixed"), sem("rc_made"), sem("rc_w")
        loaded = [sem("rc_loaded0"), sem("rc_loaded1")]
        gate_in = [sem("rc_gate0"), sem("rc_gate1")]
        NL = 8
        scored, turned, a_done = sem("rc_scored"), sem("rc_turned"), sem("rc_a_done")
        qc_done, n_done, kv_done = sem("rc_qC"), sem("rc_num"), sem("rc_kv")
        o_done, gkv_done, o_copied = sem("rc_o"), sem("rc_gkv"), sem("rc_o_copied")
        arg_ready, cols_ready, pm_ready = sem("rc_arg"), sem("rc_cols"), sem("rc_pm")
        kw_ready, kd_ready, qcs_ready = sem("rc_kw"), sem("rc_kd"), sem("rc_qcs")
        sT_ready, aT_ready, num_ready = sem("rc_sT"), sem("rc_aT"), sem("rc_num_sum")
        ms_ready, rs_ready = sem("rc_ms"), sem("rc_rs")
        y_ready, y_out, C_ready, G_ready = sem("rc_y"), sem("rc_y_out"), sem("rc_C"), sem("rc_G")

        def over_tiles(eng, step):
            with eng.Fori(0, NT // 2) as i:
                for u in range(2):
                    step(2 * i + u, u, i)

        with nc.Block() as block:
            @block.gpsimd
            def _(pool):
                pool.memset(C[:, :, :], 0.0).then_inc(made, 1)
                pool.memset(G[:, :, :], 0.0).then_inc(made, 1)
                for u in range(2):
                    pool.memset(q2[u][:, :, :, :, :], 0.0).then_inc(made, 1)
                    pool.memset(va[u][:, :, DV:DA], 1.0).then_inc(made, 1)

                def step(t, u, i):
                    pool.wait_ge(loaded[u], 16 * NL * i + 16 * NL)
                    pool.wait_ge(pm_ready, t)
                    pool.tensor_tensor(arg[:, :, :], nM[u][:, :, :],
                                       K["drop"][:, :].rearrange("p (o j) -> p o j", o=1).to_broadcast((P, H, P)),
                                       ALU.add).then_inc(arg_ready, 1)

                over_tiles(pool, step)

            @block.sync
            def _(sp):
                sp.dma_start(dec[:, :, :].rearrange("p h c -> p (h c)"),
                             S["dec"].rearrange("(o h) c -> o (h c)", o=1).to_broadcast((P, H * NT))).then_inc(fixed, 16)
                sp.dma_start(gl[:, :, :], S["gl"].rearrange("q p c -> p q c")).then_inc(fixed, 16)

                def store(t, tile):
                    sp.wait_ge(y_ready, t + 1)
                    sp.dma_start(S["y"][bass.ds(tile, 1)].rearrange("o p d -> (o p) d"), y[:, :]).then_inc(y_out, 16)

                def step(t, u, waits):
                    first, tile = (sp.snap(t * P), sp.snap(t)) if waits else (t * P, t)
                    tok, row = bass.ds(first, P), bass.ds(tile, 1)
                    if waits:
                        sp.wait_ge(gkv_done, t - 1)

                    def load(dst, src):
                        sp.dma_start(dst, src).then_inc(loaded[u], 16)

                    load(qk[u][:, :, :], S["qk"][:, :, tok].rearrange("m p t -> p m t"))
                    load(rowT[u][:, :], S["rows"][:, :, tok].rearrange("q h t -> (q h) t"))
                    load(nM[u][:, :, :], S["nM"][:, tok].rearrange("(o h) t -> o h t", o=1).to_broadcast((P, H, P)))
                    load(kr[u][:, :, :, :], S["kR"][:, :, :, tok].rearrange("q v p t -> p q v t"))
                    if not waits and t == 0:
                        sp.wait_ge(made, 6)
                    for h in range(2):
                        r = slice(h * DK, (h + 1) * DK)
                        load(q2[u][r, :, :, h, :], S["qG"][:, :, r, tok].rearrange("q v p t -> p q v t"))
                    load(va[u][:, :, 0:DV], S["val"][row, :, 0:W].rearrange("o p (h d) -> (o p) h d", h=H))
                    load(vg[u][:, :, :], S["val"][row, :, W:D].rearrange("o p (h d) -> (o p) h d", h=H))
                    if waits:
                        store(t - 2, sp.snap(t - 2))
                    sp.dma_start(gate[u][:, :], S["gate"][row].rearrange("o p d -> (o p) d")).then_inc(gate_in[u], 16)

                step(0, 0, False)
                step(1, 1, False)
                with sp.Fori(1, NT // 2) as i:
                    for u in range(2):
                        step(2 * i + u, u, True)
                for k in range(KC):
                    sp.dma_start(w_stage[:, k, :], w_out[0, k * P:(k + 1) * P, :]).then_inc(w_in_sem, 16)
                store(NT - 2, NT - 2)
                store(NT - 1, NT - 1)
                sp.wait_ge(y_out, 16 * NT)
                sp.wait_ge(w_in_sem, 16 * KC)

            @block.tensor
            def _(pe):
                pe.wait_ge(made, 6)

                def step(t, u, i):
                    pe.wait_ge(loaded[u], 16 * NL * i + 16 * NL)
                    pe.wait_ge(o_copied, t)
                    for h in range(H):
                        last = pe.matmul(ps_qk[:, h, :], qk[u][:, H + h, :], qk[u][:, h, :], start=True, stop=True)
                    last.then_inc(scored, 1)
                    pe.wait_ge(cols_ready, t)
                    pe.wait_ge(kd_ready, t)
                    pe.wait_ge(G_ready, t)
                    for h in range(H):
                        pe.transpose(ps_k[:, h, :], qk[u][:, H + h, :], K["ident"][:, :])
                    for q in range(2):
                        pe.transpose(ps_kd[:, q, :], kr[u][:, q, 4, :], K["ident"][:, :])
                    last = pe.transpose(ps_cols, rowT[u][:, :], K["ident"][0:4 * H, 0:4 * H])
                    last.then_inc(turned, 1)
                    pe.wait_ge(aT_ready, t)
                    for q in range(2):
                        for r in range(NSUB):
                            j = slice(r * SUB, (r + 1) * SUB)
                            last = pe.matmul(ps_a[:, 2 * q:2 * q + 2, j], kr[u][:, q, r, :], q2[u][:, q, 1, :, j],
                                             start=True, stop=True)
                    last.then_inc(a_done, 1)
                    pe.wait_ge(C_ready, t)
                    pe.wait_ge(qcs_ready, t)
                    pe.wait_ge(num_ready, t)
                    for h in range(H):
                        last = pe.matmul(head(C_, h), qk[u][:, h, :], C[:, h, :], start=True, stop=True)
                    last.then_inc(qc_done, 1)
                    pe.wait_ge(kw_ready, t + 1)
                    for h in range(H):
                        last = pe.matmul(head(KV_, h), kw[:, h, :], va[u][:, h, :], start=True, stop=True)
                    last.then_inc(kv_done, 1)
                    pe.wait_ge(sT_ready, t + 1)
                    for h in range(H):
                        last = pe.matmul(head(N_, h), sT[:, h, :], va[u][:, h, :], start=True, stop=True)
                    last.then_inc(n_done, 1)
                    pe.wait_ge(aT_ready, t + 1)
                    pe.wait_ge(G_ready, t)
                    for h in range(H):
                        pe.matmul(ps_o[:, h, :], aT[:, h, :], vg[u][:, h, :], start=True, stop=False)
                        last = pe.matmul(ps_o[:, h, :], q2[u][:, h // 2, 0, h % 2, :], G[:, h // 2, :],
                                         start=False, stop=True)
                    last.then_inc(o_done, 1)
                    pe.wait_ge(kd_ready, t + 1)
                    for q in range(2):
                        last = pe.matmul(ps_gkv[:, q, :], kd[:, q, :],
                                         vg[u][:, 2 * q:2 * q + 2, :].rearrange("p h d -> p (h d)"), start=True, stop=True)
                    last.then_inc(gkv_done, 1)

                over_tiles(pe, step)

            @block.scalar
            def _(act):
                act.preload_act_table_set(TABLES)

                def norm(t):
                    act.wait_ge(ms_ready, t + 1)
                    act.activation(ms_ln[:, :], ms[:, :], ACT.Ln, scale=1.0 / DV, bias=K["eps"][:, :])
                    act.drain()
                    act.wait_ge(y_ready, t)
                    act.activation(rs[:, :], ms_ln[:, :], ACT.Exp, scale=-0.5).then_inc(rs_ready, 1)

                def step(t, u, first):
                    act.wait_ge(turned, t + 1)
                    act.activation(cols[u][:, :], ps_cols, ACT.Copy).then_inc(cols_ready, 1)
                    act.drain()
                    act.wait_ge(arg_ready, t + 1)
                    if not first:
                        act.wait_ge(sT_ready, t)
                    for h in range(H):
                        last = act.activation(pm[:, h, :], arg[:, h, :], ACT.Exp, bias=cols[u][:, U + h:U + h + 1])
                    last.then_inc(pm_ready, 1)
                    if not first:
                        act.wait_ge(kv_done, t)
                    for h in range(H):
                        last = act.activation(kw[:, h, :], ps_k[:, h, :], ACT.Copy, scale=cols[u][:, WC + h:WC + h + 1])
                    last.then_inc(kw_ready, 1)
                    if not first:
                        act.wait_ge(gkv_done, t)
                    act.activation(kd[:, :, :], ps_kd, ACT.Copy).then_inc(kd_ready, 1)
                    if not first:
                        norm(t - 1)
                    act.wait_ge(n_done, t + 1)
                    if not first:
                        act.wait_ge(num_ready, t)
                    for h in range(H):
                        last = act.activation(qc[:, h, :], head(C_, h), ACT.Copy, scale=cols[u][:, A + h:A + h + 1])
                    last.then_inc(qcs_ready, 1)
                    act.wait_ge(o_done, t + 1)
                    act.activation(o_g[u][:, :, :], ps_o, ACT.Copy)
                    for h in range(H):
                        last = act.activation(junk_g[:, h, :], ps_o[:, h, :], ACT.Square, accum_out=ms[:, H + h:H + h + 1])
                    last.then_inc(o_copied, 1)
                    act.drain()

                step(0, 0, True)
                step(1, 1, False)
                with act.Fori(1, NT // 2) as i:
                    for u in range(2):
                        step(2 * i + u, u, False)
                norm(NT - 1)


            @block.vector
            def _(dve):
                dve.wait_ge(fixed, 32)

                def step(t, u, i, first):
                    dve.wait_ge(scored, t + 1)
                    if not first:
                        dve.wait_ge(n_done, t)
                    dve.wait_ge(pm_ready, t + 1)
                    dve.scalar_tensor_tensor(out=sT[:, :, :], in0=ps_qk, scalar=DV ** -0.5, in1=pm[:, :, :],
                                             op0=ALU.mult, op1=ALU.mult).then_inc(sT_ready, 1)
                    dve.wait_ge(a_done, t + 1)
                    if not first:
                        dve.wait_ge(o_done, t)
                    dve.tensor_tensor(aT[:, :, :], ps_a,
                                      K["keep"][:, :].rearrange("p (o j) -> p o j", o=1).to_broadcast((P, H, P)),
                                      ALU.mult).then_inc(aT_ready, 1)
                    if not first:
                        gated(t - 1, 1 - u, i - 1 + u)
                    dve.wait_ge(qcs_ready, t + 1)
                    for h in range(H):
                        last = dve.scalar_tensor_tensor(out=C[:, h, :], in0=C[:, h, :], scalar=dec[:, h, bass.ds(t, 1)],
                                                        in1=head(KV_, h), op0=ALU.mult, op1=ALU.add)
                    last.then_inc(C_ready, 1)
                    dve.tensor_tensor(num[u][:, 0:3, :], qc[:, 0:3, :],
                                      bank[4][:, 0:3 * DA].rearrange("p (h d) -> p h d", d=DA), ALU.add)
                    dve.tensor_tensor(num[u][:, 3, :], qc[:, 3, :], head(N_, 3), ALU.add).then_inc(num_ready, 1)
                    dve.wait_ge(gkv_done, t + 1)
                    for h in range(H):
                        r = slice((h % 2) * DK, (h % 2 + 1) * DK)
                        last = dve.scalar_tensor_tensor(out=G[r, h // 2, :], in0=G[r, h // 2, :],
                                                        scalar=gl[r, h // 2, bass.ds(t, 1)],
                                                        in1=ps_gkv[r, h // 2, (h % 2) * P:(h % 2 + 1) * P],
                                                        op0=ALU.mult, op1=ALU.add)
                    last.then_inc(G_ready, 1)

                def head_squares(t, u):
                    dve.drain()
                    den = num[u][:, :, DV:DA].rearrange("p h o -> p (h o)")
                    dve.scalar_tensor_tensor(out=nd[:, :], in0=den, scalar=-1.0, in1=den, op0=ALU.mult, op1=ALU.max)
                    dve.drain()
                    dve.tensor_tensor(nd[:, :], nd[:, :], cols[u][:, EN:EN + H], ALU.max)
                    dve.drain()
                    dve.reciprocal(nd[:, :], nd[:, :])
                    dve.drain()
                    dve.tensor_tensor(hm[:, :, :], num[u][:, :, 0:DV],
                                      nd[:, :].rearrange("p (h o) -> p h o", o=1).to_broadcast((P, H, DV)), ALU.mult)
                    dve.drain()
                    if not (isinstance(t, int) and t == 0):
                        dve.wait_ge(rs_ready, t)
                    for h in range(H):
                        last = dve.tensor_tensor_reduce(junk[:, h, :], hm[:, h, :], hm[:, h, :], 1.0, 0.0, ALU.mult, ALU.add,
                                                        ms[:, h:h + 1])
                    last.then_inc(ms_ready, 1)

                def gated(t, u, i):
                    dve.drain()
                    dve.wait_ge(rs_ready, t + 1)
                    dve.wait_ge(gate_in[u], 16 * i + 16)
                    if not (isinstance(t, int) and t == 0):
                        dve.wait_ge(y_out, 16 * t)
                    for h in range(2 * H):
                        c = slice(h * DV, (h + 1) * DV)
                        src = hm[:, h, :] if h < H else o_g[u][:, h - H, :]
                        last = dve.scalar_tensor_tensor(out=y[:, c], in0=src, scalar=rs[:, h:h + 1], in1=gate[u][:, c],
                                                        op0=ALU.mult, op1=ALU.mult)
                    last.then_inc(y_ready, 1)

                step(0, 0, 0, True)
                head_squares(0, 0)
                step(1, 1, 0, False)
                head_squares(1, 1)
                with dve.Fori(1, NT // 2) as i:
                    for u in range(2):
                        step(2 * i + u, u, i, False)
                        head_squares(2 * i + u, u)
                gated(NT - 1, 1, NT // 2 - 1)



def load_expert_slice(eng, w_gu, w_down, row, i, w_stage):
    src = (w_gu[0, row, i * P:(i + 1) * P, :] if i < KC
           else w_down[0, row, (i - KC) * P:(i - KC + 1) * P, :])
    return eng.dma_start(w_stage[:, i, :], src.rearrange("o p n -> (o p) n"))


def project_out_and_route(nc, sem, K, x, norm_ffn, w_group, b_group, w_expert, b_expert, w_gu, w_down,
                          w_stage, S, R):
    x_v = x.rearrange("b (t p) d -> (b t) p d", p=P)
    NLG = NGRP + NE
    NBC = NBLK + 2
    with ExitStack() as ctx:
        def sb(name, shape, dt=F32):
            return ctx.enter_context(nc.sbuf_tensor(name, shape, dt))

        def pb(name, shape):
            return ctx.enter_context(nc.psum_tensor(name, shape, F32))

        w_hi = sb("wo_hi", [P, KC, D], F32R)
        w_lo = sb("wo_lo", [P, KC, D], F32R)
        w_r = sb("w_router", [P, KC, NLG])
        b_r = sb("b_router", [P, NLG])
        nf = sb("norm_ffn_bc", [P, D])
        y_in = [sb(f"y_in{i}", [P, D]) for i in range(2)]
        x_in = [sb(f"xr_in{i}", [P, D]) for i in range(2)]
        yT_hi = [sb(f"yT_hi{i}", [P, KC, P], F32R) for i in range(2)]
        yT_lo = [sb(f"yT_lo{i}", [P, KC, P], F32R) for i in range(2)]
        h1 = [sb(f"h1_{i}", [P, D]) for i in range(2)]
        xt = [sb(f"xt_{i}", [P, D]) for i in range(2)]
        xtT = sb("xtT", [P, KC, P])
        sq = sb("sq_c", [P, D])
        ssq = sb("ssq_c", [P, 1])
        lnv = sb("lnv_c", [P, 1])
        rstd = sb("rstd_c", [P, 1])
        lg = sb("lg", [P, NT, NLG])
        gm = sb("gm", [P, NT])
        gd = sb("gd", [P, NT, NGRP])
        gex = sb("gex", [P, NT, NGRP])
        gsum = sb("gsum", [P, NT])
        og = sb("og", [P, NT, NGRP])
        gif = sb("gif", [P, NT])
        ig = sb("ig", [P, NT, NGRP])
        selg = sb("selg", [P, NT, EPG, NGRP])
        sel = sb("sel", [P, NT, EPG])
        em = sb("em", [P, 2, NT])
        eif = sb("eif", [P, 2, NT])
        ie = sb("ie", [P, NT, EPG])
        oe = sb("oe", [P, NT, EPG])
        e2 = sb("e2", [P, NT])
        den = sb("den_r", [P, NT])
        iota = sb("iota", [P, P])
        tokf = sb("tokf", [P, NT, 2])
        blki = sb("blki", [P, 2 * NT], I32)
        blkf = sb("blkf", [P, 2 * NT])
        lanef = sb("lanef", [P, 2 * NT])
        oh = sb("oh", [P, NT, 2, NE])
        both = sb("both", [P, NE, NT])
        upto = sb("upto", [P, NE, NT])
        before = sb("before", [P, NE, NT])
        anew = sb("anew", [P, NE, NT])
        total = sb("total", [P, NE])
        nbi = sb("nbi", [P, NE], I32)
        nbf = sb("nbf", [P, NE])
        base = sb("base", [P, NE])
        incl = sb("incl", [P, NE])
        rank = sb("rank", [P, NT, NE])
        pick = sb("pick", [P, NT, 2, NE])
        posf = sb("posf", [P, NT * 2])
        ps_y = pb("pr_y", [P, KC, P])
        ps_o = pb("pr_o", [P, D])
        ps_x = pb("pr_x", [P, KC, P])
        ps_l = pb("pr_l", [P, 512])
        ps_c = pb("pr_c", [P, 512])

        par, made = sem("rt_params"), sem("rt_made")
        w_next, w_hid, w_split = sem("rt_w_next"), sem("rt_w_hi"), sem("rt_w_split")
        y_sem, x_sem = [sem("rt_y0"), sem("rt_y1")], [sem("rt_x0"), sem("rt_x1")]
        y_turned, hi_ready, lo_ready = sem("rt_y_turned"), sem("rt_hi"), sem("rt_lo")
        out_done, h1_ready, ssq_ready = sem("rt_out"), sem("rt_h1"), sem("rt_ssq")
        scaled, xt_ready, x_turned, xtT_ready = sem("rt_scaled"), sem("rt_xt"), sem("rt_x_turned"), sem("rt_xtT")
        lg_done, lg_ready, gd_ready, gex_ready = sem("rt_logits"), sem("rt_lg"), sem("rt_gd"), sem("rt_gex")
        ed_ready, e2_ready = sem("rt_ed"), sem("rt_e2")
        h1_out, xt_out = [sem("rt_h1_out0"), sem("rt_h1_out1")], [sem("rt_xt_out0"), sem("rt_xt_out1")]
        counted, ranked, hot_ready, table_done = sem("rt_counted"), sem("rt_ranked"), sem("rt_hot"), sem("rt_table")

        def over_tiles(eng, step):
            with eng.Fori(0, NT // 2) as i:
                for u in range(2):
                    step(2 * i + u, u, i)

        lane_hot = w_hi[:, 0:4, :].rearrange("p k (c l) -> p (k c) l", l=P)
        blk_hot = w_lo[:, 0:4, :].rearrange("p k (c l) -> p (k c) l", l=P)[:, :, 0:NBC]

        with nc.Block() as block:
            @block.gpsimd
            def _(pool):
                pool.iota(iota[:, :], [[1, P]], base=0, channel_multiplier=0,
                          allow_small_or_imprecise_dtypes=True).then_inc(made, 1)
                pool.iota(tokf[:, :, :], [[P, NT], [0, 2]], base=0, channel_multiplier=1,
                          allow_small_or_imprecise_dtypes=True).then_inc(made, 1)
                pool.memset(anew[:, :, :], 1.0)
                pool.drain()
                pool.memset(anew[:, :, 0:1], 0.0).then_inc(made, 1)

            @block.sync
            def _(sp):
                for u in range(2):
                    sp.dma_start(y_in[u][:, :], S["y"][u]).then_inc(y_sem[u], 16)
                for u in range(2):
                    sp.dma_start(x_in[u][:, :], x_v[u]).then_inc(x_sem[u], 16)
                with nc.allow_non_contiguous_dma("small router weights"):
                    sp.dma_start(w_r[:, :, 0:NGRP], w_group.rearrange("l (c p) n -> p (l c) n", p=P)).then_inc(par, 16)
                    sp.dma_start(w_r[:, :, NGRP:], w_expert.rearrange("l (c p) n -> p (l c) n", p=P)).then_inc(par, 16)
                    sp.dma_start(b_r[:, 0:NGRP], b_group.to_broadcast((P, NGRP))).then_inc(par, 16)
                    sp.dma_start(b_r[:, NGRP:], b_expert.to_broadcast((P, NE))).then_inc(par, 16)
                    sp.dma_start(nf[:, :], norm_ffn.to_broadcast((P, D))).then_inc(par, 16)

                def step(t, u):
                    tile = sp.snap(t)
                    sp.wait_ge(y_turned, t - 1)
                    sp.dma_start(y_in[u][:, :], S["y"][bass.ds(tile, 1)].rearrange("o p d -> (o p) d")).then_inc(y_sem[u], 16)
                    sp.wait_ge(h1_ready, t - 1)
                    sp.dma_start(x_in[u][:, :], x_v[bass.ds(tile, 1)].rearrange("o p d -> (o p) d")).then_inc(x_sem[u], 16)

                with sp.Fori(1, NT // 2) as i:
                    for u in range(2):
                        step(2 * i + u, u)
                sp.wait_ge(w_split, KC)
                for i in range(KC + DE // P):
                    load_expert_slice(sp, w_gu, w_down, slice(0, 1), i, w_stage).then_inc(w_next, 16)
                sp.wait_ge(w_next, 16 * (KC + DE // P))

            @block.tensor
            def _(pe):
                def turn_y(t, u, n_loaded):
                    pe.wait_ge(lo_ready, t)
                    pe.wait_ge(y_sem[u], n_loaded)
                    for c in range(KC):
                        last = pe.transpose(ps_y[:, c, :], y_in[u][:, c * P:(c + 1) * P], K["ident"][:, :])
                    last.then_inc(y_turned, 1)

                def project(t, u, n):
                    if n == 0:
                        pe.wait_ge(lo_ready, t + 1)
                        pe.wait_ge(h1_ready, t)
                    c = slice(n * 512, n * 512 + 512)
                    for k in range(KC):
                        if n == 0 and isinstance(t, int) and t == 0:
                            pe.wait_ge(w_split, k + 1)
                        last = mm3(pe, ps_o[:, c], yT_hi[u][:, k, :], yT_lo[u][:, k, :],
                                   w_hi[:, k, c], w_lo[:, k, c], k == 0, k == KC - 1)
                    if n == 1:
                        last.then_inc(out_done, 1)

                def turn_x(t, u):
                    pe.wait_ge(xtT_ready, t)
                    pe.wait_ge(xt_ready, t + 1)
                    for c in range(KC):
                        last = pe.transpose(ps_x[:, c, :], xt[u][:, c * P:(c + 1) * P], K["ident"][:, :])
                    last.then_inc(x_turned, 1)

                def logits(t):
                    pe.wait_ge(xtT_ready, t + 1)
                    pe.wait_ge(lg_ready, t)
                    for c in range(KC):
                        last = pe.matmul(ps_l[:, 0:NLG], xtT[:, c, :], w_r[:, c, :], start=c == 0, stop=c == KC - 1)
                    last.then_inc(lg_done, 1)

                turn_y(0, 0, 16)
                turn_y(1, 1, 16)
                project(0, 0, 0)
                project(0, 0, 1)
                pe.wait_ge(par, 80)

                def step(t, u, i, has_next):
                    if has_next:
                        turn_y(t + 2, u, 16 * i + 32)
                    project(t + 1, 1 - u, 0)
                    turn_x(t, u)
                    project(t + 1, 1 - u, 1)
                    logits(t)

                with pe.Fori(0, NT // 2 - 1) as i:
                    for u in range(2):
                        step(2 * i + u, u, i, True)
                step(NT - 2, 0, None, False)
                turn_x(NT - 1, 1)
                logits(NT - 1)
                pe.wait_ge(counted, 1)
                pe.matmul(ps_c[:, 0:NE], K["ones"][:, :], upto[:, :, NT - 1], start=True, stop=True).then_inc(ranked, 1)
                pe.matmul(ps_l[:, :], K["below"][:, :], both[:, :, :].rearrange("p e t -> p (e t)"), start=True, stop=False)
                pe.matmul(ps_l[:, :], K["ones"][:, :], before[:, :, :].rearrange("p e t -> p (e t)"),
                          start=False, stop=True).then_inc(ranked, 1)
                for c in range(2 * NT):
                    if c % 8 == 0:
                        pe.wait_ge(hot_ready, c // 8 + 1)
                    last = pe.matmul(ps_c[:, 0:NBC], lane_hot[:, c, :], blk_hot[:, c, :],
                                     start=c == 0, stop=c == 2 * NT - 1)
                last.then_inc(table_done, 1)

            @block.scalar
            def _(act):
                act.preload_act_table_set(TABLES)

                def hi(t, u):
                    act.wait_ge(y_turned, t + 1)
                    if not (isinstance(t, int) and t < 2):
                        act.wait_ge(out_done, t - 1)
                    for half in range(2):
                        c = slice(4 * half, 4 * half + 4)
                        last = act.activation(yT_hi[u][:, c, :], ps_y[:, c, :], ACT.Copy)
                    last.then_inc(hi_ready, 1)

                for k in range(KC):
                    if k == KC // 2:
                        hi(0, 0)
                    act.activation(w_hi[:, k, :], w_stage[:, k, :], ACT.Copy).then_inc(w_hid, 1)
                hi(1, 1)
                def step(t, u, has_next):
                    if has_next:
                        hi(t + 2, u)
                    act.wait_ge(h1_ready, t + 1)
                    act.dma_start(S["h1"][bass.ds(t, 1)].rearrange("o p d -> (o p) d"), h1[u][:, :]).then_inc(h1_out[u], 16)
                    act.wait_ge(ssq_ready, t + 1)
                    act.activation(lnv[:, :], ssq[:, :], ACT.Ln, scale=1.0 / D, bias=K["eps"][:, :])
                    act.drain()
                    act.activation(rstd[:, :], lnv[:, :], ACT.Exp, scale=-0.5)
                    act.drain()
                    act.wait_ge(xt_ready, t)
                    act.activation(sq[:, :], h1[u][:, :], ACT.Copy, scale=rstd[:, 0:1]).then_inc(scaled, 1)
                    act.wait_ge(xt_ready, t + 1)
                    act.dma_start(S["xt"][bass.ds(t * P, P), :], xt[u][:, :]).then_inc(xt_out[u], 16)
                    act.wait_ge(x_turned, t + 1)
                    act.wait_ge(lg_done, t)
                    act.activation(xtT[:, 0:4, :], ps_x[:, 0:4, :], ACT.Copy)
                    act.activation(xtT[:, 4:8, :], ps_x[:, 4:8, :], ACT.Copy).then_inc(xtT_ready, 1)

                with act.Fori(0, NT // 2 - 1) as i:
                    for u in range(2):
                        step(2 * i + u, u, True)
                step(NT - 2, 0, False)
                step(NT - 1, 1, False)
                act.wait_ge(gd_ready, 1)
                act.activation(gex[:, :, :], gd[:, :, :], ACT.Exp).then_inc(gex_ready, 1)
                act.wait_ge(ed_ready, 1)
                act.activation(e2[:, :], e2[:, :], ACT.Exp).then_inc(e2_ready, 1)
                for u in range(2):
                    act.wait_ge(h1_out[u], 8 * NT)
                    act.wait_ge(xt_out[u], 8 * NT)

            @block.vector
            def _(dve):
                def lo(t, u):
                    dve.wait_ge(hi_ready, t + 1)
                    for half in range(2):
                        c = slice(4 * half, 4 * half + 4)
                        last = dve.tensor_tensor(yT_lo[u][:, c, :], ps_y[:, c, :], yT_hi[u][:, c, :].bitcast(F32), ALU.subtract)
                    last.then_inc(lo_ready, 1)

                for k in range(KC):
                    if k == KC // 2:
                        lo(0, 0)
                    dve.wait_ge(w_hid, k + 1)
                    dve.tensor_tensor(w_lo[:, k, :], w_stage[:, k, :], w_hi[:, k, :].bitcast(F32), ALU.subtract).then_inc(w_split, 1)
                lo(1, 1)
                dve.wait_ge(made, 3)
                dve.wait_ge(par, 80)

                def residual(t, u, i):
                    n_loaded = 16 * i + 16
                    dve.wait_ge(x_sem[u], n_loaded)
                    dve.wait_ge(out_done, t + 1)
                    if not (isinstance(i, int) and i == 0):
                        dve.wait_ge(h1_out[u], 16 * i)
                    dve.tensor_tensor(h1[u][:, :], ps_o[:, :], x_in[u][:, :], ALU.add).then_inc(h1_ready, 1)

                def norm(t, u):
                    dve.wait_ge(scaled, t)
                    dve.tensor_tensor_reduce(xt[u][:, :], h1[u][:, :], h1[u][:, :], 1.0, 0.0, ALU.mult, ALU.add,
                                             ssq[:, :]).then_inc(ssq_ready, 1)

                def logits(t):
                    dve.wait_ge(lg_done, t + 1)
                    dve.tensor_tensor(lg[:, bass.ds(t, 1), :].rearrange("p o n -> p (o n)"), ps_l[:, 0:NLG], b_r[:, :],
                                      ALU.add).then_inc(lg_ready, 1)

                def step(t, u, i, first, has_next):
                    residual(t, u, i)
                    dve.drain()
                    if not (isinstance(i, int) and i == 0):
                        dve.wait_ge(xt_out[u], 16 * i)
                    norm(t, u)
                    if not first:
                        logits(t - 1)
                    if has_next:
                        lo(t + 2, u)
                    dve.wait_ge(scaled, t + 1)
                    dve.tensor_tensor(xt[u][:, :], sq[:, :], nf[:, :], ALU.mult).then_inc(xt_ready, 1)

                step(0, 0, 0, True, True)
                step(1, 1, 0, False, True)
                with dve.Fori(1, NT // 2 - 1) as i:
                    for u in range(2):
                        step(2 * i + u, u, i, False, True)
                step(NT - 2, 0, NT // 2 - 1, False, False)
                step(NT - 1, 1, NT // 2 - 1, False, False)
                logits(NT - 1)

                def over(ap, n):
                    return ap.rearrange("p (t o) -> p t o", o=1).to_broadcast((P, NT, n))

                def candidates(n):
                    return iota[:, 0:n].rearrange("p (o n) -> p o n", o=1).to_broadcast((P, NT, n))

                def first_largest(index, largest, values, n, scratch):
                    dve.tensor_tensor(scratch, values, over(largest, n), ALU.is_lt)
                    dve.drain()
                    dve.scalar_tensor_tensor(out=scratch, in0=scratch, scalar=float(NE), in1=candidates(n),
                                             op0=ALU.mult, op1=ALU.add)
                    dve.drain()
                    dve.tensor_reduce(index, scratch, AX_X, ALU.min)
                    dve.drain()

                dve.drain()
                lg_g = lg[:, :, 0:NGRP]
                dve.tensor_reduce(gm[:, :], lg_g, AX_X, ALU.max)
                dve.drain()
                dve.tensor_tensor(gd[:, :, :], lg_g, over(gm[:, :], NGRP), ALU.subtract).then_inc(gd_ready, 1)
                first_largest(gif[:, :], gm[:, :], lg_g, NGRP, ig[:, :, :])
                dve.tensor_tensor(og[:, :, :], candidates(NGRP), over(gif[:, :], NGRP), ALU.is_equal)
                dve.drain()
                dve.tensor_tensor(selg[:, :, :, :].rearrange("p t e g -> p t g e"),
                                  lg[:, :, NGRP:].rearrange("p t (g e) -> p t g e", g=NGRP),
                                  og[:, :, :].rearrange("p t (g o) -> p t g o", o=1).to_broadcast((P, NT, NGRP, EPG)),
                                  ALU.mult)
                dve.drain()
                dve.tensor_reduce(sel[:, :, :], selg[:, :, :, :], AX_X, ALU.add)
                dve.drain()
                for c in range(2):
                    dve.tensor_reduce(em[:, c, :], sel[:, :, :], AX_X, ALU.max)
                    dve.drain()
                    first_largest(eif[:, c, :], em[:, c, :], sel[:, :, :], EPG, ie[:, :, :])
                    if c == 0:
                        dve.tensor_tensor(oe[:, :, :], candidates(EPG), over(eif[:, c, :], EPG), ALU.is_equal)
                        dve.drain()
                        dve.scalar_tensor_tensor(out=sel[:, :, :], in0=oe[:, :, :], scalar=-3.0e38, in1=sel[:, :, :],
                                                 op0=ALU.mult, op1=ALU.add)
                        dve.drain()
                dve.tensor_tensor(e2[:, :], em[:, 1, :], em[:, 0, :], ALU.subtract).then_inc(ed_ready, 1)
                for c in range(2):
                    dve.scalar_tensor_tensor(out=eif[:, c, :], in0=gif[:, :], scalar=float(EPG), in1=eif[:, c, :],
                                             op0=ALU.mult, op1=ALU.add)
                dve.drain()
                for c in range(2):
                    dve.tensor_tensor(oh[:, :, c, :], candidates(NE), over(eif[:, c, :], NE), ALU.is_equal)
                dve.drain()
                dve.tensor_tensor(both[:, :, :].rearrange("p e t -> p t e"), oh[:, :, 0, :], oh[:, :, 1, :], ALU.add)
                dve.drain()
                dve.tensor_tensor_scan(upto[:, :, :].rearrange("p e t -> p (e t)"), anew[:, :, :].rearrange("p e t -> p (e t)"),
                                       both[:, :, :].rearrange("p e t -> p (e t)"), 0.0, ALU.mult, ALU.add)
                dve.drain()
                dve.tensor_tensor(before[:, :, :], upto[:, :, :], both[:, :, :], ALU.subtract).then_inc(counted, 1)
                dve.wait_ge(ranked, 1)
                dve.tensor_scalar(nbi[:, :], ps_c[:, 0:NE], float(P - 1), None, ALU.add)
                dve.drain()
                dve.tensor_scalar(nbi[:, :], nbi[:, :], 7, None, ALU.arith_shift_right)
                dve.drain()
                dve.tensor_scalar(nbf[:, :], nbi[:, :], 1.0, None, ALU.max)
                dve.drain()
                dve.tensor_copy(R["nb"][:, :], nbf[:, :])
                dve.tensor_tensor_scan(incl[:, :], K["ones"][:, 0:NE], nbf[:, :], 0.0, ALU.mult, ALU.add)
                dve.drain()
                dve.tensor_tensor(base[:, :], incl[:, :], nbf[:, :], ALU.subtract)
                dve.tensor_copy(R["incl"][:, :], incl[:, :])
                dve.drain()
                dve.tensor_copy(R["first"][:, :], base[:, :])
                dve.tensor_scalar(base[:, :], base[:, :], float(P), None, ALU.mult)
                dve.drain()
                dve.wait_ge(ranked, 2)
                dve.tensor_tensor(rank[:, :, :], ps_l[:, :].rearrange("p (e t) -> p t e", t=NT),
                                  base[:, :].rearrange("p (o e) -> p o e", o=1).to_broadcast((P, NT, NE)), ALU.add)
                dve.drain()
                for c in range(2):
                    dve.tensor_tensor(pick[:, :, c, :], oh[:, :, c, :], rank[:, :, :], ALU.mult)
                dve.drain()
                dve.tensor_reduce(posf[:, :], pick[:, :, :, :].rearrange("p t c e -> p (t c) e"), AX_X, ALU.add)
                dve.drain()
                dve.tensor_copy(R["pos"][:, :], posf[:, :])
                dve.drain()
                dve.tensor_scalar(blki[:, :], R["pos"][:, :], 7, None, ALU.arith_shift_right)
                dve.drain()
                dve.tensor_copy(blkf[:, :], blki[:, :])
                dve.drain()
                dve.scalar_tensor_tensor(out=lanef[:, :], in0=blkf[:, :], scalar=-float(P), in1=posf[:, :],
                                         op0=ALU.mult, op1=ALU.add)
                dve.drain()
                for q in range(2 * NT // 8):
                    c = slice(8 * q, 8 * q + 8)

                    def spread(ap, n):
                        return ap[:, c].rearrange("p (c o) -> p c o", o=1).to_broadcast((P, 8, n))

                    def counting(n):
                        return iota[:, 0:n].rearrange("p (o n) -> p o n", o=1).to_broadcast((P, 8, n))

                    dve.tensor_tensor(blk_hot[:, c, :], counting(NBC), spread(blkf, NBC), ALU.is_equal)
                    dve.tensor_tensor(lane_hot[:, c, :], counting(P), spread(lanef, P), ALU.is_equal)
                    dve.drain()
                    dve.tensor_tensor(blk_hot[:, c, :], blk_hot[:, c, :].bitcast(F32),
                                      spread(tokf[:, :, :].rearrange("p t c -> p (t c)"), NBC), ALU.mult
                                      ).then_inc(hot_ready, 1)
                dve.wait_ge(gex_ready, 1)
                dve.tensor_reduce(gsum[:, :], gex[:, :, :], AX_X, ALU.add)
                dve.drain()
                dve.wait_ge(e2_ready, 1)
                dve.scalar_tensor_tensor(out=den[:, :], in0=e2[:, :], scalar=1.0, in1=gsum[:, :], op0=ALU.add, op1=ALU.mult)
                dve.drain()
                dve.reciprocal(R["wt"][:, :, 0], den[:, :])
                dve.drain()
                dve.tensor_tensor(R["wt"][:, :, 1], R["wt"][:, :, 0], e2[:, :], ALU.mult)
                dve.wait_ge(table_done, 1)
                dve.tensor_copy(R["slots"][:, :], ps_c[:, 0:NBC])


def experts(nc, sem, K, w_gu, w_down, w_stage, S, R, norm_final, h1, nf):
    KD = DE // P
    NPC = KC + KD
    gate_c, up_c, all_c = slice(0, DE), slice(DE, D), slice(0, D)
    gate_ks = [(0, 1), (1, 2), (2, 4), (4, 6), (6, 8)]
    up_ks = [(k, k + 2) for k in range(0, KC, 2)]
    PIECES = ([(slice(*k), gate_c) for k in gate_ks] + [(slice(*k), up_c) for k in up_ks]
              + [(slice(k, k + 1), all_c) for k in range(KC, NPC)])
    UP, DP, NP = len(gate_ks), len(gate_ks) + len(up_ks), len(PIECES)

    def piece_of(k, c):
        return next((i for i, (ks, cs) in enumerate(PIECES) if ks.start == k and cs == c), None)

    HE = DE // 2
    with ExitStack() as ctx:
        def sb(name, shape, dt=F32):
            return ctx.enter_context(nc.sbuf_tensor(name, shape, dt))

        def pb(name, shape):
            return ctx.enter_context(nc.psum_tensor(name, shape, F32))

        w_hi = sb("we_hi", [P, NPC, D], F32R)
        w_lo = sb("we_lo", [P, NPC, D], F32R)
        none = sb("idx_zero", [P, 1], I32)
        tok = sb("idx_tok", [P, 1], I32)
        xg = sb("xg", [P, D])
        xT_hi = sb("xe_hi", [P, KC, P], F32R)
        xT_lo = sb("xe_lo", [P, KC, P], F32R)
        sg = sb("sg", [P, DE])
        hh = sb("hh", [P, DE])
        hT_hi = sb("hT_hi", [P, KD, P], F32R)
        hT_lo = sb("hT_lo", [P, KD, P], F32R)
        ysb = sb("ysb", [P, D])
        ps_g = pb("pe_g", [P, DE])
        ps_u = [pb(f"pe_u{i}", [P, DE])[:, 0:HE] for i in range(2)]
        ps_x = pb("pe_x", [P, KC, P])
        ps_h = [pb("pe_h", [P, DE])[:, 0:HE].rearrange("p (c t) -> p c t", t=P),
                ps_g[:, 0:HE].rearrange("p (c t) -> p c t", t=P)]
        ps_y = pb("pe_y", [P, D])

        w_in_sem = [sem(f"ex_w{i}") for i in range(NPC)]
        w_hid, w_split = sem("ex_w_hi"), sem("ex_w_split")
        ahead, xg_sem = sem("ex_ahead"), sem("ex_xg")
        x_turned, x_hi, x_lo = sem("ex_x_turned"), sem("ex_x_hi"), sem("ex_x_lo")
        gate_done, up_done, silu_ready, h_ready = sem("ex_gate"), sem("ex_up"), sem("ex_silu"), sem("ex_h")
        h_turned, h_hi, h_lo = sem("ex_h_turned"), sem("ex_h_hi"), sem("ex_h_lo")
        down_done, y_ready, y_out = sem("ex_down"), sem("ex_y"), sem("ex_y_out")

        def counts(eng, e):
            col = slice(e, e + 1) if isinstance(e, int) else bass.ds(e, 1)
            return (eng.value_load(R["first"][0:1, col], min_val=0, max_val=NBLK - 1),
                    eng.value_load(R["nb"][0:1, col], min_val=1, max_val=T // P))

        def over_blocks(eng, top, block_step):
            def expert(e):
                first, n = top(e)
                block_step(e, eng.snap(first), True)
                with eng.If(eng.snap(n) > 1):
                    with eng.Fori(1, n) as j:
                        block_step(e, eng.snap(first + j), False)

            expert(0)
            with eng.Fori(1, NE) as e:
                expert(e)

        with nc.Block() as block:
            @block.sync
            def _(sp):
                with sp.Fori(1, NE) as e:
                    row = bass.ds(sp.snap(e), 1)
                    for i in range(NPC):
                        last = UP + i // 2 if i < KC else DP + i - KC
                        sp.wait_ge(w_split, NP * e + (last + 1 - NP))
                        load_expert_slice(sp, w_gu, w_down, row, i, w_stage).then_inc(w_in_sem[i], 16)
                sp.dma_start(nf[:, :], norm_final.rearrange("(o d) -> o d", o=1).to_broadcast((P, D))).then_inc(ahead, 16)
                for t in range(2):
                    sp.dma_start(h1[t][:, :], S["h1"][t]).then_inc(ahead, 16)
                sp.wait_ge(ahead, 48)

            @block.gpsimd
            def _(pool):
                pool.memset(none[:, :], 0).then_inc(y_out, 16)
                pool.drain()
                total = pool.value_load(R["incl"][0:1, NE - 1:NE], min_val=NE, max_val=NBLK)

                def gather(b):
                    col = slice(b, b + 1) if isinstance(b, int) else bass.ds(b, 1)
                    if not isinstance(b, int):
                        pool.wait_ge(x_turned, b)
                    pool.tensor_tensor(tok[:, :], R["slots"][:, col], none[:, :], ALU.add)
                    pool.drain()
                    pool.indirect_dma_start(xg[:, :], None, S["xt"], bass.IndirectOffsetOnAxis(ap=tok[:, 0:1], axis=0)
                                            ).then_inc(xg_sem, 16)
                    pool.wait_ge(xg_sem, 16 * b + 16)

                gather(0)
                with pool.Fori(1, total + 1) as b:
                    gather(b)
                pool.wait_ge(y_out, total * 16 + 16)

            @block.tensor
            def _(pe):
                def turn_x(b):
                    pe.wait_ge(x_lo, b)
                    pe.wait_ge(xg_sem, 16 * b + 16)
                    for c in range(KC):
                        last = pe.transpose(ps_x[:, c, :], xg[:, c * P:(c + 1) * P], K["ident"][:, :])
                    last.then_inc(x_turned, 1)

                def turn_h(b, a):
                    pe.wait_ge(h_ready, 2 * b + a + 1)
                    for c in range(2):
                        col = (2 * a + c) * P
                        last = pe.transpose(ps_h[a][:, c, :], hh[:, col:col + P], K["ident"][:, :])
                    last.then_inc(h_turned, 1)

                def step(e, b, first):
                    pe.wait_ge(x_lo, b + 1)
                    pe.wait_ge(h_lo, 2 * b)
                    for k in range(KC):
                        if first and piece_of(k, gate_c) is not None:
                            pe.wait_ge(w_split, NP * e + piece_of(k, gate_c) + 1)
                        last = mm3(pe, ps_g[:, :], xT_hi[:, k, :], xT_lo[:, k, :], w_hi[:, k, 0:DE],
                                   w_lo[:, k, 0:DE], k == 0, k == KC - 1)
                    last.then_inc(gate_done, 1)
                    cut = KC - 2 if first else KC
                    for ks in ((0, cut), (cut, KC)):
                        for a in range(2):
                            for k in range(*ks):
                                if first and a == 0 and k % 2 == 0:
                                    pe.wait_ge(w_split, NP * e + UP + k // 2 + 1)
                                c = slice(DE + a * HE, DE + (a + 1) * HE)
                                last = mm3(pe, ps_u[a], xT_hi[:, k, :], xT_lo[:, k, :], w_hi[:, k, c],
                                           w_lo[:, k, c], k == 0, k == KC - 1)
                                if k == KC - 1:
                                    last.then_inc(up_done, 1)
                    turn_h(b, 0)
                    turn_x(b + 1)
                    turn_h(b, 1)
                    pe.wait_ge(y_ready, b)
                    for k in range(KD):
                        if first:
                            pe.wait_ge(w_split, NP * e + DP + k + 1)
                        if k % 2 == 0:
                            pe.wait_ge(h_lo, 2 * b + k // 2 + 1)
                        for h in range(2):
                            c = slice(h * 512, h * 512 + 512)
                            last = mm3(pe, ps_y[:, c], hT_hi[:, k, :], hT_lo[:, k, :], w_hi[:, KC + k, c],
                                       w_lo[:, KC + k, c], k == 0, k == KD - 1)
                    last.then_inc(down_done, 1)

                turn_x(0)
                over_blocks(pe, lambda e: counts(pe, e), step)

            @block.scalar
            def _(act):
                act.preload_act_table_set("silu_and_others")

                def x_high(b):
                    act.wait_ge(x_turned, b + 1)
                    act.activation(xT_hi[:, 0:4, :], ps_x[:, 0:4, :], ACT.Copy)
                    act.activation(xT_hi[:, 4:8, :], ps_x[:, 4:8, :], ACT.Copy).then_inc(x_hi, 1)

                def w_high(e, i):
                    k, c = PIECES[i]
                    if not isinstance(e, int):
                        for s in range(k.start, k.stop):
                            act.wait_ge(w_in_sem[s], 16 * e)
                    act.activation(w_hi[:, k, c], w_stage[:, k, c], ACT.Copy).then_inc(w_hid, 1)

                def top(e):
                    for i in range(DP):
                        w_high(e, i)
                        if isinstance(e, int) and i == UP - 1:
                            x_high(0)
                    first, n = counts(act, e)
                    if not isinstance(e, int):
                        act.wait_ge(down_done, first)
                    w_high(e, DP)
                    return first, n

                def row_before(b):
                    return nc.s_assert_within(act.snap(b * P - P), 0, (YB - 1) * P,
                                              skip_runtime_bounds_check_because="b is from 1 to NBLK")

                def y_copy(b):
                    act.wait_ge(down_done, b)
                    act.wait_ge(y_out, 16 * b)
                    act.activation(ysb[:, :], ps_y[:, :], ACT.Copy).then_inc(y_ready, 1)

                def y_store(b, row):
                    act.wait_ge(y_ready, b)
                    act.dma_start(S["ys"][bass.ds(row, P), :], ysb[:, :]).then_inc(y_out, 16)

                def step(e, b, first):
                    if not (first and isinstance(e, int)):
                        row = row_before(b)
                    act.wait_ge(gate_done, b + 1)
                    act.wait_ge(h_ready, 2 * b)
                    act.activation(sg[:, :], ps_g[:, :], ACT.Silu).then_inc(silu_ready, 1)
                    has_last = not (first and isinstance(e, int))
                    if has_last:
                        y_copy(b)
                    if first:
                        for i in range(DP + 1, NP):
                            w_high(e, i)
                    if has_last:
                        y_store(b, row)
                    for a in range(2):
                        act.wait_ge(h_turned, 2 * b + a + 1)
                        act.activation(hT_hi[:, 2 * a:2 * a + 2, :], ps_h[a], ACT.Copy).then_inc(h_hi, 1)
                    act.wait_ge(up_done, 2 * b + 2)
                    x_high(b + 1)

                over_blocks(act, top, step)
                total = act.value_load(R["incl"][0:1, NE - 1:NE], min_val=NE, max_val=NBLK)
                y_copy(total)
                y_store(total, row_before(total))

            @block.vector
            def _(dve):
                def x_low(b):
                    dve.wait_ge(x_hi, b + 1)
                    for c in (slice(0, 4), slice(4, 8)):
                        last = dve.tensor_tensor(xT_lo[:, c, :], ps_x[:, c, :], xT_hi[:, c, :].bitcast(F32), ALU.subtract)
                    last.then_inc(x_lo, 1)

                def w_low(e, i):
                    k, c = PIECES[i]
                    dve.wait_ge(w_hid, NP * e + i + 1)
                    dve.tensor_tensor(w_lo[:, k, c], w_stage[:, k, c], w_hi[:, k, c].bitcast(F32), ALU.subtract).then_inc(w_split, 1)

                def top(e):
                    for i in range(UP):
                        w_low(e, i)
                    if isinstance(e, int):
                        x_low(0)
                    found = counts(dve, e)
                    for i in range(UP, DP + 1):
                        w_low(e, i)
                    return found

                def step(e, b, first):
                    if first:
                        w_low(e, DP + 1)
                    dve.wait_ge(silu_ready, b + 1)
                    for a in range(2):
                        c = slice(a * HE, (a + 1) * HE)
                        dve.wait_ge(up_done, 2 * b + a + 1)
                        dve.wait_ge(h_turned, 2 * b + a)
                        dve.tensor_tensor(hh[:, c], sg[:, c], ps_u[a], ALU.mult).then_inc(h_ready, 1)
                    for a in range(2):
                        dve.wait_ge(h_hi, 2 * b + a + 1)
                        k = slice(2 * a, 2 * a + 2)
                        dve.tensor_tensor(hT_lo[:, k, :], ps_h[a], hT_hi[:, k, :].bitcast(F32), ALU.subtract).then_inc(h_lo, 1)
                        if first:
                            w_low(e, DP + 2 + a)
                    x_low(b + 1)

                over_blocks(dve, top, step)


def combine(nc, sem, K, h1, nf, S, R, out):
    out_v = out.rearrange("b (t p) d -> (b t) p d", p=P)
    with ExitStack() as ctx:
        def sb(name, shape, dt=F32):
            return ctx.enter_context(nc.sbuf_tensor(name, shape, dt))

        NB = 2
        y0 = [sb(f"f_y0{i}", [P, D]) for i in range(NB)]
        y1 = [sb(f"f_y1{i}", [P, D]) for i in range(NB)]
        o = [sb(f"f_o{i}", [P, D]) for i in range(NB)]
        ssq = sb("f_ssq", [P, 1])
        lnv = sb("f_ln", [P, 1])
        rstd = sb("f_rstd", [P, 1])
        h_sem, y0_sem, y1_sem, o_out = [[sem(f"fn_{n}{i}") for i in range(NB)] for n in ("h", "y0_", "y1_", "out")]
        summed, ssq_ready, rstd_ready, o_ready = sem("fn_summed"), sem("fn_ssq"), sem("fn_rstd"), sem("fn_o")

        with nc.Block() as block:
            @block.gpsimd
            def _(pool):
                for t in range(NT):
                    u = t % NB
                    if t >= NB:
                        pool.wait_ge(summed, t - NB + 1)
                    for c, (y, s) in enumerate(((y0, y0_sem), (y1, y1_sem))):
                        pool.indirect_dma_start(y[u][:, :], None, S["ys"][0:NBLK * P, :], bass.IndirectOffsetOnAxis(
                            ap=R["pos"][:, 2 * t + c:2 * t + c + 1], axis=0)).then_inc(s[u], 16)

            @block.sync
            def _(sp):
                def load(t, u):
                    sp.dma_start(h1[u][:, :], S["h1"][bass.ds(t, 1)].rearrange("o p d -> (o p) d")).then_inc(h_sem[u], 16)

                def store(t, u):
                    sp.wait_ge(o_ready, t + 1)
                    sp.dma_start(out_v[bass.ds(t, 1)].rearrange("o p d -> (o p) d"), o[u][:, :]).then_inc(o_out[u], 16)

                with sp.Fori(0, NT // 2 - 1) as i:
                    for u in range(2):
                        t = sp.snap(2 * i + u)
                        store(t, u)
                        load(t + 2, u)
                store(NT - 2, 0)
                store(NT - 1, 1)
                for u in range(2):
                    sp.wait_ge(o_out[u], 8 * NT)

            @block.scalar
            def _(act):
                act.preload_act_table_set(TABLES)
                with act.Fori(0, NT) as t:
                    act.wait_ge(ssq_ready, t + 1)
                    act.activation(lnv[:, :], ssq[:, :], ACT.Ln, scale=1.0 / D, bias=K["eps"][:, :])
                    act.drain()
                    act.wait_ge(o_ready, t)
                    act.activation(rstd[:, :], lnv[:, :], ACT.Exp, scale=-0.5).then_inc(rstd_ready, 1)

            @block.vector
            def _(dve):
                def pair(i):
                    for u in range(2):
                        t = 2 * i + u
                        wt = R["wt"][:, bass.ds(t, 1), :].rearrange("p o c -> p (o c)")
                        if not isinstance(i, int):
                            dve.wait_ge(h_sem[u], 16 * i)
                        for s in (y0_sem, y1_sem):
                            dve.wait_ge(s[u], 16 * i + 16)
                        dve.scalar_tensor_tensor(out=h1[u][:, :], in0=y0[u][:, :], scalar=wt[:, 0:1], in1=h1[u][:, :],
                                                 op0=ALU.mult, op1=ALU.add)
                        dve.drain()
                        dve.scalar_tensor_tensor(out=h1[u][:, :], in0=y1[u][:, :], scalar=wt[:, 1:2], in1=h1[u][:, :],
                                                 op0=ALU.mult, op1=ALU.add).then_inc(summed, 1)
                        dve.drain()
                        dve.wait_ge(rstd_ready, t)
                        dve.wait_ge(o_out[u], 16 * i)
                        dve.tensor_tensor_reduce(o[u][:, :], h1[u][:, :], h1[u][:, :], 1.0, 0.0, ALU.mult, ALU.add,
                                                 ssq[:, :]).then_inc(ssq_ready, 1)
                        dve.drain()
                        dve.wait_ge(rstd_ready, t + 1)
                        dve.scalar_tensor_tensor(out=o[u][:, :], in0=h1[u][:, :], scalar=rstd[:, 0:1], in1=nf[:, :],
                                                 op0=ALU.mult, op1=ALU.mult).then_inc(o_ready, 1)

                pair(0)
                with dve.Fori(1, NT // 2) as i:
                    pair(i)


def program(nc, x, norm_mix, w_in, conv_w, conv_b, b_mlstm_gate, w_gla_gate, b_gla_gate,
            head_norm, w_out, norm_ffn, w_group, b_group, w_expert, b_expert, w_gu,
            w_down, norm_final, out):
    def scratch(name, shape, dt=F32):
        return nc.dram_tensor(name, shape, dt).ap()

    S = {
        "xT": scratch("s_xT", (KC, P, T)),
        "gate": scratch("s_gate", (NT, P, D)),
        "val": scratch("s_val", (NT, P, D)),
        "qk": scratch("s_qk", (8, P, T)),
        "kR": scratch("s_kR", (2, 5, P, T)),
        "qG": scratch("s_qG", (2, 2, P, T)),
        "gl": scratch("s_gl", (2, P, NT)),
        "rows": scratch("s_rows", (4, H, T)),
        "nM": scratch("s_nM", (H, T)),
        "y": scratch("s_y", (NT, P, D)),
        "h1": scratch("s_h1", (NT, P, D)),
        "xt": scratch("s_xt", (T, D)),
        "ys": scratch("s_ys", (YB * P, D)),
        "dec": scratch("s_dec", (H, NT)),
    }
    def phase(build, *args):
        own = []

        def sem(name):
            own.append(nc.alloc_semaphore(name=name))
            return own[-1]

        build(nc, sem, *args)
        nc.clear_and_free_semaphores(own)
        nc.all_engine_barrier()

    with ExitStack() as ctx:
        K = {}
        phase(constants, ctx, K)
        phase(project_tokens, K, x, norm_mix, w_in, head_norm, S)
        phase(project_channels, K, norm_mix, w_in, conv_w, conv_b, b_mlstm_gate, w_gla_gate, b_gla_gate, S)
        w_stage = ctx.enter_context(nc.sbuf_tensor("w_stage", [P, KC + DE // P, D], F32))
        phase(recur, K, S, w_out, w_stage)
        R = {
            "slots": ctx.enter_context(nc.sbuf_tensor("slots", [P, NBLK + 2], I32)),
            "pos": ctx.enter_context(nc.sbuf_tensor("pos", [P, 2 * NT], I32)),
            "wt": ctx.enter_context(nc.sbuf_tensor("wt", [P, NT, 2], F32)),
            "nb": ctx.enter_context(nc.sbuf_tensor("nb", [P, NE], I32)),
            "first": ctx.enter_context(nc.sbuf_tensor("first", [P, NE], I32)),
            "incl": ctx.enter_context(nc.sbuf_tensor("incl_i", [P, NE], I32)),
        }
        phase(project_out_and_route, K, x, norm_ffn, w_group, b_group, w_expert, b_expert, w_gu, w_down, w_stage, S, R)
        h1 = [ctx.enter_context(nc.sbuf_tensor(f"f_h1{i}", [P, D], F32)) for i in range(2)]
        nf = ctx.enter_context(nc.sbuf_tensor("f_norm", [P, D], F32))
        phase(experts, K, w_gu, w_down, w_stage, S, R, norm_final, h1, nf)
        phase(combine, K, h1, nf, S, R, out)


_INS = ["x", "norm_mix", "w_in", "conv_w", "conv_b", "b_mlstm_gate", "w_gla_gate", "b_gla_gate", "head_norm",
        "w_out", "norm_ffn", "w_group", "b_group", "w_expert", "b_expert", "w_gu", "w_down", "norm_final"]


def kernel(**inputs):
    import numpy as np
    import concourse.bacc as bacc
    from concourse.bass_utils import run_bass_kernel_spmd

    nc = bacc.Bacc("TRN2", target_bir_lowering=False, num_devices=1)
    arrays, args = {}, []
    for name in _INS:
        a = np.ascontiguousarray(inputs[name])
        arrays[f"in_{name}_dram"] = a
        args.append(nc.dram_tensor(f"in_{name}_dram", a.shape, mybir.dt.from_np(a.dtype), kind="ExternalInput").ap())
    out = nc.dram_tensor("out_0_dram", (1, T, D), F32, kind="ExternalOutput").ap()
    program(nc, *args, out)
    r = run_bass_kernel_spmd(nc, [arrays], core_ids=[0])
    return r.results[0]["out_0_dram"]
```
